# Optimizing a Trainium2 kernel written in Bass

```python
import jax, jax.numpy as jnp
from jax import lax
import numpy as np

D_MODEL = 1024
BATCH = 1
SEQ = 1024
DEPTH = 1

ATT_HEADS = 12
ATT_HEAD_DIM = 64
ATT_WIDTH = ATT_HEADS * ATT_HEAD_DIM
ROPE_DIM = ATT_HEAD_DIM // 4
ROPE_THETA = 500000.0
DILATED_PATTERNS = ((128, 1), (512, 4), (2048, 16))
ATT_BLOCK = 128
SSD_INNER = 2 * D_MODEL
SSD_HEAD_DIM = 64
SSD_HEADS = SSD_INNER // SSD_HEAD_DIM
SSD_GROUPS = 8
SSD_STATE = 128
SSD_CONV = 4
SSD_CHUNK = 128
SSD_CONV_CH = SSD_INNER + 2 * SSD_GROUPS * SSD_STATE
D_FF = 2816
N_BRANCH = 2
N_MOD = 9
NORM_EPS = 1e-6
IN_SIZES = (ATT_WIDTH, ATT_WIDTH, ATT_WIDTH, SSD_INNER, SSD_CONV_CH, SSD_HEADS, N_BRANCH * D_MODEL)
IN_WIDTH = sum(IN_SIZES)

kernel_name = "hybrid_gated_dilated_attn_ssd_macaron_block"

def rmsnorm(x, w):
    xf = x.astype(jnp.float32)
    y = xf * lax.rsqrt(jnp.mean(xf * xf, axis=-1, keepdims=True) + NORM_EPS)
    return (y * w.astype(jnp.float32)).astype(x.dtype)

def modulate(h, shift, scale):
    return h * (1.0 + scale[:, None, :]) + shift[:, None, :]

def swiglu(h, w_gu, w_down):
    g, u = jnp.split(h @ w_gu, 2, axis=-1)
    return (jax.nn.silu(g) * u) @ w_down

def partial_rope(t, positions):
    inv_freq = ROPE_THETA ** (-jnp.arange(0, ROPE_DIM, 2, dtype=jnp.float32) / ROPE_DIM)
    ang = positions.astype(jnp.float32)[..., None] * inv_freq
    cos, sin = jnp.cos(ang)[:, :, None, :], jnp.sin(ang)[:, :, None, :]
    tf = t.astype(jnp.float32)
    half = ROPE_DIM // 2
    t1, t2, rest = tf[..., :half], tf[..., half:ROPE_DIM], tf[..., ROPE_DIM:]
    out = jnp.concatenate([t1 * cos - t2 * sin, t2 * cos + t1 * sin, rest], axis=-1)
    return out.astype(t.dtype)

def dilated_window_attention(q, k, v, window, dilation):
    b, s, h, d = q.shape
    r = dilation
    reach = window // dilation
    n_sub = s // r
    blk = min(ATT_BLOCK, n_sub)
    n_blk = -(-n_sub // blk)
    pad = n_blk * blk - n_sub

    def to_sub(t):
        t = t.reshape(b, n_sub, r, h, d).transpose(0, 2, 1, 3, 4).reshape(b * r, n_sub, h, d)
        t = jnp.pad(t, ((0, 0), (0, pad), (0, 0), (0, 0)))
        return t.reshape(b * r, n_blk, blk, h, d)

    def with_prev(t):
        prev = jnp.pad(t, ((0, 0), (1, 0), (0, 0), (0, 0), (0, 0)))[:, :-1]
        return jnp.concatenate([prev, t], axis=2)

    qb = to_sub(q)
    kc, vc = with_prev(to_sub(k)), with_prev(to_sub(v))
    scores = jnp.einsum('nbqhd,nbkhd->nbhqk', qb, kc)
    qi = jnp.arange(blk)[:, None]
    ki = jnp.arange(2 * blk)[None, :]
    dist = qi + blk - ki
    band = (dist >= 0) & (dist <= reach)
    has_prev = (jnp.arange(n_blk)[:, None, None] > 0) | (ki >= blk)[None]
    valid = band[None] & has_prev
    scores = jnp.where(valid[None, :, None], scores, -jnp.inf)
    m = jnp.max(scores, axis=-1, keepdims=True)
    p = jnp.exp(scores - m)
    den = jnp.sum(p, axis=-1, keepdims=True)
    o = jnp.einsum('nbhqk,nbkhd->nbqhd', p / den, vc)
    lse = jnp.swapaxes((m + jnp.log(den))[..., 0], 2, 3)

    def from_sub(t):
        t = t.reshape((b, r, n_blk * blk) + t.shape[3:])[:, :, :n_sub]
        t = jnp.moveaxis(t, 1, 2)
        return t.reshape((b, s) + t.shape[3:])

    return from_sub(o), from_sub(lse)

def dilated_mixture_attention(q, k, v):
    outs, lses = [], []
    for window, dilation in DILATED_PATTERNS:
        o, l = dilated_window_attention(q, k, v, window, dilation)
        outs.append(o)
        lses.append(l)
    alpha = jax.nn.softmax(jnp.stack(lses), axis=0)
    return jnp.einsum('pbsh,pbshd->bshd', alpha, jnp.stack(outs))

def causal_depthwise_conv(u, w, bias):
    kw, ch = w.shape
    y = lax.conv_general_dilated(u, w[:, None, :].astype(u.dtype), window_strides=(1,),
                                 padding=[(kw - 1, 0)], dimension_numbers=('NWC', 'WIO', 'NWC'),
                                 feature_group_count=ch)
    return y + bias

def segsum(a):
    cs = jnp.cumsum(a, axis=-1)
    diff = cs[..., :, None] - cs[..., None, :]
    t = a.shape[-1]
    mask = jnp.tril(jnp.ones((t, t), dtype=bool))
    return jnp.where(mask, diff, -jnp.inf)

def ssd_chunked(xh, dt, a, bmat, cmat):
    b, s, h, p = xh.shape
    g, n = bmat.shape[-2:]
    e = h // g
    q = SSD_CHUNK
    c = s // q
    xdt = (xh * dt[..., None]).reshape(b, c, q, g, e, p)
    a_dt = (dt * a).reshape(b, c, q, h).transpose(0, 3, 1, 2)
    a_cs = jnp.cumsum(a_dt, axis=-1)
    bc = bmat.reshape(b, c, q, g, n)
    cc = cmat.reshape(b, c, q, g, n)
    decay_in = jnp.exp(segsum(a_dt)).reshape(b, g, e, c, q, q)
    cb = jnp.einsum('bclgn,bcsgn->bcgls', cc, bc)
    y_diag = jnp.einsum('bcgls,bgecls,bcsgep->bclgep', cb, decay_in, xdt)
    decay_to_end = jnp.exp(a_cs[..., -1:] - a_cs).reshape(b, g, e, c, q)
    states = jnp.einsum('bclgn,bgecl,bclgep->bcgepn', bc, decay_to_end, xdt)
    chunk_tot = jnp.pad(a_cs[..., -1], ((0, 0), (0, 0), (1, 0)))
    decay_chunk = jnp.exp(segsum(chunk_tot)).reshape(b, g, e, c + 1, c + 1)
    states = jnp.concatenate([jnp.zeros_like(states[:, :1]), states], axis=1)
    states = jnp.einsum('bgezk,bkgepn->bzgepn', decay_chunk, states)[:, :-1]
    decay_from_start = jnp.exp(a_cs).reshape(b, g, e, c, q)
    y_off = jnp.einsum('bclgn,bcgepn,bgecl->bclgep', cc, states, decay_from_start)
    return (y_diag + y_off).reshape(b, s, h, p)

def hybrid_mixer(h, positions, w_in, conv_w, conv_b, dt_bias, a_log, d_skip, ssd_norm_w,
                 w_att_out, w_ssd_out, w_mix_out):
    b, s, _ = h.shape
    offs = np.cumsum(IN_SIZES)[:-1].tolist()
    q, k, v, z, xbc, dt_raw, gates = jnp.split(h @ w_in, offs, axis=-1)

    q = partial_rope(q.reshape(b, s, ATT_HEADS, ATT_HEAD_DIM), positions).astype(jnp.float32)
    k = partial_rope(k.reshape(b, s, ATT_HEADS, ATT_HEAD_DIM), positions).astype(jnp.float32)
    v = v.reshape(b, s, ATT_HEADS, ATT_HEAD_DIM).astype(jnp.float32)
    o_att = dilated_mixture_attention(q * (ATT_HEAD_DIM ** -0.5), k, v)
    y_att = o_att.reshape(b, s, ATT_WIDTH).astype(h.dtype) @ w_att_out

    xbc = jax.nn.silu(causal_depthwise_conv(xbc, conv_w, conv_b)).astype(jnp.float32)
    xs, bm, cm = jnp.split(xbc, [SSD_INNER, SSD_INNER + SSD_GROUPS * SSD_STATE], axis=-1)
    xh = xs.reshape(b, s, SSD_HEADS, SSD_HEAD_DIM)
    dt = jax.nn.softplus(dt_raw.astype(jnp.float32) + dt_bias.astype(jnp.float32))
    a = -jnp.exp(a_log.astype(jnp.float32))
    y = ssd_chunked(xh, dt, a, bm.reshape(b, s, SSD_GROUPS, SSD_STATE),
                    cm.reshape(b, s, SSD_GROUPS, SSD_STATE))
    y = y + d_skip.astype(jnp.float32)[:, None] * xh
    y = y.reshape(b, s, SSD_INNER) * jax.nn.silu(z.astype(jnp.float32))
    y_ssd = rmsnorm(y, ssd_norm_w).astype(h.dtype) @ w_ssd_out

    g = jax.nn.sigmoid(gates.astype(jnp.float32)).reshape(b, s, N_BRANCH, D_MODEL)
    merged = g[:, :, 0] * y_att.astype(jnp.float32) + g[:, :, 1] * y_ssd.astype(jnp.float32)
    return merged.astype(h.dtype) @ w_mix_out

def setup_inputs(seed: int = 0) -> dict:
    key = jax.random.key(seed)
    ks = jax.random.split(key, 24)
    f32 = jnp.float32

    def nrm(k, shape, scale):
        return jax.random.normal(k, shape, f32) * scale

    def gain(k, shape):
        return 1.0 + 0.02 * jax.random.normal(k, shape, f32)

    L = DEPTH
    dt0 = jnp.exp(jax.random.uniform(ks[10], (L, SSD_HEADS), f32, np.log(1e-3), np.log(1e-1)))
    return {
        "x": nrm(ks[0], (BATCH, SEQ, D_MODEL), 1.0),
        "c": nrm(ks[1], (BATCH, D_MODEL), 1.0),
        "positions": jnp.broadcast_to(jnp.arange(SEQ, dtype=jnp.int32), (BATCH, SEQ)),
        "w_ada": nrm(ks[2], (L, D_MODEL, N_MOD * D_MODEL), 0.5 * D_MODEL ** -0.5),
        "b_ada": nrm(ks[3], (L, N_MOD * D_MODEL), 0.01),
        "norm1_w": gain(ks[4], (L, D_MODEL)),
        "ffn1_w_gu": nrm(ks[5], (L, D_MODEL, 2 * D_FF), D_MODEL ** -0.5),
        "ffn1_w_down": nrm(ks[6], (L, D_FF, D_MODEL), D_FF ** -0.5),
        "norm2_w": gain(ks[7], (L, D_MODEL)),
        "w_in": nrm(ks[8], (L, D_MODEL, IN_WIDTH), D_MODEL ** -0.5),
        "conv_w": nrm(ks[9], (L, SSD_CONV, SSD_CONV_CH), SSD_CONV ** -0.5),
        "conv_b": nrm(ks[11], (L, SSD_CONV_CH), 0.01),
        "dt_bias": dt0 + jnp.log(-jnp.expm1(-dt0)),
        "a_log": jnp.log(jax.random.uniform(ks[12], (L, SSD_HEADS), f32, 1.0, 16.0)),
        "d_skip": gain(ks[13], (L, SSD_HEADS)),
        "ssd_norm_w": gain(ks[14], (L, SSD_INNER)),
        "w_att_out": nrm(ks[15], (L, ATT_WIDTH, D_MODEL), ATT_WIDTH ** -0.5),
        "w_ssd_out": nrm(ks[16], (L, SSD_INNER, D_MODEL), SSD_INNER ** -0.5),
        "w_mix_out": nrm(ks[17], (L, D_MODEL, D_MODEL), D_MODEL ** -0.5),
        "norm3_w": gain(ks[18], (L, D_MODEL)),
        "ffn2_w_gu": nrm(ks[19], (L, D_MODEL, 2 * D_FF), D_MODEL ** -0.5),
        "ffn2_w_down": nrm(ks[20], (L, D_FF, D_MODEL), D_FF ** -0.5),
        "final_norm_w": gain(ks[21], (D_MODEL,)),
    }

def reference(x, c, positions, w_ada, b_ada, norm1_w, ffn1_w_gu, ffn1_w_down, norm2_w, w_in,
              conv_w, conv_b, dt_bias, a_log, d_skip, ssd_norm_w, w_att_out, w_ssd_out,
              w_mix_out, norm3_w, ffn2_w_gu, ffn2_w_down, final_norm_w):
    b = x.shape[0]
    c_act = jax.nn.silu(c)
    for l in range(DEPTH):
        mod = (c_act @ w_ada[l] + b_ada[l]).reshape(b, N_MOD, D_MODEL)
        sh1, sc1, g1, sh2, sc2, g2, sh3, sc3, g3 = [mod[:, i] for i in range(N_MOD)]
        h = modulate(rmsnorm(x, norm1_w[l]), sh1, sc1)
        x = x + 0.5 * g1[:, None, :] * swiglu(h, ffn1_w_gu[l], ffn1_w_down[l])
        h = modulate(rmsnorm(x, norm2_w[l]), sh2, sc2)
        y = hybrid_mixer(h, positions, w_in[l], conv_w[l], conv_b[l], dt_bias[l], a_log[l],
                         d_skip[l], ssd_norm_w[l], w_att_out[l], w_ssd_out[l], w_mix_out[l])
        x = x + g2[:, None, :] * y
        h = modulate(rmsnorm(x, norm3_w[l]), sh3, sc3)
        x = x + 0.5 * g3[:, None, :] * swiglu(h, ffn2_w_gu[l], ffn2_w_down[l])
    return rmsnorm(x, final_norm_w)


_drawn_inputs = setup_inputs


def setup_inputs(seed=0):
    import zlib

    import numpy as np

    out = dict(_drawn_inputs(seed))
    spreads = {}
    factors = {'b_ada': 6.161,
     'norm1_w': 8.0,
     'norm2_w': 8.0,
     'conv_b': 64.0,
     'd_skip': 64.0,
     'ssd_norm_w': 64.0,
     'norm3_w': 22.427,
     'final_norm_w': 7.494}
    for name, (base, spread) in spreads.items():
        noise = np.random.default_rng([zlib.crc32(name.encode()), seed]).standard_normal(out[name].shape)
        drawn = base * np.exp(spread * noise) if base else spread * noise
        out[name] = __import__('jax').numpy.asarray(drawn.astype(out[name].dtype))
    for name, factor in factors.items():
        out[name] = (out[name] * factor).astype(out[name].dtype)
    return out
```

```python
from contextlib import ExitStack, contextmanager

import numpy as np
import concourse.bass as bass
from concourse import mybir

F32 = mybir.dt.float32
F32R = mybir.dt.float32r
I32 = mybir.dt.int32
ALU = mybir.AluOpType
ACT = mybir.ActivationFunctionType
AXX = mybir.AxisListType.X

P = 128
D = 1024
T = 1024
DT_ = D // P
NT = T // P
FF = 2816
FT = FF // P
AH, HD = 12, 64
PAIRS = AH // 2
NG, GH = 8, 4
SH = NG * GH
INNER = 2 * D
AW = AH * HD
ROPE, THETA = HD // 4, 500000.0
O_Q, O_K, O_V = 0, AW, 2 * AW
O_Z = 3 * AW
O_X = O_Z + INNER
O_B = O_X + INNER
O_C = O_B + NG * P
O_DT = O_C + NG * P
O_G0 = O_DT + SH
O_G1 = O_G0 + D
EPS = 1e-6
NEG = -1e30
PATTERNS = ((128, 1), (512, 4), (2048, 16))

PARTS = ((0, 7), (7, 7), (14, 4), (18, 4))
ADA_W = 512
ADA_FIRST = 2 * D // ADA_W
ADA_ALL = 9 * D // ADA_W
assert PARTS[0][1] + PARTS[1][1] == ADA_ALL - ADA_FIRST

K_ID, K_ONE, K_NEG, K_ROT, K_INVF = 0, P, 2 * P, 3 * P, 4 * P
K_PERSIST = 4 * P + 1
K_MASK = K_PERSIST
K_ALL = K_MASK + T

R_ADA, R_N1, R_N2, R_N3, R_SN, R_C = 0, 72, 80, 88, 96, 112
R_P1 = 120
R_CW = R_P1
R_CB = R_CW + 4 * 32
R_ALL = R_CB + 32


def constants():
    k = np.zeros((P, K_ALL), np.float32)
    k[:, K_ID:K_ID + P] = np.eye(P)
    k[:, K_ONE:K_ONE + P] = 1.0
    s, l = np.arange(P)[:, None], np.arange(P)[None, :]
    k[:, K_NEG:K_NEG + P] = np.where(s <= l, 0.0, NEG)
    half = ROPE // 2
    for h in (0, HD):
        for m in range(half):
            k[h + m + half, K_ROT + h + m] = -1.0
            k[h + m, K_ROT + h + m + half] = 1.0
        inv = np.float32(THETA) ** (-np.arange(0, ROPE, 2, dtype=np.float32) / np.float32(ROPE))
        k[h:h + half, K_INVF] = inv
        k[h + half:h + ROPE, K_INVF] = inv
    dist = np.arange(P)[:, None] - np.arange(T)[None, :] + (T - P)
    n = sum(((dist >= 0) & (dist <= w) & (dist % r == 0)).astype(int) for w, r in PATTERNS)
    k[:, K_MASK:] = np.where(n > 0, -np.log(np.maximum(n, 1)), -NEG)
    return k


class Chain:

    def __init__(self, eng, sem):
        self.eng, self.sem, self.base, self.term, self.count = eng, sem, 0, None, 0

    def value(self):
        v = self.base + self.count
        return v if self.term is None else self.term + v

    def link(self, instruction):
        self.count += 1
        instruction.then_inc(self.sem, 1)
        self.eng.wait_ge(self.sem, self.value())

    @contextmanager
    def loop(self, start, end, rate):
        base = self.base + self.count
        with self.eng.Fori(start, end) as i:
            self.base, self.count, self.term = base - start * rate, 0, i * rate if rate else None
            yield i
            assert self.count == rate, (self.count, rate)
        self.base, self.count, self.term = base + (end - start) * rate, 0, None


def at_least(eng, sem, value):
    if not (isinstance(value, int) and value <= 0):
        eng.wait_ge(sem, value)


CREDIT = 64


def past(eng, sem, value):
    eng.wait_ge(sem, value + CREDIT)


def plan():
    w, o0, o1 = {}, {}, {}
    n, m0, m1 = 0, 0, 0

    def section(name, blocks, outs0, outs1):
        nonlocal n, m0, m1
        w[name], o0[name], o1[name] = n, m0, m1
        n, m0, m1 = n + blocks, m0 + outs0, m1 + outs1

    def ffn(x):
        for p, (_, cnt) in enumerate(PARTS):
            section(f"gu{x}{p}", 2 * cnt, cnt, cnt)
            section(f"dn{x}{p}", 8, 4, 4)

    ffn(0)
    section("dt", 2, 1, 0)
    section("att", 4 * PAIRS, 3 * PAIRS, 3 * PAIRS)
    section("ga", 16, 8, 8)
    section("gb", 8, 4, 4)
    section("ssdx", 4, 2, 2)
    section("ssd", 6 * (NG - 1) + 2, 3 * (NG - 1) + 1, 3 * (NG - 1) + 1)
    section("yo", 16, 4, 4)
    section("mix", 8, 4, 4)
    ffn(1)
    section("end", 0, 0, 0)
    return w, (o0, o1)


W, O = plan()
BLOCKS = W["end"]

ASTEPS = [(q, h) for q in range(NT) for h in range(2)]
AGROUPS = [1 + (q >= 4) for q, _ in ASTEPS]
AGROUP0 = [sum(AGROUPS[:s]) for s in range(len(ASTEPS) + 1)]
AGB0 = [sum(g - 1 for g in AGROUPS[:s]) for s in range(len(ASTEPS) + 1)]
NA = len(ASTEPS)


def att_events():
    ev = [("half", 0, k, t) for k in range(8) for t in range(2)]
    ev += [("half", 1, k, t) for k in range(8) for t in range(2)]
    ev += [("rot", 0)]
    ev += [("half", 2, k, t) for k in range(4) for t in range(2)]
    ev += [("rot", 1)]
    ev += [("half", 3, k, t) for k in range(4, 8) for t in range(2)]
    return ev


AEV = att_events()
A_PER_STEP = 3


def kernel_program(nc, x, c, positions, w_ada, b_ada, norm1_w, ffn1_w_gu, ffn1_w_down, norm2_w, w_in,
                   conv_w, conv_b, dt_bias, a_log, d_skip, ssd_norm_w, w_att_out, w_ssd_out, w_mix_out,
                   norm3_w, ffn2_w_gu, ffn2_w_down, final_norm_w, table, out):
    ctx = ExitStack()
    with ctx:
        def dram(name, shape):
            return nc.dram_tensor(name, shape, F32, kind="Internal").ap()

        x_keep = dram("x_keep", (P, DT_, T))
        merged_keep = dram("merged_keep", (DT_, P, T))
        gate_keep = dram("gate_keep", (DT_, P, T))
        y_keep = dram("y_keep", (NG, P, 2, T))
        cs_keep = dram("cs_keep", (SH, T))
        dec_keep = dram("dec_keep", (SH, NT))

        ctx.enter_context(nc.sbuf_tensor("slab", [P, 207 * 256], F32))
        origin = 16512

        def sb(name, kb, shape, dt=F32):
            size = int(np.prod(shape)) * 4
            assert kb * 1024 + size <= 207 * 1024, name
            return nc.alloc_sbuf_tensor_at(name, [P, *shape], dt, offset=origin + int(kb * 1024))

        w_raw = sb("w_raw", 0, [2, 8, P])
        w_hi = sb("w_hi", 8, [2, 8, P], F32R)
        w_lo = sb("w_lo", 16, [2, 8, P], F32R)
        h_hi = sb("h_hi", 24, [8, T], F32R)
        h_lo = sb("h_lo", 56, [8, T], F32R)
        xT = sb("xT", 88, [8, T])
        hid_hi = sb("hid_hi", 120, [7, T], F32R)
        hid_lo = sb("hid_lo", 148, [7, T], F32R)
        ada = sb("ada", 176, [8, ADA_W])
        acc = sb("acc", 176, [T])
        rstd = sb("rstd", 180, [T])
        sq = sb("sq", 184, [2, T])
        tmp = sb("tmp", 192, [2, T])
        x_nat = sb("x_nat", 120, [4, D])
        ada_a = sb("ada_a", 136, [8, ADA_W])
        ada_b = sb("ada_b", 152, [8, ADA_W])
        par1 = sb("par1", 168, [3, P])
        w_final = sb("w_final", 120, [D])
        o_row = sb("o_row", 124, [2, D])
        cosT = sb("cosT", 88, [T])
        sinT = sb("sinT", 92, [T])
        q_st = sb("q_st", 96, [T])
        k_st = sb("k_st", 100, [T])
        v_st = sb("v_st", 96, [T])
        dt_keep = sb("dt_keep", 104, [NT * SH])
        o_tok = sb("o_tok", 105, [2, P])
        qT = sb("qT", 108, [2, T])
        kT = sb("kT", 116, [2, T])
        v_tok = sb("v_tok", 124, [2, NT, P])
        prob = sb("prob", 132, [2, T])
        mask = sb("mask", 140, [T])
        o_hi = sb("o_hi", 144, [PAIRS, T], F32R)
        o_lo = sb("o_lo", 168, [PAIRS, T], F32R)
        probT = sb("probT", 192, [2, T])
        pos_i = sb("pos_i", 132, [T], I32)
        ang = sb("ang", 136, [T])
        rt1 = sb("rt1", 124, [T])
        rt2 = sb("rt2", 128, [T])
        dt_w = [sb(f"dt_w{j}", 144 + 4 * j, [T]) for j in range(4)]
        dtT = sb("dtT", 160, [T])
        csT = sb("csT", 164, [T])
        dteT = sb("dteT", 168, [T])
        conv_in = sb("conv_in", 88, [2, T + 4])
        xbc = sb("xbc", 97, [2, 4, T])
        z_sil = sb("z_sil", 129, [2, T])
        cs_b = sb("cs_b", 137, [NT, GH, P])
        decay = sb("decay", 153, [2, GH, P])
        wT = sb("wT", 157, [2, GH, P])
        c_scaled = sb("c_scaled", 161, [2, GH, P])
        ecs = sb("ecs", 165, [2, GH, P])
        xdt = sb("xdt", 169, [2, 2 * P])
        xdte = sb("xdte", 171, [2, 2 * P])
        b_tok = sb("b_tok", 173, [2, P])
        state = sb("state", 174, [2, 2 * P])
        y_sq = sb("y_sq", 176, [T])
        y_acc = sb("y_acc", 180, [T])
        y_hi = sb("y_hi", 24, [16, T], F32R)
        y_lo = sb("y_lo", 88, [16, T], F32R)
        y_raw = sb("y_raw", 88, [16, T])
        merged = sb("merged", 152, [8, T])
        y_rstd = sb("y_rstd", 184, [T])
        gate = sb("gate", 188, [T])
        m_hi = sb("m_hi", 24, [8, T], F32R)
        m_lo = sb("m_lo", 56, [8, T], F32R)
        kst = sb("kst", 200, [K_PERSIST + 1])
        par = sb("par", 202.125, [R_ALL])
        mod = sb("mod", 203.25, [72])
        small = sb("small", 203.5625, [112])
        ada_red = sb("ada_red", 204, [ADA_W])
        cs_tok = sb("cs_tok", 204, [NT, SH])
        dte_tok = sb("dte_tok", 205, [NT, SH])
        dec_b = sb("dec_b", 206, [SH, NT])
        dt_tok = sb("dt_tok", 191, [NT, SH])
        assert K_PERSIST + 1 <= 544 and R_ALL <= 288 and 202.125 + R_ALL / 256 <= 203.25

        ident = kst[:, K_ID:K_ID + P]
        ones = kst[:, K_ONE:K_ONE + P]
        causal = kst[:, K_NEG:K_NEG + P]
        rotm = kst[:, K_ROT:K_ROT + P]
        invf = kst[:, K_INVF:K_INVF + 1]
        c_act = small[:, 0:8]
        scale1, scale2, scale3 = (small[:, 8 + 8 * j:16 + 8 * j] for j in range(3))
        gate1, gate3 = small[:, 32:40], small[:, 40:48]
        d_col = small[:, 48:64]
        negmax = small[:, 64:66]
        den = small[:, 74:78]
        rden = small[:, 68:70]
        head_col = small[0:SH, 70:73]
        d_row = small[:, 78:110]
        eps_col = small[:, 110:111]
        dec_head = dt_w[3][0:SH, 0:NT]
        SH1, SC1, G1, SH2, SC2, G2, SH3, SC3, G3 = (8 * j for j in range(9))

        psG = ctx.enter_context(nc.psum_tensor("psG", [P, 2, 2, 512], F32))
        psS = ctx.enter_context(nc.psum_tensor("psS", [P, 2, 512], F32))
        psT = ctx.enter_context(nc.psum_tensor("psT", [P, 512], F32))
        psO = ctx.enter_context(nc.psum_tensor("psO", [P, 512], F32))

        def sem(name):
            return ctx.enter_context(nc.semaphore(name))

        w_loaded = [sem("w_loaded0"), sem("w_loaded1")]
        w_hi_done, w_lo_done, w_used = sem("w_hi_done"), sem("w_lo_done"), sem("w_used")
        freed = [sem("psum0_read"), sem("psum1_read")]
        s_table, s_rows, s_small, s_xin, s_xtr, s_xt = (sem(n) for n in (
            "table_loaded", "rows_loaded", "small_loaded", "x_loaded", "x_transposed", "xT_written"))
        s_par_ps, s_par, s_cact = sem("par_transposed"), sem("par_written"), sem("c_act_done")
        s_ada = [sem(f"ada_loaded{j}") for j in range(3)]
        s_ada_mul, s_ada_red, s_ada_mm, s_ada_done = (sem(n) for n in (
            "ada_scaled", "ada_reduced", "ada_summed", "mod_written"))
        s_first_cols, s_g1 = sem("scale_columns"), sem("gate1_column")
        s_sq, s_acc, s_ms, s_rt, s_rstd, s_xr, s_hhi, s_hlo = (sem(n) for n in (
            "squared", "squares_added", "mean_square", "root_done", "rstd_done", "x_scaled",
            "h_hi_done", "h_lo_done"))
        s_hid_hi, s_hid_lo = sem("hid_hi_done"), sem("hid_lo_done")
        s_xkeep, s_xback = sem("x_kept"), sem("x_back")
        s_dt_e, s_dt_ln, s_dt_cs, s_dt_dte, s_dt_ready, s_dt_tr, s_dt_tok = (sem(n) for n in (
            "dt_abs", "dt_log", "cs_done", "dte_exp", "dte_done", "dt_transposed", "dt_tok_done"))
        s_cs_kept, s_dec, s_dec_kept = sem("cs_kept"), sem("dec_loaded"), sem("dec_kept")
        s_pos, s_mask, s_ang, s_trig = sem("pos_loaded"), sem("mask_loaded"), sem("angle_done"), sem("trig_done")
        s_qk, s_masked, s_exp, s_tr, s_pta, s_ptb, s_pv, s_o, s_otr, s_ohi, s_olo = (sem(n) for n in (
            "qk_done", "masked", "exp_done", "prob_transposed", "probT_a", "probT_b", "pv_done", "o_scaled",
            "o_transposed", "o_hi_done", "o_lo_done"))
        s_rot, s_roped, s_vtr, s_vtok = sem("rot_done"), sem("roped"), sem("v_transposed"), sem("v_tok_done")
        s_mg_out, s_gt_out = sem("merged_kept"), [sem("gate_kept0"), sem("gate_kept1")]
        s_conv_in, s_conv, s_conv_act = sem("conv_in_done"), sem("conv_done"), sem("conv_act_done")
        s_csb = [sem(f"cs_b_loaded{j}") for j in range(NT)]
        s_arg, s_dec_exp, s_ecs, s_cscaled, s_tokT, s_cb, s_btok, s_xdte, s_wT, s_y, s_st, s_state, s_yev = (
            sem(n) for n in ("decay_arg", "decay_exp", "ecs_done", "c_scaled_done", "tok_transposed", "cb_done",
                             "b_tok_done", "xdte_done", "wT_done", "y_done", "state_mm", "state_done", "y_evac"))
        s_gated, s_ysq, s_yacc, s_yout = sem("y_gated"), sem("y_squared"), sem("y_sq_added"), sem("y_kept")
        s_yms, s_yrt, s_yrstd = sem("y_mean_square"), sem("y_root"), sem("y_rstd_done")
        s_yin = [sem(f"y_loaded{j}") for j in range(4)]
        s_yhi, s_ylo = sem("y_hi_done"), sem("y_lo_done")
        s_mg_in, s_gt_in = sem("merged_loaded"), sem("gate_loaded")
        s_mg, s_mhi, s_mlo = sem("merged_done"), sem("m_hi_done"), sem("m_lo_done")
        s_wf, s_fms, s_frt, s_ftr, s_orow = (sem(n) for n in (
            "w_final_loaded", "final_mean_square", "final_root", "final_transposed", "row_done"))
        s_out = [sem("out_written0"), sem("out_written1")]
        pe_phase, act_phase, dve_phase, pool_phase = (sem(n) for n in (
            "pe_phase", "act_phase", "dve_phase", "pool_phase"))
        sp_turn, dve_turn = sem("sp_turn"), sem("dve_turn")
        c_act_sem, c_dve_sem, c_pool_sem = sem("act_chain"), sem("dve_chain"), sem("pool_chain")
        block = ctx.enter_context(nc.Block())

        def gu_cols(w, col):
            return w[0].rearrange("(k p) m -> p k m", p=P)[:, :, bass.ds(col, P)]

        ffn_w = ((ffn1_w_gu, ffn1_w_down), (ffn2_w_gu, ffn2_w_down))

        @block.sync
        def _(sp):
            def load(n, j, src, kt):
                at_least(sp, w_lo_done, n - 1)
                sp.sem_inc(sp_turn, 1)
                sp.dma_start(w_raw[:, j, 0:kt, :], src).then_inc(w_loaded[j], 16)

            def load_ada(chunk, dst, which):
                src = w_ada[0].rearrange("(k p) m -> p k m", p=P)[:, :, bass.ds(chunk * ADA_W, ADA_W)]
                sp.dma_start(dst, src).then_inc(s_ada[which], 16)

            def ffn_loads(x, after_first=None):
                w_gu, w_dn = ffn_w[x]
                for p, (f0, cnt) in enumerate(PARTS):
                    n0 = W[f"gu{x}{p}"]

                    def pair(i, n0=n0, f0=f0):
                        load(n0 + i * 2, 0, gu_cols(w_gu, (i + f0) * P), 8)
                        load(n0 + 1 + i * 2, 1, gu_cols(w_gu, (i + f0) * P + FF), 8)
                        if x == 0 and p < 2:
                            q = i + f0
                            sp.wait_ge(s_ada_red, q + ADA_FIRST)
                            if isinstance(i, int) and q == 0:
                                sp.wait_ge(s_xr, 8)
                            load_ada(q + ADA_FIRST, ada[:], 2)
                    if p == 0:
                        pair(0)
                        with sp.Fori(1, cnt) as i:
                            pair(i)
                    else:
                        with sp.Fori(0, cnt) as i:
                            pair(i)
                    n1 = W[f"dn{x}{p}"]
                    rows = w_dn[0][f0 * P:(f0 + cnt) * P, :].rearrange("(k p) m -> p k m", p=P)
                    with sp.Fori(0, 4) as i:
                        for j in range(2):
                            load(n1 + i * 2 + j, j, rows[:, :, bass.ds((i * 2 + j) * P, P)], cnt)

            sp.dma_start(kst[:, 0:K_PERSIST], table[:, 0:K_PERSIST]).then_inc(s_table, 16)
            sp.dma_start(par1[0:72, 0, :], b_ada.rearrange("o (r p) -> (o r) p", p=P)).then_inc(s_rows, 16)
            for r0, v in ((R_N1, norm1_w), (R_N2, norm2_w), (R_N3, norm3_w), (R_SN, ssd_norm_w), (R_C, c)):
                rows = v.shape[1] // P
                sp.dma_start(par1[r0:r0 + rows, 0, :], v.rearrange("o (r p) -> (o r) p", p=P)).then_inc(s_rows, 16)
            sp.dma_start(par1[:, 1, :], conv_w[0].rearrange("j (r p) -> (j r) p", p=P)).then_inc(s_rows, 16)
            sp.dma_start(par1[0:32, 2, :], conv_b.rearrange("o (r p) -> (o r) p", p=P)).then_inc(s_rows, 16)
            load_ada(0, ada_a[:], 0)
            load_ada(1, ada_b[:], 1)
            x_rows = x[0].rearrange("(h q p) d -> h p q d", h=2, p=P)
            sp.dma_start(x_nat[:], x_rows[0]).then_inc(s_xin, 16)
            sp.wait_ge(s_xtr, 8)
            sp.dma_start(x_nat[:], x_rows[1]).then_inc(s_xin, 16)
            sp.wait_ge(s_ada_red, 1)
            load_ada(2, ada_a[:], 0)
            sp.wait_ge(s_ada_red, 2)
            load_ada(3, ada_b[:], 1)
            sp.dma_start(d_row, d_skip.to_broadcast([P, SH])).then_inc(s_small, 16)
            with nc.allow_non_contiguous_dma(reason="32 heads' scalars, one per partition"):
                sp.dma_start(head_col[:, 0:1], dt_bias.rearrange("o h -> h o")).then_inc(s_small, 16)
                sp.dma_start(head_col[:, 1:2], a_log.rearrange("o h -> h o")).then_inc(s_small, 16)
            ffn_loads(0)

            win = w_in[0].rearrange("(k p) m -> p k m", p=P)
            load(W["dt"], 0, win[:, 0:4, O_DT:O_DT + P], 4)
            load(W["dt"] + 1, 1, win[:, 4:8, O_DT:O_DT + P], 4)
            sp.wait_ge(freed[0], O[0]["dt"])
            sp.wait_ge(freed[1], O[1]["dt"])
            sp.dma_start(x_keep, xT[:]).then_inc(s_xkeep, 16)
            na = W["att"]
            with sp.Fori(0, PAIRS) as i:
                load(na + i * 4, 0, win[:, :, bass.ds(i * P + O_Q, P)], 8)
                load(na + i * 4 + 1, 1, win[:, :, bass.ds(i * P + O_K, P)], 8)
                load(na + i * 4 + 2, 0, win[:, 0:4, bass.ds(i * P + O_V, P)], 4)
                load(na + i * 4 + 3, 1, win[:, 4:8, bass.ds(i * P + O_V, P)], 4)
            wao = w_att_out[0].rearrange("(k p) m -> p k m", p=P)
            with sp.Fori(0, 8) as i:
                load(W["ga"] + i * 2, 0, win[:, :, bass.ds(i * P + O_G0, P)], 8)
                load(W["ga"] + 1 + i * 2, 1, wao[:, :, bass.ds(i * P, P)], 6)
            with sp.Fori(0, 4) as i:
                for j in range(2):
                    load(W["gb"] + i * 2 + j, j, win[:, :, bass.ds((i * 2 + j) * P + O_G1, P)], 8)

            def ssd_x(n, g):
                load(n, 0, win[:, :, bass.ds(g * 2 * P + O_X, P)], 8)
                load(n + 1, 1, win[:, :, bass.ds(g * 2 * P + O_X + P, P)], 8)
                load(n + 2, 0, win[:, :, bass.ds(g * P + O_B, P)], 8)
                load(n + 3, 1, win[:, :, bass.ds(g * P + O_C, P)], 8)

            def ssd_z(n, g):
                load(n, 0, win[:, :, bass.ds(g * 2 * P + O_Z, P)], 8)
                load(n + 1, 1, win[:, :, bass.ds(g * 2 * P + O_Z + P, P)], 8)

            ssd_x(W["ssdx"], 0)
            with sp.Fori(0, NG - 1) as g:
                ssd_x(W["ssd"] + g * 6, g + 1)
                ssd_z(W["ssd"] + g * 6 + 4, g)
            ssd_z(W["ssd"] + (NG - 1) * 6, NG - 1)
            wso = w_ssd_out[0].rearrange("(k p) m -> p k m", p=P)
            load(W["yo"], 0, wso[:, 0:8, 0:P], 8)
            load(W["yo"] + 1, 1, wso[:, 8:16, 0:P], 8)
            for e in (pe_phase, act_phase, dve_phase, pool_phase):
                sp.wait_ge(e, 2)
            past(sp, s_yout, 16 * NG)
            for j in range(4):
                sp.dma_start(y_raw[:, 4 * j:4 * j + 4, :].rearrange("p (g u) t -> p g u t", u=2),
                             y_keep[2 * j:2 * j + 2].rearrange("g p u t -> p g u t")).then_inc(s_yin[j], 16)
            sp.wait_ge(s_mg_out, 16 * 8)
            sp.dma_start(merged[:], merged_keep.rearrange("d p t -> p d t")).then_inc(s_mg_in, 16)
            for s in s_gt_out:
                sp.wait_ge(s, 16 * 4)
            sp.dma_start(gate[:], gate_keep[0]).then_inc(s_gt_in, 16)
            with sp.Fori(1, 8) as i:
                for j in range(2):
                    load(W["yo"] + i * 2 + j, j, wso[:, 8 * j:8 * j + 8, bass.ds(i * P, P)], 8)
                sp.wait_ge(s_mg, i)
                sp.dma_start(gate[:], gate_keep[bass.ds(i, 1)].rearrange("o p t -> (o p) t")).then_inc(s_gt_in, 16)
            wmo = w_mix_out[0].rearrange("(k p) m -> p k m", p=P)
            load(W["mix"], 0, wmo[:, :, 0:P], 8)
            load(W["mix"] + 1, 1, wmo[:, :, P:2 * P], 8)
            sp.wait_ge(w_used, W["mix"])
            sp.wait_ge(s_xkeep, 16)
            sp.dma_start(xT[:], x_keep).then_inc(s_xback, 16)
            with sp.Fori(1, 4) as i:
                for j in range(2):
                    load(W["mix"] + i * 2 + j, j, wmo[:, :, bass.ds((i * 2 + j) * P, P)], 8)
            ffn_loads(1)
            sp.wait_ge(w_used, BLOCKS)
            sp.dma_start(w_final[:], final_norm_w.rearrange("(o d) -> o d", o=1).to_broadcast([P, D])).then_inc(s_wf, 16)
            for t in range(NT):
                sp.wait_ge(s_orow, 2 * (t + 1))
                sp.dma_start(out[0, t * P:(t + 1) * P, :], o_row[:, t % 2, :]).then_inc(s_out[t % 2], 16)
            for s in s_out:
                sp.wait_ge(s, 16 * NT // 2)

        @block.tensor
        def _(pe):
            mm = nc.tensor.matmul
            for s in (s_qk, s_tr, s_pv, s_otr, s_rot, s_vtr, s_tokT, s_cb, s_y, s_st):
                pe.sem_inc(s, CREDIT)

            def passes(out_, j, k, rh, rl, first, last):
                mm(out_, w_lo[:, j, k, :], rh, start=first, stop=False)
                mm(out_, w_hi[:, j, k, :], rl, start=False, stop=False)
                return mm(out_, w_hi[:, j, k, :], rh, start=False, stop=last)

            def product(n, j, b, m, hi, lo, kt, k_off=0, first=True, last=True, ready=None):
                pe.wait_ge(w_lo_done, n + 1)
                if first:
                    at_least(pe, freed[b], m)
                for k in range(kt):
                    if ready is not None:
                        pe.wait_ge(s_hlo, ready + k + 1)
                    for t in range(2):
                        cols = slice(512 * t, 512 * t + 512)
                        ins = passes(psG[:, b, t, :], j, k, hi[:, k_off + k, cols], lo[:, k_off + k, cols],
                                     first and k == 0, last and k == kt - 1)
                ins.then_inc(w_used, 1)

            def transpose(out_, in_, rows=P):
                return nc.tensor.transpose(out_, in_, ident[0:rows, 0:rows])

            def ada_sum(q):
                src, dst = ada_red, psO[:, 0:4]
                pe.wait_ge(s_ada_red, q + 1)
                at_least(pe, s_ada_done, q)
                for j in range(4):
                    ins = mm(dst[:, j:j + 1], src[:, j * P:(j + 1) * P], ones[:, 0:1], start=True, stop=True)
                ins.then_inc(s_ada_mm, 1)

            def norm_sum(idx):
                pe.wait_ge(s_acc, 8 * (idx + 1))
                for t in range(2):
                    ins = mm(psS[:, t, :], ones, acc[:, 512 * t:512 * t + 512], start=True, stop=True)
                ins.then_inc(s_ms, 1)

            def ffn(x, idx):
                for p, (f0, cnt) in enumerate(PARTS):
                    s = f"gu{x}{p}"
                    n0, a0, a1 = W[s], O[0][s], O[1][s]

                    def pair(i, ready=None):
                        if x == 0 and p < 2:
                            ada_sum_step(i, f0)
                        product(n0 + i * 2, 0, 0, a0 + i, h_hi, h_lo, 8, ready=ready)
                        product(n0 + 1 + i * 2, 1, 1, a1 + i, h_hi, h_lo, 8)

                    def ada_sum_step(i, f0):
                        if isinstance(i, int) and i + f0 == 0:
                            return
                        ada_sum(i + (f0 + ADA_FIRST - 1))

                    if p == 0:
                        pair(0, ready=8 * idx)
                        with pe.Fori(1, cnt) as i:
                            pair(i)
                    else:
                        with pe.Fori(0, cnt) as i:
                            pair(i)
                    if x == 0 and p == 1:
                        ada_sum(ADA_ALL - 1)
                    s = f"dn{x}{p}"
                    n0, a0, a1 = W[s], O[0][s], O[1][s]
                    pe.wait_ge(s_hid_lo, FT * x + f0 + cnt)
                    with pe.Fori(0, 4) as i:
                        for j in range(2):
                            product(n0 + i * 2 + j, j, j, (a0, a1)[j] + i, hid_hi, hid_lo, cnt)

            pe.wait_ge(s_table, 16)
            pe.wait_ge(s_rows, 16 * 8)
            transpose(psT[:, 0:R_P1], par1[0:R_P1, 0, :], R_P1)
            transpose(psT[:, R_CW:R_CW + P], par1[:, 1, :])
            transpose(psT[:, R_CB:R_CB + 32], par1[0:32, 2, :], 32).then_inc(s_par_ps, 1)
            for t in range(NT):
                pe.wait_ge(s_xin, 16 * (t // 4 + 1))
                for u in range(2):
                    i = 2 * t + u
                    at_least(pe, s_xt, i - 1)
                    for j in range(4):
                        ins = transpose(psS[:, u, j * P:(j + 1) * P], x_nat[:, t % 4, (4 * u + j) * P:(4 * u + j + 1) * P])
                    ins.then_inc(s_xtr, 1)
            for q in range(ADA_FIRST):
                ada_sum(q)
            pe.wait_ge(s_xt, 2 * NT)
            norm_sum(0)
            ffn(0, 0)

            pe.wait_ge(s_rt, 1)
            norm_sum(1)
            product(W["dt"], 0, 0, O[0]["dt"], h_hi, h_lo, 4, 0, True, False, ready=8)
            n = W["dt"] + 1
            pe.wait_ge(w_lo_done, n + 1)
            for k in range(4):
                pe.wait_ge(s_hlo, 8 + 4 + k + 1)
                for t in range(2):
                    cols = slice(512 * t, 512 * t + 512)
                    ins = passes(psG[:, 0, t, :], 1, k, h_hi[:, 4 + k, cols], h_lo[:, 4 + k, cols], False, k == 3)
            ins.then_inc(w_used, 1)

            def att_half(i, j, k, t):
                n = W["att"] + i * 4 + j
                b = (0, 1, 0, 0)[j]
                m = (O[0]["att"] + i * 3, O[1]["att"] + i * 3, O[0]["att"] + i * 3 + 2, 0)[j]
                kk = k - 4 if j == 3 else k
                if kk == 0 and t == 0:
                    pe.wait_ge(w_lo_done, n + 1)
                    if j < 3:
                        pe.wait_ge(freed[b], m)
                cols = slice(512 * t, 512 * t + 512)
                ins = passes(psG[:, b, t, :], j % 2, kk, h_hi[:, k, cols], h_lo[:, k, cols], k == 0, k == 7)
                if t == 1 and kk == (3 if j > 1 else 7):
                    ins.then_inc(w_used, 1)

            def att_rot(i, b):
                m = O[b]["att"] + i * 3 + 1
                pe.wait_ge(freed[b], m)
                src = (q_st, k_st)[b]
                for t in range(2):
                    ins = mm(psG[:, b, t, :], rotm, src[:, 512 * t:512 * t + 512], start=True, stop=True)
                ins.then_inc(s_rot, 1)

            def att_vtr(i):
                pe.wait_ge(freed[1], O[1]["att"] + i * 3 + 2)
                pe.wait_ge(freed[0], O[0]["att"] + i * 3 + 3)
                for t in range(NT):
                    ins = transpose(psG[:, 1, t // 4, (t % 4) * P:(t % 4 + 1) * P], v_st[:, t * P:(t + 1) * P])
                ins.then_inc(s_vtr, 1)

            def att_event(i, e):
                if e[0] == "half":
                    att_half(i, *e[1:])
                else:
                    att_rot(i, e[1])

            def att_iter(i, par_, att, gemm):
                S = i * NA
                TR = i * AGROUP0[NA]
                for s in range(NA + 3):
                    evs = [] if not gemm else AEV[s * A_PER_STEP:(s + 1) * A_PER_STEP]
                    slots = [evs[0:1], evs[1:2], evs[2:]]
                    if att and s < NA:
                        q, h = ASTEPS[s]
                        rows = slice(HD * h, HD * h + HD)
                        if s == 0:
                            past(pe, s_roped, i * 2 + 2)
                            past(pe, s_vtok, i + 1)
                        past(pe, s_masked, S + s)
                        width = (q + 1) * P
                        for t in range((width + 511) // 512):
                            c0, c1 = 512 * t, min(width, 512 * t + 512)
                            ins = mm(psS[:, t, 0:c1 - c0], qT[rows, par_, q * P:(q + 1) * P],
                                     kT[rows, par_, c0:c1], start=True, stop=True)
                        ins.then_inc(s_qk, 1)
                    for e in slots[0]:
                        att_event(i + 1, e)
                    r = s - 1
                    if att and 0 <= r < NA:
                        q, h = ASTEPS[r]
                        past(pe, s_exp, S + r + 1)
                        past(pe, s_olo, i * NT + max(0, (s - 3) // 2))
                        past(pe, s_pta, S + r)
                        past(pe, s_ptb, i * AGB0[NA] + AGB0[r])
                        for j in range(min(q + 1, 4)):
                            ins = transpose(psT[:, j * P:(j + 1) * P], prob[:, r % 2, j * P:(j + 1) * P])
                        ins.then_inc(s_tr, 1)
                    for e in slots[1]:
                        att_event(i + 1, e)
                    if att and 0 <= r < NA and ASTEPS[r][0] >= 4:
                        q, h = ASTEPS[r]
                        past(pe, s_pta, S + r + 1)
                        for j in range(4, q + 1):
                            ins = transpose(psT[:, (j - 4) * P:(j - 3) * P], prob[:, r % 2, j * P:(j + 1) * P])
                        ins.then_inc(s_tr, 1)
                    for e in slots[2]:
                        att_event(i + 1, e)
                    r = s - 2
                    if att and 0 <= r < NA:
                        q, h = ASTEPS[r]
                        past(pe, s_pta, S + r + 1)
                        if q >= 4:
                            past(pe, s_ptb, i * AGB0[NA] + AGB0[r + 1])
                        past(pe, s_o, S + r)
                        for j in range(q + 1):
                            ins = mm(psO[:, 0:HD], probT[:, r % 2, j * P:(j + 1) * P],
                                     v_tok[:, par_, j, HD * h:HD * h + HD], start=(j == 0), stop=(j == q))
                        ins.then_inc(s_pv, 1)
                    r = s - 3
                    if att and 0 <= r < NA and r % 2 == 1:
                        q = ASTEPS[r][0]
                        past(pe, s_o, S + r + 1)
                        past(pe, s_pta, S + min(s, NA))
                        past(pe, s_ptb, i * AGB0[NA] + AGB0[min(s, NA)])
                        transpose(psT[:, 0:P], o_tok[:, q % 2, :]).then_inc(s_otr, 1)
                if gemm:
                    att_vtr(i + 1)

            att_iter(-1, 0, False, True)
            pe.wait_ge(s_dt_cs, 1)
            pe.wait_ge(s_dt_ready, 1)
            for u, src in enumerate((csT, dtT, dteT)):
                for t in range(NT):
                    dst = psS[:, u // 2, (u % 2) * 256 + t * SH:(u % 2) * 256 + (t + 1) * SH]
                    ins = transpose(dst, src[0:SH, t * P:(t + 1) * P], SH)
            ins.then_inc(s_dt_tr, 1)
            pe.wait_ge(s_dt_tok, 1)
            with pe.Fori(0, PAIRS // 2 - 1) as i2:
                att_iter(i2 * 2, 0, True, True)
                att_iter(i2 * 2 + 1, 1, True, True)
            att_iter(PAIRS - 2, 0, True, True)
            att_iter(PAIRS - 1, 1, True, False)

            past(pe, s_olo, PAIRS * NT)
            with pe.Fori(0, 8) as i:
                product(W["ga"] + i * 2, 0, 0, O[0]["ga"] + i, h_hi, h_lo, 8)
                product(W["ga"] + 1 + i * 2, 1, 1, O[1]["ga"] + i, o_hi, o_lo, 6)
            with pe.Fori(0, 4) as i:
                for j in range(2):
                    product(W["gb"] + i * 2 + j, j, j, O[j]["gb"] + i, h_hi, h_lo, 8)

            for j in range(4):
                product(W["ssdx"] + j, j % 2, j % 2, O[j % 2]["ssdx"] + j // 2, h_hi, h_lo, 8)

            def ssd_front(i, p, c):
                n = i * NT + c
                tok = slice(c * P, (c + 1) * P)
                if c == 0:
                    past(pe, s_conv_act, i * 4 + 4)
                past(pe, s_xdte, n)
                past(pe, s_btok, n)
                for j in range(3):
                    ins = transpose(psT[:, j * P:(j + 1) * P], xbc[:, p, j, tok])
                ins.then_inc(s_tokT, 1)
                past(pe, s_wT, n)
                mm(psS[:, 0, 0:P], xbc[:, p, 2, tok], xbc[:, p, 3, tok], start=True, stop=True).then_inc(s_cb, 1)

            def ssd_back(i, p, c):
                n = i * NT + c
                past(pe, s_wT, n + 1)
                past(pe, s_xdte, n + 1)
                past(pe, s_cscaled, n + 1)
                past(pe, s_yev, n)
                if c > 0:
                    past(pe, s_state, i * (NT - 1) + c)
                for e in range(GH):
                    dst = psS[HD * (e % 2):HD * (e % 2) + HD, 1, (e // 2) * P:(e // 2 + 1) * P]
                    cols = slice(e * HD, (e + 1) * HD)
                    ins = mm(dst, xdt[:, c % 2, cols], wT[:, c % 2, e, :], start=True, stop=(c == 0))
                    if c > 0:
                        ins = mm(dst, state[:, (c - 1) % 2, cols], c_scaled[:, c % 2, e, :], start=False, stop=True)
                ins.then_inc(s_y, 1)
                if c < NT - 1:
                    past(pe, s_btok, n + 1)
                    past(pe, s_state, i * (NT - 1) + c)
                    mm(psO[:, 0:2 * P], b_tok[:, c % 2, :], xdte[:, c % 2, :], start=True, stop=True).then_inc(s_st, 1)

            def ssd_iter(i, p, gemm):
                n0 = W["ssd"] + i * 6
                blocks = range(6) if gemm else range(4, 6)
                halves = [(j, k) for j in blocks for k in range(8)]
                per = len(halves) // NT

                def slice_(part):
                    for j, k in part:
                        n = n0 + j if gemm else n0 + j - 4
                        b = j % 2
                        if k == 0:
                            pe.wait_ge(w_lo_done, n + 1)
                            pe.wait_ge(freed[b], O[b]["ssd"] + i * 3 + (j // 2 if gemm else 0))
                        for t in range(2):
                            cols = slice(512 * t, 512 * t + 512)
                            ins = passes(psG[:, b, t, :], b, k, h_hi[:, k, cols], h_lo[:, k, cols], k == 0, k == 7)
                        if k == 7:
                            ins.then_inc(w_used, 1)

                for c in range(NT):
                    part = halves[per * c:per * (c + 1)]
                    ssd_front(i, p, c)
                    slice_(part[:per // 2])
                    ssd_back(i, p, c)
                    slice_(part[per // 2:])

            pe.wait_ge(s_dec, 16)
            with pe.Fori(0, NG // 2 - 1) as i2:
                ssd_iter(i2 * 2, 0, True)
                ssd_iter(i2 * 2 + 1, 1, True)
            ssd_iter(NG - 2, 0, True)
            ssd_iter(NG - 1, 1, False)
            past(pe, s_yacc, NG * 2 + 1)
            for t in range(2):
                ins = mm(psS[:, t, :], ones, y_acc[:, 512 * t:512 * t + 512], start=True, stop=True)
            ins.then_inc(s_yms, 1)
            nc.tensor.drain().then_inc(pe_phase, 2)

            for i in range(1):
                for j in range(2):
                    n = W["yo"] + j
                    pe.wait_ge(w_lo_done, n + 1)
                    if j == 0:
                        pe.wait_ge(freed[0], O[0]["yo"])
                    for k in range(8):
                        pe.wait_ge(s_ylo, 8 * j + k + 1)
                        for t in range(2):
                            cols = slice(512 * t, 512 * t + 512)
                            ins = passes(psG[:, 0, t, :], j, k, y_hi[:, 8 * j + k, cols], y_lo[:, 8 * j + k, cols],
                                         j == 0 and k == 0, j == 1 and k == 7)
                    ins.then_inc(w_used, 1)

            def y_out(n, b, m):
                product(n, 0, b, m, y_hi, y_lo, 8, 0, True, False)
                product(n + 1, 1, b, m, y_hi, y_lo, 8, 8, False, True)

            y_out(W["yo"] + 2, 1, O[1]["yo"])
            with pe.Fori(1, 4) as i:
                y_out(W["yo"] + i * 4, 0, O[0]["yo"] + i)
                y_out(W["yo"] + 2 + i * 4, 1, O[1]["yo"] + i)
            pe.wait_ge(s_mlo, 8)
            with pe.Fori(0, 4) as i:
                for j in range(2):
                    product(W["mix"] + i * 2 + j, j, j, O[j]["mix"] + i, m_hi, m_lo, 8)
            norm_sum(2)
            ffn(1, 2)

            pe.wait_ge(s_acc, 8 * 4)
            for t in range(NT):
                ins = mm(psO[:, t:t + 1], acc[:, t * P:(t + 1) * P], ones[:, 0:1], start=True, stop=True)
            ins.then_inc(s_fms, 1)
            for t in range(NT):
                for u in range(2):
                    i = 2 * t + u
                    at_least(pe, s_orow, i - 1)
                    for j in range(4):
                        ins = transpose(psS[:, u, j * P:(j + 1) * P], xT[:, 4 * u + j, t * P:(t + 1) * P])
                    ins.then_inc(s_ftr, 1)

        @block.scalar
        def _(act):
            ch = Chain(act, c_act_sem)
            for s in (s_exp, s_pta, s_ohi, s_conv_act, s_dec_exp, s_ecs, s_btok, s_ysq, s_yout):
                act.sem_inc(s, CREDIT)
            fn = nc.scalar.activation

            def split_at(base, i, rate, j):
                n = i * rate + base
                assert base % 2 == j and rate % 2 == 0
                act.wait_ge(w_loaded[j], i * (8 * rate) + 16 * (base // 2 + 1))
                at_least(act, w_used, n - 1)
                fn(w_hi[:, j], w_raw[:, j], ACT.Copy).then_inc(w_hi_done, 1)

            def norm_apply(idx, scale, shift, h_free):
                act.wait_ge(s_ms, idx + 1)
                fn(rstd[:], psS[:].rearrange("p a b -> p (a b)"), ACT.Sqrt, scale=1.0 / D, bias=eps_col).then_inc(s_rt, 1)
                for d in range(8):
                    act.wait_ge(s_xr, 8 * idx + d + 1)
                    if d == 0 and h_free:
                        act.wait_ge(w_used, h_free)
                    ch.link(fn(tmp[:, d % 2], tmp[:, d % 2], ACT.Identity, scale=scale[:, d:d + 1],
                               bias=mod[:, shift + d:shift + d + 1]))
                    fn(h_hi[:, d], tmp[:, d % 2], ACT.Copy).then_inc(s_hhi, 1)

            def square(count, src, j, xt_sem, xt_value):
                act.wait_ge(xt_sem, xt_value)
                at_least(act, s_acc, count - 1)
                fn(sq[:, j], src, ACT.Square).then_inc(s_sq, 1)

            def ffn(x, idx):
                for p, (f0, cnt) in enumerate(PARTS):
                    s = f"gu{x}{p}"
                    n0 = W[s]
                    F0 = FT * x + f0
                    U0 = O[1][s]
                    free_at = W[s] if p else (0 if x == 0 else None)

                    def body(i):
                        split_at(n0 + 2, i, 2, 0)
                        act.wait_ge(w_used, i * 2 + n0 + 1)
                        at_least(act, freed[1], i + U0)
                        fn(tmp[:, 0], psG[:, 0].rearrange("p a b -> p (a b)"), ACT.Silu).then_inc(freed[0], 1)
                        split_at(n0 + 3, i, 2, 1)
                        act.wait_ge(freed[1], i + U0 + 1)
                        if p:
                            act.wait_ge(w_used, n0)
                        fn(hid_hi[:, bass.ds(i, 1), :].rearrange("p o t -> p (o t)"), tmp[:, 1], ACT.Copy).then_inc(s_hid_hi, 1)
                    if p == 0:
                        body(0)
                        with ch.loop(1, cnt, 0) as i:
                            body(i)
                    else:
                        with ch.loop(0, cnt, 0) as i:
                            body(i)
                    s = f"dn{x}{p}"
                    n1 = W[s]

                    def down(i, tail=False):
                        for j in range(2):
                            if not tail:
                                split_at(n1 + 2 + j, i, 2, j)
                            if p == 3:
                                d = i * 2 + j
                                src = xT[:, bass.ds(d, 1), :].rearrange("p o t -> p (o t)")
                                square(d + 8 * (idx + 1), src, j, freed[j], O[j][s] + i + 1)
                    last = x == 1 and p == 3
                    with ch.loop(0, 3 if last else 4, 0) as i:
                        down(i)
                    if last:
                        down(3, True)

            act.wait_ge(s_par, 1)
            fn(c_act, par[:, R_C:R_C + 8], ACT.Silu).then_inc(s_cact, 1)
            for t in range(NT):
                for u in range(2):
                    act.wait_ge(s_xtr, 2 * t + u + 1)
                    fn(xT[:, 4 * u:4 * u + 4, t * P:(t + 1) * P], psS[:, u].rearrange("p (j t) -> p j t", j=4),
                       ACT.Copy).then_inc(s_xt, 1)
            for d in range(8):
                square(d, xT[:, d], d % 2, s_xt, 2 * NT)
            split_at(0, 0, 2, 0)
            split_at(1, 0, 2, 1)
            act.wait_ge(s_first_cols, 1)
            norm_apply(0, scale1, SH1, 0)
            ffn(0, 0)
            act.wait_ge(s_first_cols, 2)
            norm_apply(1, scale2, SH2, W["dn03"])

            split_at(W["dt"] + 2, 0, 2, 0)
            split_at(W["dt"] + 3, 0, 2, 1)
            act.wait_ge(s_dt_e, 1)
            ch.link(fn(dt_w[2][0:SH], dt_w[1][0:SH], ACT.Exp, scale=-1.0))
            ch.link(fn(head_col[:, 2:3], head_col[:, 1:2], ACT.Exp))
            fn(dt_w[3][0:SH], dt_w[2][0:SH], ACT.Ln, bias=1.0).then_inc(s_dt_ln, 1)
            act.wait_ge(s_dt_cs, 1)
            for t in range(NT):
                ins = fn(dteT[0:SH, t * P:(t + 1) * P], csT[0:SH, t * P:(t + 1) * P], ACT.Exp, scale=-1.0,
                         bias=csT[0:SH, (t + 1) * P - 1:(t + 1) * P])
            ins.then_inc(s_dt_dte, 1)
            ch.link(fn(dec_head, csT[0:SH, P - 1:T:P], ACT.Exp))
            act.dma_start(cs_keep, csT[0:SH]).then_inc(s_cs_kept, 16)
            act.dma_start(dec_keep, dec_head).then_inc(s_dec_kept, 16)
            act.wait_ge(s_dec_kept, 16)
            act.dma_start(dec_b[:], dec_keep.rearrange("h t -> (h t)")[None, :].to_broadcast([P, SH * NT])
                          .rearrange("p (h t) -> p h t", t=NT)).then_inc(s_dec, 16)
            act.wait_ge(s_ang, 1)
            fn(sinT[:], rt2[:], ACT.Sin).then_inc(s_trig, 1)
            act.wait_ge(s_ang, 2)
            fn(cosT[:], rt2[:], ACT.Sin).then_inc(s_trig, 1)

            def att_done(i, e):
                if e[0] != "half" or e[3] == 0:
                    return
                j, k = e[1], e[2]
                if k != (7, 7, 3, 7)[j]:
                    return
                n = W["att"] + j
                split_at(n + 2, i, 4, j % 2)
                act.wait_ge(w_used, i * 4 + n + 1)
                if j == 0:
                    past(act, s_vtok, i)
                    fn(q_st[:], psG[:, 0].rearrange("p a b -> p (a b)"), ACT.Copy, scale=-(HD ** -0.5)).then_inc(freed[0], 1)
                if j == 1:
                    past(act, s_roped, i * 2)
                    fn(k_st[:], psG[:, 1].rearrange("p a b -> p (a b)"), ACT.Copy).then_inc(freed[1], 1)
                if j == 3:
                    past(act, s_roped, i * 2 + 1)
                    fn(v_st[:], psG[:, 0].rearrange("p a b -> p (a b)"), ACT.Copy).then_inc(freed[0], 1)

            def att_iter(i, par_, att, gemm):
                S = i * NA
                for s in range(NA + 3):
                    if att and s < NA:
                        q, h = ASTEPS[s]
                        past(act, s_masked, S + s + 1)
                        past(act, s_o, S + s - 3)
                        fn(prob[:, s % 2, 0:(q + 1) * P], prob[:, s % 2, 0:(q + 1) * P], ACT.Exp, scale=-1.0,
                           bias=negmax[:, s % 2:s % 2 + 1], accum_out=den[:, s % 4:s % 4 + 1]).then_inc(s_exp, 1)
                    r = s - 1
                    if att and 0 <= r < NA:
                        q, h = ASTEPS[r]
                        past(act, s_tr, i * AGROUP0[NA] + AGROUP0[r] + 1)
                        past(act, s_pv, S + r - 1)
                        w = min(q + 1, 4) * P
                        fn(probT[:, r % 2, 0:w], psT[:, 0:w], ACT.Copy).then_inc(s_pta, 1)
                    if gemm:
                        for e in AEV[s * A_PER_STEP:(s + 1) * A_PER_STEP]:
                            att_done(i + 1, e)
                    r = s - 3
                    if att and 0 <= r < NA and r % 2 == 1:
                        q = ASTEPS[r][0]
                        past(act, s_otr, i * NT + q + 1)
                        dst = o_hi[:, bass.ds(i, 1), q * P:(q + 1) * P].rearrange("p o t -> p (o t)")
                        fn(dst, psT[:, 0:P], ACT.Copy).then_inc(s_ohi, 1)

            act.wait_ge(s_cs_kept, 16)
            att_iter(-1, 0, False, True)
            with ch.loop(0, PAIRS // 2 - 1, 0) as i2:
                att_iter(i2 * 2, 0, True, True)
                att_iter(i2 * 2 + 1, 1, True, True)
            att_iter(PAIRS - 2, 0, True, True)
            att_iter(PAIRS - 1, 1, True, False)
            nc.scalar.drain().then_inc(act_phase, 1)

            with ch.loop(0, 8, 0) as i:
                split_at(W["ga"] + 2, i, 2, 0)
                act.wait_ge(w_used, i * 2 + W["ga"] + 1)
                act.wait_ge(freed[1], i + O[1]["ga"])
                fn(tmp[:, 0], psG[:, 0].rearrange("p a b -> p (a b)"), ACT.Sigmoid).then_inc(freed[0], 1)
                split_at(W["ga"] + 3, i, 2, 1)
                act.wait_ge(freed[1], i + O[1]["ga"] + 1)
                act.dma_start(merged_keep[bass.ds(i, 1)].rearrange("o p t -> (o p) t"), tmp[:, 1]).then_inc(s_mg_out, 16)
            act.wait_ge(s_mg_out, 16 * 8)

            def gb(i, first):
                for j in range(2):
                    split_at(W["gb"] + 2 + j, i, 2, j)
                    act.wait_ge(w_used, i * 2 + W["gb"] + j + 1)
                    if not first:
                        act.wait_ge(s_gt_out[j], i * 16)
                    fn(tmp[:, j], psG[:, j].rearrange("p a b -> p (a b)"), ACT.Sigmoid).then_inc(freed[j], 1)
                    act.wait_ge(freed[j], i + O[j]["gb"] + 1)
                    act.dma_start(gate_keep[bass.ds(i * 2 + j, 1)].rearrange("o p t -> (o p) t"),
                                  tmp[:, j]).then_inc(s_gt_out[j], 16)
            gb(0, True)
            with ch.loop(1, 4, 0) as i:
                gb(i, False)

            def load_cs(g, c):
                src = cs_keep.rearrange("(g e) (c l) -> g c e l", e=GH, l=P)[bass.ds(g, 1), c]
                act.dma_start(cs_b[:, c], src.to_broadcast([P, GH, P])).then_inc(s_csb[c], 16)

            def conv_out(base, i, rate, j, C):
                n = i * rate + base
                act.wait_ge(w_used, n + 1)
                past(act, s_conv, C - 1)
                fn(conv_in[:, j % 2, 4:4 + T], psG[:, j % 2].rearrange("p a b -> p (a b)"), ACT.Copy).then_inc(freed[j % 2], 1)

            def conv_act(i, p, j):
                past(act, s_conv, i * 4 + j + 1)
                t = conv_tile(i, j)
                ins = fn(xbc[:, p, j], xbc[:, p, j], ACT.Silu, bias=par[:, bass.ds(t + R_CB, 1)])
                ins.then_inc(s_conv_act, 1)

            def conv_tile(i, j):
                return (i * 2 + j) if j < 2 else i + (16 if j == 2 else 24)

            act.wait_ge(dve_phase, 1)
            act.wait_ge(pool_phase, 1)
            for c in range(NT):
                load_cs(0, c)
            for j in range(4):
                split_at(W["ssdx"] + 2 + j, 0, 2, j % 2)
                conv_out(W["ssdx"] + j, 0, 2, j, j)
                if j:
                    conv_act(0, 0, j - 1)
            conv_act(0, 0, 3)

            def ssd_iter(i, p, gemm):
                n0 = W["ssd"]
                blocks = range(6) if gemm else range(4, 6)
                per = len(blocks)

                def done(j):
                    base = n0 + j
                    if gemm:
                        split_at(base + 2, i, 6, j % 2)
                        act.wait_ge(w_used, i * 6 + base + 1)
                    else:
                        split_at(W["yo"] + j - 4, 0, 2, j % 2)
                        act.wait_ge(w_used, W["yo"] - 2 + j - 4 + 1)
                    if j == 0:
                        past(act, s_yout, i * 16)
                    if j < 4:
                        conv_out(base, i, 6, j, i * 4 + 4 + j)
                        if j:
                            conv_act(i + 1, 1 - p, j - 1)
                    else:
                        if j == 4 and gemm:
                            conv_act(i + 1, 1 - p, 3)
                        past(act, s_gated, i * 2 + j - 5)
                        fn(z_sil[:, j - 4], psG[:, j % 2].rearrange("p a b -> p (a b)"), ACT.Silu).then_inc(freed[j % 2], 1)

                for c in range(NT):
                    n = i * NT + c
                    past(act, s_tokT, n + 1)
                    past(act, s_st, i * (NT - 1) + max(c - 1, 0))
                    fn(b_tok[:, c % 2], psT[:, 2 * P:3 * P], ACT.Copy).then_inc(s_btok, 1)
                    act.wait_ge(s_csb[c], i * 16 + 16)
                    past(act, s_cscaled, n - 1)
                    fn(ecs[:, c % 2], cs_b[:, c], ACT.Exp).then_inc(s_ecs, 1)
                    past(act, s_arg, n + 1)
                    fn(decay[:, c % 2], decay[:, c % 2], ACT.Exp).then_inc(s_dec_exp, 1)
                    if gemm:
                        past(act, s_ecs, n + 1)
                        load_cs(i + 1, c)
                    for j in blocks:
                        k = (j if gemm else j - 4) * 8 + 7
                        if k // per == c:
                            done(j)
                for j in range(2):
                    past(act, s_gated, i * 2 + j + 1)
                    past(act, s_yacc, i * 2 + j + 1)
                    fn(y_sq[:], xbc[:, p, j], ACT.Square).then_inc(s_ysq, 1)
                act.dma_start(y_keep[bass.ds(i, 1)].rearrange("o p u t -> (o p) u t"), xbc[:, p, 0:2]).then_inc(s_yout, 16)

            with ch.loop(0, NG // 2 - 1, 0) as i2:
                ssd_iter(i2 * 2, 0, True)
                ssd_iter(i2 * 2 + 1, 1, True)
            ssd_iter(NG - 2, 0, True)
            ssd_iter(NG - 1, 1, False)
            act.wait_ge(s_yms, 1)
            fn(y_rstd[:], psS[:].rearrange("p a b -> p (a b)"), ACT.Sqrt, scale=1.0 / INNER, bias=eps_col).then_inc(s_yrt, 1)
            nc.scalar.drain().then_inc(act_phase, 1)

            act.wait_ge(w_used, W["yo"])
            for k in range(16):
                act.wait_ge(s_yin[k // 4], 16)
                fn(y_hi[:, k], y_raw[:, k], ACT.Copy, scale=par[:, R_SN + k:R_SN + k + 1]).then_inc(s_yhi, 1)
            for i in range(1):
                for j in range(2):
                    split_at(W["yo"] + 2 + j, 0, 2, j)
            with ch.loop(1, 8, 0) as i:
                for j in range(2):
                    split_at(W["yo"] + 2 + j, i, 2, j)
            for d in range(8):
                act.wait_ge(s_mg, d + 1)
                if d == 0:
                    act.wait_ge(w_used, W["mix"])
                fn(m_hi[:, d], merged[:, d], ACT.Copy).then_inc(s_mhi, 1)
            with ch.loop(0, 4, 0) as i:
                for j in range(2):
                    split_at(W["mix"] + 2 + j, i, 2, j)
                    d = i * 2 + j
                    src = xT[:, bass.ds(d, 1), :].rearrange("p o t -> p (o t)")
                    square(d + 16, src, j, freed[j], O[j]["mix"] + i + 1)
            norm_apply(2, scale3, SH3, W["gu10"])
            ffn(1, 2)
            act.wait_ge(s_fms, 1)
            fn(rstd[:, 0:NT], psO[:, 0:NT], ACT.Sqrt, scale=1.0 / D, bias=eps_col).then_inc(s_frt, 1)

        @block.vector
        def _(dve):
            ch = Chain(dve, c_dve_sem)
            for s in (s_masked, s_ptb, s_o, s_olo, s_roped, s_vtok, s_conv, s_arg, s_xdte, s_wT, s_state, s_yev, s_gated):
                dve.sem_inc(s, CREDIT)
            v = nc.vector

            def flat(ps):
                return ps.rearrange("p a b -> p (a b)")

            def ada_reduce(q, src):
                dve.wait_ge(s_ada_mul, q + 1)
                at_least(dve, s_ada_mm, q)
                v.tensor_reduce(ada_red[:], src.rearrange("p k m -> p m k"), AXX, ALU.add).then_inc(s_ada_red, 1)

            def ada_finish(q):
                dve.wait_ge(s_ada_mm, q + 1)
                if isinstance(q, int):
                    cols = slice(4 * q, 4 * q + 4)
                else:
                    cols = bass.ds(q * 4, 4)
                v.tensor_tensor(mod[:, cols], psO[:, 0:4], par[:, cols], ALU.add).then_inc(s_ada_done, 1)

            def norm_apply(idx):
                dve.wait_ge(s_rt, idx + 1)
                ch.link(v.reciprocal(rstd[:], rstd[:]))
                for d in range(8):
                    at_least(dve, s_hlo, 8 * idx + d - 1)
                    v.tensor_tensor(tmp[:, d % 2], xT[:, d], rstd[:], ALU.mult).then_inc(s_xr, 1)

            def ffn(x):
                for p, (f0, cnt) in enumerate(PARTS):
                    s = f"gu{x}{p}"
                    n0, G0, U0, F0 = W[s], O[0][s], O[1][s], FT * x + f0

                    def body(i):
                        if x == 0 and p < 2:
                            if not (isinstance(i, int) and i + f0 == 0):
                                ada_finish(i + (f0 + ADA_FIRST - 1))
                            ada_reduce(i + (f0 + ADA_FIRST), ada[:])
                        dve.wait_ge(freed[0], i + G0 + 1)
                        dve.wait_ge(w_used, i * 2 + n0 + 2)
                        at_least(dve, s_hid_lo, i + F0)
                        v.tensor_tensor(tmp[:, 1], tmp[:, 0], flat(psG[:, 1]), ALU.mult).then_inc(freed[1], 1)
                    if p == 0:
                        body(0)
                        with ch.loop(1, cnt, 0) as i:
                            body(i)
                    else:
                        with ch.loop(0, cnt, 0) as i:
                            body(i)
                    if x == 0 and p == 0:
                        dve.wait_ge(s_ada_done, G1 // 4 + 2)
                        v.tensor_scalar(gate1, mod[:, G1:G1 + 8], 0.5, None, ALU.mult).then_inc(s_g1, 1)
                        dve.wait_ge(s_g1, 1)
                    if x == 0 and p == 1:
                        ada_finish(ADA_ALL - 1)
                        dve.wait_ge(s_ada_done, ADA_ALL)
                        ch.link(v.tensor_scalar(gate3, mod[:, G3:G3 + 8], 0.5, None, ALU.mult))
                        ch.link(v.scalar_tensor_tensor(scale3, mod[:, SC3:SC3 + 8], 1.0, par[:, R_N3:R_N3 + 8], ALU.add, ALU.mult))
                        v.scalar_tensor_tensor(scale2, mod[:, SC2:SC2 + 8], 1.0, par[:, R_N2:R_N2 + 8],
                                               ALU.add, ALU.mult).then_inc(s_first_cols, 1)
                    s = f"dn{x}{p}"
                    n1 = W[s]
                    g = gate1 if x == 0 else gate3
                    with ch.loop(0, 4, 0) as i:
                        for j in range(2):
                            d = i * 2 + j
                            dve.wait_ge(w_used, d + n1 + 1)
                            xd = xT[:, bass.ds(d, 1), :].rearrange("p o t -> p (o t)")
                            v.scalar_tensor_tensor(xd, flat(psG[:, j]), g[:, bass.ds(d, 1)], xd,
                                                   ALU.mult, ALU.add).then_inc(freed[j], 1)

            ch.link(v.memset(eps_col, EPS))
            dve.wait_ge(s_par_ps, 1)
            v.tensor_copy(par[:], psT[:, 0:R_ALL]).then_inc(s_par, 1)
            for q in range(ADA_FIRST):
                ada_reduce(q, (ada_a, ada_b)[q % 2][:])
                ada_finish(q)
            dve.wait_ge(s_ada_done, ADA_FIRST)
            v.scalar_tensor_tensor(scale1, mod[:, SC1:SC1 + 8], 1.0, par[:, R_N1:R_N1 + 8],
                                   ALU.add, ALU.mult).then_inc(s_first_cols, 1)
            norm_apply(0)
            ffn(0)
            norm_apply(1)

            dve.wait_ge(s_small, 16 * 3)
            for j in range(2):
                rows = slice(HD * j, HD * j + HD)
                ch.link(v.tensor_copy(d_col[rows], d_row[rows].rearrange("p (a b) -> p b a", b=2)[:, j]))
            dve.wait_ge(w_used, W["dt"] + 2)
            ch.link(v.tensor_scalar(dt_w[0][0:SH], flat(psG[0:SH, 0]), head_col[:, 0:1], None, ALU.add))
            dve.sem_inc(freed[0], 1)
            v.scalar_tensor_tensor(dt_w[1][0:SH], dt_w[0][0:SH], -1.0, dt_w[0][0:SH], ALU.mult, ALU.max).then_inc(s_dt_e, 1)
            dve.wait_ge(s_dt_ln, 1)
            ch.link(v.scalar_tensor_tensor(dtT[0:SH], dt_w[0][0:SH], 0.0, dt_w[3][0:SH], ALU.max, ALU.add))
            ch.link(v.tensor_scalar(dt_w[1][0:SH], dtT[0:SH], head_col[:, 2:3], -1.0, ALU.mult, ALU.mult))
            ch.link(v.memset(dt_w[2][0:SH], 1.0))
            for t in range(NT):
                tok = slice(t * P, (t + 1) * P)
                ins = v.tensor_tensor_scan(csT[0:SH, tok], dt_w[2][0:SH, tok], dt_w[1][0:SH, tok], 0.0, ALU.mult, ALU.add)
            ins.then_inc(s_dt_cs, 1)
            dve.wait_ge(s_dt_dte, 1)
            v.tensor_tensor(dteT[0:SH], dteT[0:SH], dtT[0:SH], ALU.mult).then_inc(s_dt_ready, 1)

            dve.wait_ge(s_pos, 16)
            two_pi = 2.0 * np.pi
            c1 = 6.28125
            c2 = float(np.float32(np.round((two_pi - c1) * 2 ** 19) / 2 ** 19))
            c3 = float(np.float32(two_pi - c1 - c2))
            magic = 1.5 * 2 ** 23
            ch.link(v.tensor_copy(rt1[:], pos_i[:]))
            ch.link(v.tensor_scalar(ang[:], rt1[:], invf, None, ALU.mult))
            for u, (turn, shift) in enumerate(((0.0, 0.0), (0.25, float(np.pi / 2)))):
                ch.link(v.tensor_scalar(rt1[:], ang[:], float(1 / two_pi), turn, ALU.mult, ALU.add))
                ch.link(v.tensor_scalar(rt1[:], rt1[:], magic, None, ALU.add))
                ch.link(v.tensor_scalar(rt1[:], rt1[:], magic, None, ALU.subtract))
                if u:
                    dve.wait_ge(s_trig, 1)
                ch.link(v.scalar_tensor_tensor(rt2[:], rt1[:], -c1, ang[:], ALU.mult, ALU.add))
                ch.link(v.scalar_tensor_tensor(rt2[:], rt1[:], -c2, rt2[:], ALU.mult, ALU.add))
                ch.link(v.scalar_tensor_tensor(rt2[:], rt1[:], -c3, rt2[:], ALU.mult, ALU.add))
                ch.link(v.tensor_scalar(rt2[:], rt2[:], shift, None, ALU.add))
                v.tensor_scalar(rt2[:], rt2[:], 3.1415925, -3.1415925, ALU.min, ALU.max).then_inc(s_ang, 1)

            def att_done(i, par_, e, end=False):
                if end:
                    past(dve, s_vtr, i + 1)
                    v.tensor_copy(v_tok[:, par_].rearrange("p a b -> p (a b)"), flat(psG[:, 1])).then_inc(s_vtok, 1)
                    past(dve, s_vtok, i + 1)
                    dve.sem_inc(freed[1], 1)
                    return
                if e[0] != "rot":
                    return
                b = e[1]
                src, dst = (q_st, k_st)[b], (qT, kT)[b]
                past(dve, s_rot, i * 2 + b + 1)
                ch.link(v.tensor_tensor(dst[:, par_], src[:], cosT[:], ALU.mult))
                v.tensor_tensor(src[:], flat(psG[:, b]), sinT[:], ALU.mult).then_inc(freed[b], 1)
                dve.wait_ge(freed[b], i * 3 + O[b]["att"] + 2)
                v.tensor_tensor(dst[:, par_], dst[:, par_], src[:], ALU.add).then_inc(s_roped, 1)
                past(dve, s_roped, i * 2 + b + 1)

            def att_iter(i, par_, att, gemm):
                S = i * NA
                for s in range(NA + 3):
                    if att and s < NA:
                        q, h = ASTEPS[s]
                        w = (q + 1) * P
                        past(dve, s_qk, S + s + 1)
                        past(dve, s_tr, i * AGROUP0[NA] + (AGROUP0[s - 1] if s else -AGROUPS[NA - 1]))
                        dve.sem_inc(dve_turn, 1)
                        v.tensor_tensor_reduce(out=prob[:, s % 2, 0:w], in0=flat(psS)[:, 0:w], in1=mask[:, T - w:T],
                                               scale=1.0, scalar=3.0e38, op0=ALU.add, op1=ALU.min,
                                               accum_out=negmax[:, s % 2:s % 2 + 1]).then_inc(s_masked, 1)
                    r = s - 1
                    if att and 0 <= r < NA and ASTEPS[r][0] >= 4:
                        q, h = ASTEPS[r]
                        past(dve, s_tr, i * AGROUP0[NA] + AGROUP0[r] + 2)
                        past(dve, s_pv, S + r - 1)
                        v.tensor_copy(probT[:, r % 2, 512:(q + 1) * P], psT[:, 0:(q - 3) * P]).then_inc(s_ptb, 1)
                    r = s - 2
                    if att and 0 <= r < NA:
                        q, h = ASTEPS[r]
                        ch.link(v.reciprocal(rden[:, r % 2:r % 2 + 1], den[:, r % 4:r % 4 + 1]))
                        past(dve, s_pv, S + r + 1)
                        if h == 0:
                            past(dve, s_otr, i * NT + q - 1)
                        v.tensor_scalar(o_tok[:, q % 2, HD * h:HD * h + HD], psO[:, 0:HD],
                                        rden[:, r % 2:r % 2 + 1], None, ALU.mult).then_inc(s_o, 1)
                    r = s - 3
                    if att and 0 <= r < NA and r % 2 == 1:
                        q = ASTEPS[r][0]
                        past(dve, s_ohi, i * NT + q + 1)
                        tok = slice(q * P, (q + 1) * P)
                        hi = o_hi[:, bass.ds(i, 1), tok].rearrange("p o t -> p (o t)").bitcast(F32)
                        lo = o_lo[:, bass.ds(i, 1), tok].rearrange("p o t -> p (o t)")
                        v.tensor_tensor(lo, psT[:, 0:P], hi, ALU.subtract).then_inc(s_olo, 1)
                    if gemm:
                        for e in AEV[s * A_PER_STEP:(s + 1) * A_PER_STEP]:
                            att_done(i + 1, 1 - par_, e)
                if gemm:
                    att_done(i + 1, 1 - par_, None, True)

            dve.wait_ge(s_trig, 2)
            att_iter(-1, 1, False, True)
            dve.wait_ge(s_dt_tr, 1)
            dve.wait_ge(s_mask, 16)
            ch.link(v.tensor_copy(cs_tok[:].rearrange("p a b -> p (a b)"), psS[:, 0, 0:256]))
            ch.link(v.tensor_copy(dt_keep[:], psS[:, 0, 256:512]))
            v.tensor_copy(dte_tok[:].rearrange("p a b -> p (a b)"), psS[:, 1, 0:256]).then_inc(s_dt_tok, 1)
            dve.wait_ge(s_dt_tok, 1)
            with ch.loop(0, PAIRS // 2 - 1, 2 * NA + 4) as i2:
                att_iter(i2 * 2, 0, True, True)
                att_iter(i2 * 2 + 1, 1, True, True)
            att_iter(PAIRS - 2, 0, True, True)
            att_iter(PAIRS - 1, 1, True, False)
            past(dve, s_olo, PAIRS * NT)
            nc.vector.drain().then_inc(dve_phase, 1)

            def ga(i, first):
                dve.wait_ge(freed[0], i + O[0]["ga"] + 1)
                dve.wait_ge(w_used, i * 2 + W["ga"] + 2)
                if not first:
                    dve.wait_ge(s_mg_out, i * 16)
                v.tensor_tensor(tmp[:, 1], tmp[:, 0], flat(psG[:, 1]), ALU.mult).then_inc(freed[1], 1)
            dve.wait_ge(act_phase, 1)
            ga(0, True)
            with ch.loop(1, 8, 0) as i:
                ga(i, False)

            def conv(i, p, j, n):
                C = i * 4 + j
                dve.wait_ge(freed[j % 2], n)
                t = (i * 2 + j) if j < 2 else i + (16 if j == 2 else 24)
                for u in range(4):
                    tap = par[:, bass.ds(t + (R_CW + 32 * (3 - u)), 1)]
                    src = conv_in[:, j % 2, 4 - u:4 - u + T]
                    if u == 0:
                        ch.link(v.tensor_scalar(xbc[:, p, j], src, tap, None, ALU.mult))
                    else:
                        ins = v.scalar_tensor_tensor(xbc[:, p, j], src, tap, xbc[:, p, j], ALU.mult, ALU.add)
                        if u < 3:
                            ch.link(ins)
                ins.then_inc(s_conv, 1)

            dve.wait_ge(w_used, W["gb"])
            dve.wait_ge(s_dec, 16)
            ch.link(v.tensor_copy(dt_tok[:].rearrange("p a b -> p (a b)"), dt_keep[:]))
            for j in range(2):
                ch.link(v.memset(conv_in[:, j, 0:4], 0.0))
            for j in range(4):
                conv(0, 0, j, O[j % 2]["ssdx"] + j // 2 + 1)

            def ssd_iter(i, p, gemm):
                blocks = range(4) if gemm else ()
                for c in range(NT):
                    n = i * NT + c
                    heads = bass.ds(i * GH, GH)
                    dve.wait_ge(s_csb[c], i * 16 + 16)
                    past(dve, s_wT, n - 1)
                    for e in range(GH):
                        ins = v.scalar_tensor_tensor(decay[:, c % 2, e], cs_b[:, c, e], cs_tok[:, c, bass.ds(i * GH + e, 1)],
                                                     causal, ALU.subtract, ALU.add)
                    ins.then_inc(s_arg, 1)
                    past(dve, s_tokT, n + 1)
                    past(dve, s_btok, n + 1)
                    past(dve, s_y, n - 1)
                    past(dve, s_st, i * (NT - 1) + max(c - 1, 0))
                    xt = psT[:, 0:2 * P].rearrange("p (e d) -> p e d", e=GH)
                    v.tensor_tensor(xdt[:, c % 2].rearrange("p (e d) -> p e d", e=GH), xt,
                                    dt_tok[:, c, heads].unsqueeze(2).to_broadcast([P, GH, HD]), ALU.mult)
                    v.tensor_tensor(xdte[:, c % 2].rearrange("p (e d) -> p e d", e=GH), xt,
                                    dte_tok[:, c, heads].unsqueeze(2).to_broadcast([P, GH, HD]), ALU.mult).then_inc(s_xdte, 1)
                    past(dve, s_dec_exp, n + 1)
                    past(dve, s_cb, n + 1)
                    v.tensor_tensor(wT[:, c % 2], decay[:, c % 2],
                                    psS[:, 0, 0:P].unsqueeze(1).to_broadcast([P, GH, P]), ALU.mult).then_inc(s_wT, 1)
                    past(dve, s_y, n + 1)
                    for j in range(2):
                        tok = slice(c * P, (c + 1) * P)
                        ins = v.scalar_tensor_tensor(xbc[:, p, j, tok], xbc[:, p, j, tok], d_col[:, bass.ds(i * 2 + j, 1)],
                                                     psS[:, 1, j * P:(j + 1) * P], ALU.mult, ALU.add)
                    ins.then_inc(s_yev, 1)
                    if c < NT - 1:
                        past(dve, s_st, i * (NT - 1) + c + 1)
                        if c == 0:
                            v.tensor_copy(state[:, 0], psO[:, 0:2 * P]).then_inc(s_state, 1)
                        else:
                            dcol = dec_b[:, heads, c:c + 1].to_broadcast([P, GH, HD])
                            cur = state[:, c % 2].rearrange("p (e d) -> p e d", e=GH)
                            old = state[:, (c - 1) % 2].rearrange("p (e d) -> p e d", e=GH)
                            ch.link(v.tensor_tensor(cur, old, dcol, ALU.mult))
                            v.tensor_tensor(state[:, c % 2], state[:, c % 2], psO[:, 0:2 * P], ALU.add).then_inc(s_state, 1)
                        past(dve, s_state, i * (NT - 1) + c + 1)
                    for j in blocks:
                        if (8 * j + 7) // 6 == c:
                            conv(i + 1, 1 - p, j, i * 3 + O[j % 2]["ssd"] + j // 2 + 1)
                past(dve, s_yev, i * NT + NT)
                for j in range(2):
                    last_out = i * 3 + O[j]["ssd"] + (3 if gemm else 1)
                    dve.wait_ge(freed[j], last_out)
                    v.tensor_tensor(xbc[:, p, j], xbc[:, p, j], z_sil[:, j], ALU.mult).then_inc(s_gated, 1)

            with ch.loop(0, NG // 2 - 1, 2 * (6 + 12)) as i2:
                ssd_iter(i2 * 2, 0, True)
                ssd_iter(i2 * 2 + 1, 1, True)
            ssd_iter(NG - 2, 0, True)
            ssd_iter(NG - 1, 1, False)
            nc.vector.drain().then_inc(dve_phase, 1)
            dve.wait_ge(s_yrt, 1)
            ch.link(v.reciprocal(y_rstd[:], y_rstd[:]))
            for k in range(16):
                dve.wait_ge(s_yhi, k + 1)
                v.scalar_tensor_tensor(y_lo[:, k], y_raw[:, k], par[:, R_SN + k:R_SN + k + 1], y_hi[:, k].bitcast(F32),
                                       ALU.mult, ALU.subtract).then_inc(s_ylo, 1)
            dve.wait_ge(s_mg_in, 16)
            with ch.loop(0, 4, 2) as i:
                for j in range(2):
                    d = i * 2 + j
                    md = merged[:, bass.ds(d, 1), :].rearrange("p o t -> p (o t)")
                    dve.wait_ge(w_used, i * 4 + (W["yo"] + 2 * j + 2))
                    v.tensor_tensor(tmp[:, j], flat(psG[:, j]), y_rstd[:], ALU.mult).then_inc(freed[j], 1)
                    dve.wait_ge(freed[j], i + O[j]["yo"] + 1)
                    dve.wait_ge(s_gt_in, d * 16 + 16)
                    ch.link(v.tensor_tensor(tmp[:, j], tmp[:, j], gate[:], ALU.mult))
                    v.tensor_tensor(md, md, tmp[:, j], ALU.add).then_inc(s_mg, 1)
            dve.wait_ge(s_xback, 16)
            with ch.loop(0, 4, 0) as i:
                for j in range(2):
                    d = i * 2 + j
                    dve.wait_ge(w_used, d + W["mix"] + 1)
                    xd = xT[:, bass.ds(d, 1), :].rearrange("p o t -> p (o t)")
                    v.scalar_tensor_tensor(xd, flat(psG[:, j]), mod[:, bass.ds(d + G2, 1)], xd,
                                           ALU.mult, ALU.add).then_inc(freed[j], 1)
            norm_apply(2)
            ffn(1)
            dve.wait_ge(s_frt, 1)
            ch.link(v.reciprocal(rstd[:, NT:2 * NT], rstd[:, 0:NT]))
            dve.wait_ge(s_wf, 16)
            for t in range(NT):
                for u in range(2):
                    dve.wait_ge(s_ftr, 2 * t + u + 1)
                    if t >= 2 and u == 0:
                        dve.wait_ge(s_out[t % 2], 16 * (t // 2))
                    cols = slice(512 * u, 512 * u + 512)
                    v.scalar_tensor_tensor(o_row[:, t % 2, cols], psS[:, u, :], rstd[:, NT + t:NT + t + 1],
                                           w_final[:, cols], ALU.mult, ALU.mult).then_inc(s_orow, 1)

        @block.gpsimd
        def _(pool):
            ch = Chain(pool, c_pool_sem)
            for s in (s_cscaled, s_yacc):
                pool.sem_inc(s, CREDIT)
            g = nc.gpsimd

            def split(n, j):
                pool.wait_ge(w_hi_done, n + 1)
                g.tensor_tensor(w_lo[:, j], w_raw[:, j], w_hi[:, j].bitcast(F32), ALU.subtract).then_inc(w_lo_done, 1)

            def ada_mul(q, buf, loaded, value):
                pool.wait_ge(loaded, value)
                g.tensor_tensor(buf, buf, c_act.unsqueeze(2).to_broadcast([P, 8, ADA_W]), ALU.mult).then_inc(s_ada_mul, 1)

            def norm_apply(idx):
                for d in range(8):
                    pool.wait_ge(s_hhi, 8 * idx + d + 1)
                    g.tensor_tensor(h_lo[:, d], tmp[:, d % 2], h_hi[:, d].bitcast(F32), ALU.subtract).then_inc(s_hlo, 1)

            def add_square(count, j, first):
                pool.wait_ge(s_sq, count + 1)
                if first:
                    g.tensor_copy(acc[:], sq[:, j]).then_inc(s_acc, 1)
                else:
                    pool.wait_ge(s_acc, count)
                    g.tensor_tensor(acc[:], acc[:], sq[:, j], ALU.add).then_inc(s_acc, 1)

            def ffn(x, idx):
                for p, (f0, cnt) in enumerate(PARTS):
                    s = f"gu{x}{p}"
                    n0, F0 = W[s], FT * x + f0

                    def body(i):
                        if x == 0 and p < 2:
                            ada_mul(i + f0 + ADA_FIRST, ada[:], s_ada[2], i * 16 + (16 * f0 + 16))
                        split(i * 2 + (n0 + 2), 0)
                        split(n0 + 3 + i * 2, 1)
                        pool.wait_ge(s_hid_hi, i + F0 + 1)
                        at = hid_hi[:, bass.ds(i, 1), :].rearrange("p o t -> p (o t)").bitcast(F32)
                        to = hid_lo[:, bass.ds(i, 1), :].rearrange("p o t -> p (o t)")
                        g.tensor_tensor(to, tmp[:, 1], at, ALU.subtract).then_inc(s_hid_lo, 1)
                    if p == 0:
                        body(0)
                        with ch.loop(1, cnt, 0) as i:
                            body(i)
                    else:
                        with ch.loop(0, cnt, 0) as i:
                            body(i)
                    s = f"dn{x}{p}"
                    n1 = W[s]

                    def down(i, tail=False):
                        for j in range(2):
                            if not tail:
                                split(n1 + 2 + j + i * 2, j)
                            if p == 3:
                                add_square(i * 2 + j + 8 * (idx + 1), j, isinstance(i, int) and i == 0 and j == 0)
                    last = x == 1 and p == 3
                    down(0)
                    with ch.loop(1, 3 if last else 4, 0) as i:
                        down(i)
                    if last:
                        down(3, True)

            pool.wait_ge(s_cact, 1)
            for q in range(ADA_FIRST):
                ada_mul(q, (ada_a, ada_b)[q % 2][:], s_ada[q % 2], 16 * (q // 2 + 1))
            for d in range(8):
                add_square(d, d % 2, d == 0)
            split(0, 0)
            split(1, 1)
            norm_apply(0)
            ffn(0, 0)
            norm_apply(1)
            pool.wait_ge(s_xkeep, 16)
            g.dma_start(pos_i[:], positions.to_broadcast([P, T])).then_inc(s_pos, 16)
            g.dma_start(mask[:], table[:, K_MASK:K_MASK + T]).then_inc(s_mask, 16)
            split(W["dt"] + 2, 0)
            split(W["dt"] + 3, 1)
            with ch.loop(0, PAIRS, 0) as i:
                for j in range(4):
                    split(W["att"] + 2 + j + i * 4, j % 2)
            nc.gpsimd.drain().then_inc(pool_phase, 1)
            with ch.loop(0, 12, 0) as i:
                for j in range(2):
                    split(W["ga"] + 2 + j + i * 2, j)
            g.memset(y_acc[:], 0.0).then_inc(s_yacc, 1)
            past(pool, s_yacc, 1)
            for j in range(4):
                split(W["ssdx"] + 2 + j, j % 2)

            def ssd_iter(i, p, gemm):
                blocks = range(6) if gemm else range(4, 6)
                per = len(blocks)
                for c in range(NT):
                    n = i * NT + c
                    if c == 0:
                        past(pool, s_conv_act, i * 4 + 4)
                    past(pool, s_ecs, n + 1)
                    past(pool, s_y, n - 1)
                    g.tensor_tensor(c_scaled[:, c % 2], ecs[:, c % 2],
                                    xbc[:, p, 3, c * P:(c + 1) * P].unsqueeze(1).to_broadcast([P, GH, P]),
                                    ALU.mult).then_inc(s_cscaled, 1)
                    for j in blocks:
                        k = (j if gemm else j - 4) * 8 + 7
                        if k // per == c:
                            split((W["ssd"] + 2 + j + i * 6) if gemm else W["yo"] + j - 4, j % 2)
                for j in range(2):
                    past(pool, s_ysq, i * 2 + j + 1)
                    past(pool, s_yacc, i * 2 + j + 1)
                    g.tensor_tensor(y_acc[:], y_acc[:], y_sq[:], ALU.add).then_inc(s_yacc, 1)

            with ch.loop(0, NG // 2 - 1, 0) as i2:
                ssd_iter(i2 * 2, 0, True)
                ssd_iter(i2 * 2 + 1, 1, True)
            ssd_iter(NG - 2, 0, True)
            ssd_iter(NG - 1, 1, False)
            nc.gpsimd.drain().then_inc(pool_phase, 1)
            with ch.loop(0, 8, 0) as i:
                for j in range(2):
                    split(W["yo"] + 2 + j + i * 2, j)
            for d in range(8):
                pool.wait_ge(s_mhi, d + 1)
                g.tensor_tensor(m_lo[:, d], merged[:, d], m_hi[:, d].bitcast(F32), ALU.subtract).then_inc(s_mlo, 1)

            def mix(i):
                for j in range(2):
                    split(W["mix"] + 2 + j + i * 2, j)
                    add_square(i * 2 + j + 16, j, isinstance(i, int) and i == 0 and j == 0)
            mix(0)
            with ch.loop(1, 4, 0) as i:
                mix(i)
            norm_apply(2)
            ffn(1, 2)


_INS = ["x", "c", "positions", "w_ada", "b_ada", "norm1_w", "ffn1_w_gu", "ffn1_w_down", "norm2_w", "w_in",
        "conv_w", "conv_b", "dt_bias", "a_log", "d_skip", "ssd_norm_w", "w_att_out", "w_ssd_out", "w_mix_out",
        "norm3_w", "ffn2_w_gu", "ffn2_w_down", "final_norm_w"]


def kernel(**inputs):
    import numpy as _np
    import concourse.bacc as _bacc
    from concourse import mybir as _mybir
    from concourse.bass_utils import run_bass_kernel_spmd as _run

    nc = _bacc.Bacc("TRN2", target_bir_lowering=False, num_devices=1)
    arrays, args = {}, []
    for name in _INS:
        a = _np.ascontiguousarray(inputs[name])
        arrays[f"in_{name}"] = a
        args.append(nc.dram_tensor(f"in_{name}", a.shape, _mybir.dt.from_np(a.dtype), kind="ExternalInput").ap())
    arrays["in_table"] = constants()
    args.append(nc.dram_tensor("in_table", arrays["in_table"].shape, F32, kind="ExternalInput").ap())
    shape = tuple(inputs["x"].shape)
    args.append(nc.dram_tensor("out_0", shape, F32, kind="ExternalOutput").ap())
    kernel_program(nc, *args)
    r = _run(nc, [arrays], core_ids=[0])
    return r.results[0]["out_0"]
```

```python
from contextlib import ExitStack, contextmanager

import numpy as np
import concourse.bass as bass
from concourse import mybir

F32 = mybir.dt.float32
F32R = mybir.dt.float32r
I32 = mybir.dt.int32
ALU = mybir.AluOpType
ACT = mybir.ActivationFunctionType
AXX = mybir.AxisListType.X

P = 128
D = 1024
T = 1024
DT_ = D // P
NT = T // P
FF = 2816
FT = FF // P
AH, HD = 12, 64
PAIRS = AH // 2
NG, GH = 8, 4
SH = NG * GH
INNER = 2 * D
AW = AH * HD
ROPE, THETA = HD // 4, 500000.0
O_Q, O_K, O_V = 0, AW, 2 * AW
O_Z = 3 * AW
O_X = O_Z + INNER
O_B = O_X + INNER
O_C = O_B + NG * P
O_DT = O_C + NG * P
O_G0 = O_DT + SH
O_G1 = O_G0 + D
EPS = 1e-6
NEG = -1e30
PATTERNS = ((128, 1), (512, 4), (2048, 16))

PARTS = ((0, 7), (7, 7), (14, 4), (18, 4))
ADA_W = 512
ADA_FIRST = 2 * D // ADA_W
ADA_ALL = 9 * D // ADA_W
assert PARTS[0][1] + PARTS[1][1] == ADA_ALL - ADA_FIRST

K_ID, K_ONE, K_NEG, K_ROT, K_INVF = 0, P, 2 * P, 3 * P, 4 * P
K_PERSIST = 4 * P + 1
K_MASK = K_PERSIST
K_ALL = K_MASK + T

R_ADA, R_N1, R_N2, R_N3, R_SN, R_C = 0, 72, 80, 88, 96, 112
R_P1 = 120
R_CW = R_P1
R_CB = R_CW + 4 * 32
R_ALL = R_CB + 32


def constants():
    k = np.zeros((P, K_ALL), np.float32)
    k[:, K_ID:K_ID + P] = np.eye(P)
    k[:, K_ONE:K_ONE + P] = 1.0
    s, l = np.arange(P)[:, None], np.arange(P)[None, :]
    k[:, K_NEG:K_NEG + P] = np.where(s <= l, 0.0, NEG)
    half = ROPE // 2
    for h in (0, HD):
        for m in range(half):
            k[h + m + half, K_ROT + h + m] = -1.0
            k[h + m, K_ROT + h + m + half] = 1.0
        inv = np.float32(THETA) ** (-np.arange(0, ROPE, 2, dtype=np.float32) / np.float32(ROPE))
        k[h:h + half, K_INVF] = inv
        k[h + half:h + ROPE, K_INVF] = inv
    dist = np.arange(P)[:, None] - np.arange(T)[None, :] + (T - P)
    n = sum(((dist >= 0) & (dist <= w) & (dist % r == 0)).astype(int) for w, r in PATTERNS)
    k[:, K_MASK:] = np.where(n > 0, -np.log(np.maximum(n, 1)), -NEG)
    return k


class Chain:

    def __init__(self, eng, sem):
        self.eng, self.sem, self.base, self.term, self.count = eng, sem, 0, None, 0

    def value(self):
        v = self.base + self.count
        return v if self.term is None else self.term + v

    def link(self, instruction):
        self.count += 1
        instruction.then_inc(self.sem, 1)
        self.eng.wait_ge(self.sem, self.value())

    @contextmanager
    def loop(self, start, end, rate):
        base = self.base + self.count
        with self.eng.Fori(start, end) as i:
            self.base, self.count, self.term = base - start * rate, 0, i * rate if rate else None
            yield i
            assert self.count == rate, (self.count, rate)
        self.base, self.count, self.term = base + (end - start) * rate, 0, None


def at_least(eng, sem, value):
    if not (isinstance(value, int) and value <= 0):
        eng.wait_ge(sem, value)


CREDIT = 64


def past(eng, sem, value):
    eng.wait_ge(sem, value + CREDIT)


def plan():
    w, o0, o1 = {}, {}, {}
    n, m0, m1 = 0, 0, 0

    def section(name, blocks, outs0, outs1):
        nonlocal n, m0, m1
        w[name], o0[name], o1[name] = n, m0, m1
        n, m0, m1 = n + blocks, m0 + outs0, m1 + outs1

    def ffn(x):
        for p, (_, cnt) in enumerate(PARTS):
            section(f"gu{x}{p}", 2 * cnt, cnt, cnt)
            section(f"dn{x}{p}", 8, 4, 4)

    ffn(0)
    section("dt", 2, 1, 0)
    section("att", 4 * PAIRS, 3 * PAIRS, 3 * PAIRS)
    section("gba", 4, 2, 2)
    section("ga", 16, 8, 8)
    section("ssdx", 4, 2, 2)
    section("ssd", 6 * NG, 3 * NG, 3 * NG)
    section("yo", 16, 4, 4)
    section("mix", 8, 4, 4)
    ffn(1)
    section("end", 0, 0, 0)
    return w, (o0, o1)


def following(i, p, c):
    return (i, p, c + 1) if c < NT - 1 else (i + 1, 1 - p, 0)


W, O = plan()
BLOCKS = W["end"]

ASTEPS = [(q, h) for q in range(NT) for h in range(2)]
AGROUPS = [1 + (q >= 4) for q, _ in ASTEPS]
AGROUP0 = [sum(AGROUPS[:s]) for s in range(len(ASTEPS) + 1)]
AGB0 = [sum(g - 1 for g in AGROUPS[:s]) for s in range(len(ASTEPS) + 1)]
NA = len(ASTEPS)


def att_events():
    ev = [("half", 0, k, t) for k in range(8) for t in range(2)]
    ev += [("half", 1, k, t) for k in range(4) for t in range(2)]
    ev += [("rot", 0)]
    ev += [("half", 1, k, t) for k in range(4, 8) for t in range(2)]
    ev += [("half", 2, k, t) for k in range(4) for t in range(2)]
    ev += [("rot", 1)]
    ev += [("half", 3, k, t) for k in range(4, 8) for t in range(2)]
    return ev


AEV = att_events()
A_PER_STEP = 3
GEV = [("gate", j, k, t) for j in range(4) for k in range(8) for t in range(2)]
G_PER_STEP = 4


def step_events(s, gemm):
    ev, per = (AEV, A_PER_STEP) if gemm else (GEV, G_PER_STEP)
    return ev[s * per:(s + 1) * per]


def kernel_program(nc, x, c, positions, w_ada, b_ada, norm1_w, ffn1_w_gu, ffn1_w_down, norm2_w, w_in,
                   conv_w, conv_b, dt_bias, a_log, d_skip, ssd_norm_w, w_att_out, w_ssd_out, w_mix_out,
                   norm3_w, ffn2_w_gu, ffn2_w_down, final_norm_w, table, out):
    ctx = ExitStack()
    with ctx:
        def dram(name, shape):
            return nc.dram_tensor(name, shape, F32, kind="Internal").ap()

        x_keep = dram("x_keep", (P, DT_, T))
        merged_keep = dram("merged_keep", (DT_, P, T))
        gate_keep = dram("gate_keep", (DT_, P, T))
        y_keep = dram("y_keep", (NG, P, 2, T))
        cs_keep = dram("cs_keep", (SH, T))
        dec_keep = dram("dec_keep", (SH, NT))

        SLAB_KB = 207.125
        origin = 16512
        ctx.enter_context(nc.sbuf_tensor("slab", [P, int(SLAB_KB * 256)], F32))

        def sb(name, kb, shape, dt=F32):
            size = int(np.prod(shape)) * 4
            assert kb * 1024 + size <= SLAB_KB * 1024, name
            return nc.alloc_sbuf_tensor_at(name, [P, *shape], dt, offset=origin + int(kb * 1024))

        w_raw = sb("w_raw", 0, [2, 8, P])
        w_hi = sb("w_hi", 8, [2, 8, P], F32R)
        w_lo = sb("w_lo", 16, [2, 8, P], F32R)
        h_hi = sb("h_hi", 24, [8, T], F32R)
        h_lo = sb("h_lo", 56, [8, T], F32R)
        xT = sb("xT", 88, [8, T])
        hid_hi = sb("hid_hi", 120, [7, T], F32R)
        hid_lo = sb("hid_lo", 148, [7, T], F32R)
        ada = sb("ada", 176, [8, ADA_W])
        acc = sb("acc", 176, [T])
        rstd = sb("rstd", 180, [T])
        sq = sb("sq", 184, [2, T])
        tmp = sb("tmp", 192, [2, T])
        x_nat = sb("x_nat", 120, [4, D])
        ada_a = sb("ada_a", 136, [8, ADA_W])
        ada_b = sb("ada_b", 152, [8, ADA_W])
        par1 = sb("par1", 168, [3, P])
        w_final = sb("w_final", 120, [D])
        o_row = sb("o_row", 124, [2, D])
        cosT = sb("cosT", 88, [T])
        sinT = sb("sinT", 92, [T])
        q_st = sb("q_st", 96, [T])
        k_st = sb("k_st", 100, [T])
        v_st = sb("v_st", 96, [T])
        dt_keep = sb("dt_keep", 104, [NT * SH])
        o_tok = sb("o_tok", 105, [2, P])
        qT = sb("qT", 108, [2, T])
        kT = sb("kT", 116, [2, T])
        v_tok = sb("v_tok", 124, [2, NT, P])
        prob = sb("prob", 132, [2, T])
        mask = sb("mask", 140, [T])
        o_hi = sb("o_hi", 144, [PAIRS, T], F32R)
        o_lo = sb("o_lo", 168, [PAIRS, T], F32R)
        probT = sb("probT", 192, [2, T])
        pos_i = sb("pos_i", 132, [T], I32)
        ang = sb("ang", 136, [T])
        rt1 = sb("rt1", 124, [T])
        rt2 = sb("rt2", 128, [T])
        dt_w = [sb(f"dt_w{j}", 144 + 4 * j, [T]) for j in range(4)]
        dtT = sb("dtT", 160, [T])
        csT = sb("csT", 164, [T])
        dteT = sb("dteT", 168, [T])
        conv_in = sb("conv_in", 88, [2, T + 4])
        xbc = sb("xbc", 97, [2, 4, T])
        z_sil = sb("z_sil", 129, [2, T])
        cs_b = sb("cs_b", 137, [NT, GH, P])
        decay = sb("decay", 153, [2, GH, P])
        wT = sb("wT", 157, [2, GH, P])
        c_scaled = sb("c_scaled", 161, [2, GH, P])
        ecs = sb("ecs", 165, [2, GH, P])
        xdt = sb("xdt", 169, [2, 2 * P])
        xdte = sb("xdte", 171, [2, 2 * P])
        b_tok = sb("b_tok", 173, [2, P])
        state = sb("state", 174, [2, 2 * P])
        y_sq = sb("y_sq", 176, [T])
        y_acc = sb("y_acc", 180, [T])
        y_hi = sb("y_hi", 24, [16, T], F32R)
        y_lo = sb("y_lo", 88, [16, T], F32R)
        y_raw = sb("y_raw", 88, [16, T])
        merged = sb("merged", 152, [8, T])
        y_rstd = sb("y_rstd", 184, [T])
        gate = sb("gate", 188, [T])
        m_hi = sb("m_hi", 24, [8, T], F32R)
        m_lo = sb("m_lo", 56, [8, T], F32R)
        kst = sb("kst", 200, [K_PERSIST + 1])
        par = sb("par", 202.125, [R_ALL])
        mod = sb("mod", 203.25, [72])
        small = sb("small", 203.5625, [112])
        rcol = sb("rcol", 207, [NT])
        ada_red = sb("ada_red", 204, [ADA_W])
        cs_tok = sb("cs_tok", 204, [NT, SH])
        dte_tok = sb("dte_tok", 205, [NT, SH])
        dec_b = sb("dec_b", 206, [SH, NT])
        dt_tok = sb("dt_tok", 191, [NT, SH])
        assert K_PERSIST + 1 <= 544 and R_ALL <= 288 and 202.125 + R_ALL / 256 <= 203.25

        Y_EARLY = 3
        assert 88 + 8 * Y_EARLY <= 97 + 16

        ident = kst[:, K_ID:K_ID + P]
        ones = kst[:, K_ONE:K_ONE + P]
        causal = kst[:, K_NEG:K_NEG + P]
        rotm = kst[:, K_ROT:K_ROT + P]
        invf = kst[:, K_INVF:K_INVF + 1]
        c_act = small[:, 0:8]
        scale1, scale2, scale3 = (small[:, 8 + 8 * j:16 + 8 * j] for j in range(3))
        gate1, gate3 = small[:, 32:40], small[:, 40:48]
        d_col = small[:, 48:64]
        negmax = small[:, 64:66]
        den = small[:, 74:78]
        rden = small[:, 68:70]
        head_col = small[0:SH, 70:73]
        d_row = small[:, 78:110]
        eps_col = small[:, 110:111]
        dec_head = dt_w[3][0:SH, 0:NT]
        SH1, SC1, G1, SH2, SC2, G2, SH3, SC3, G3 = (8 * j for j in range(9))

        psG = ctx.enter_context(nc.psum_tensor("psG", [P, 2, 2, 512], F32))
        psS = ctx.enter_context(nc.psum_tensor("psS", [P, 2, 512], F32))
        psT = ctx.enter_context(nc.psum_tensor("psT", [P, 512], F32))
        psO = ctx.enter_context(nc.psum_tensor("psO", [P, 512], F32))

        def sem(name):
            return ctx.enter_context(nc.semaphore(name))

        w_loaded = [sem("w_loaded0"), sem("w_loaded1")]
        w_hi_done, w_lo_done, w_used = sem("w_hi_done"), sem("w_lo_done"), sem("w_used")
        freed = [sem("psum0_read"), sem("psum1_read")]
        s_table, s_rows, s_small, s_xin, s_xtr, s_xt = (sem(n) for n in (
            "table_loaded", "rows_loaded", "small_loaded", "x_loaded", "x_transposed", "xT_written"))
        s_par_ps, s_par, s_cact = sem("par_transposed"), sem("par_written"), sem("c_act_done")
        s_ada = [sem(f"ada_loaded{j}") for j in range(3)]
        s_ada_mul, s_ada_red, s_ada_mm, s_ada_done = (sem(n) for n in (
            "ada_scaled", "ada_reduced", "ada_summed", "mod_written"))
        s_first_cols, s_g1 = sem("scale_columns"), sem("gate1_column")
        s_sq, s_acc, s_ms, s_rt, s_diag, s_spread, s_xr, s_hhi = (sem(n) for n in (
            "squared", "squares_added", "square_sums", "root_done", "diagonals", "rstd_spread", "x_scaled",
            "h_hi_done"))
        s_hlo, s_eps = [sem("h_lo_even"), sem("h_lo_odd")], sem("eps_written")
        s_hid_hi, s_hid_lo = sem("hid_hi_done"), sem("hid_lo_done")
        s_xkeep, s_xback = sem("x_kept"), sem("x_back")
        s_dt_e, s_dt_ln, s_dt_cs, s_dt_dte, s_dt_ready, s_dt_tr, s_dt_tok = (sem(n) for n in (
            "dt_abs", "dt_log", "cs_done", "dte_exp", "dte_done", "dt_transposed", "dt_tok_done"))
        s_cs_kept, s_dec, s_dec_kept = sem("cs_kept"), sem("dec_loaded"), sem("dec_kept")
        s_pos, s_mask, s_ang, s_trig = sem("pos_loaded"), sem("mask_loaded"), sem("angle_done"), sem("trig_done")
        s_qk, s_masked, s_exp, s_tr, s_pta, s_ptb, s_pv, s_o, s_otr, s_ohi, s_olo = (sem(n) for n in (
            "qk_done", "masked", "exp_done", "prob_transposed", "probT_a", "probT_b", "pv_done", "o_scaled",
            "o_transposed", "o_hi_done", "o_lo_done"))
        s_rot, s_roped, s_vtr, s_vtok = sem("rot_done"), sem("roped"), sem("v_transposed"), sem("v_tok_done")
        s_mg_out, s_gt_out = sem("merged_kept"), [sem("gate_kept0"), sem("gate_kept1")]
        s_conv_in, s_conv, s_conv_act = sem("conv_in_done"), sem("conv_done"), sem("conv_act_done")
        s_csb = [sem(f"cs_b_loaded{j}") for j in range(NT)]
        s_arg, s_dec_exp, s_ecs, s_cscaled, s_tokT, s_cb, s_btok, s_xdte, s_wT, s_y, s_st, s_state, s_yev = (
            sem(n) for n in ("decay_arg", "decay_exp", "ecs_done", "c_scaled_done", "tok_transposed", "cb_done",
                             "b_tok_done", "xdte_done", "wT_done", "y_done", "state_mm", "state_done", "y_evac"))
        s_gated, s_ysq, s_yacc, s_yout = sem("y_gated"), sem("y_squared"), sem("y_sq_added"), sem("y_kept")
        s_yin = [sem(f"y_loaded{g}") for g in range(NG)]
        s_yhi, s_ylo = sem("y_hi_done"), sem("y_lo_done")
        s_mg_in, s_gt_in, s_gate = sem("merged_loaded"), sem("gate_loaded"), sem("gate_done")
        s_mg, s_mhi = sem("merged_done"), sem("m_hi_done")
        s_mlo = [sem("m_lo_even"), sem("m_lo_odd")]
        s_wf, s_ftr, s_orow = sem("w_final_loaded"), sem("final_transposed"), sem("row_done")
        s_out = [sem("out_written0"), sem("out_written1")]
        pe_phase, act_phase, dve_phase, pool_phase = (sem(n) for n in (
            "pe_phase", "act_phase", "dve_phase", "pool_phase"))
        sp_turn, dve_turn = sem("sp_turn"), sem("dve_turn")
        c_act_sem, c_dve_sem, c_pool_sem = sem("act_chain"), sem("dve_chain"), sem("pool_chain")
        block = ctx.enter_context(nc.Block())

        def gu_cols(w, col):
            return w[0].rearrange("(k p) m -> p k m", p=P)[:, :, bass.ds(col, P)]

        ffn_w = ((ffn1_w_gu, ffn1_w_down), (ffn2_w_gu, ffn2_w_down))

        @block.sync
        def _(sp):
            def load(n, j, src, kt):
                at_least(sp, w_lo_done, n - 1)
                sp.sem_inc(sp_turn, 1)
                sp.dma_start(w_raw[:, j, 0:kt, :], src).then_inc(w_loaded[j], 16)

            def load_ada(chunk, dst, which):
                src = w_ada[0].rearrange("(k p) m -> p k m", p=P)[:, :, bass.ds(chunk * ADA_W, ADA_W)]
                sp.dma_start(dst, src).then_inc(s_ada[which], 16)

            def ffn_loads(x, after_first=None):
                w_gu, w_dn = ffn_w[x]
                for p, (f0, cnt) in enumerate(PARTS):
                    n0 = W[f"gu{x}{p}"]

                    def pair(i, n0=n0, f0=f0):
                        load(n0 + i * 2, 0, gu_cols(w_gu, (i + f0) * P), 8)
                        load(n0 + 1 + i * 2, 1, gu_cols(w_gu, (i + f0) * P + FF), 8)
                        if x == 0 and p < 2:
                            q = i + f0
                            sp.wait_ge(s_ada_red, q + ADA_FIRST)
                            if isinstance(i, int) and q == 0:
                                sp.wait_ge(s_xr, 8)
                            load_ada(q + ADA_FIRST, ada[:], 2)
                    if p == 0:
                        pair(0)
                        with sp.Fori(1, cnt) as i:
                            pair(i)
                    else:
                        with sp.Fori(0, cnt) as i:
                            pair(i)
                    n1 = W[f"dn{x}{p}"]
                    rows = w_dn[0][f0 * P:(f0 + cnt) * P, :].rearrange("(k p) m -> p k m", p=P)
                    with sp.Fori(0, 4) as i:
                        for j in range(2):
                            load(n1 + i * 2 + j, j, rows[:, :, bass.ds((i * 2 + j) * P, P)], cnt)

            sp.dma_start(kst[:, 0:K_PERSIST], table[:, 0:K_PERSIST]).then_inc(s_table, 16)
            sp.dma_start(par1[0:72, 0, :], b_ada.rearrange("o (r p) -> (o r) p", p=P)).then_inc(s_rows, 16)
            for r0, v in ((R_N1, norm1_w), (R_N2, norm2_w), (R_N3, norm3_w), (R_SN, ssd_norm_w), (R_C, c)):
                rows = v.shape[1] // P
                sp.dma_start(par1[r0:r0 + rows, 0, :], v.rearrange("o (r p) -> (o r) p", p=P)).then_inc(s_rows, 16)
            sp.dma_start(par1[:, 1, :], conv_w[0].rearrange("j (r p) -> (j r) p", p=P)).then_inc(s_rows, 16)
            sp.dma_start(par1[0:32, 2, :], conv_b.rearrange("o (r p) -> (o r) p", p=P)).then_inc(s_rows, 16)
            load_ada(0, ada_a[:], 0)
            load_ada(1, ada_b[:], 1)
            x_rows = x[0].rearrange("(h q p) d -> h p q d", h=2, p=P)
            sp.dma_start(x_nat[:], x_rows[0]).then_inc(s_xin, 16)
            sp.wait_ge(s_xtr, 8)
            sp.dma_start(x_nat[:], x_rows[1]).then_inc(s_xin, 16)
            sp.wait_ge(s_ada_red, 1)
            load_ada(2, ada_a[:], 0)
            sp.wait_ge(s_ada_red, 2)
            load_ada(3, ada_b[:], 1)
            sp.dma_start(d_row, d_skip.to_broadcast([P, SH])).then_inc(s_small, 16)
            with nc.allow_non_contiguous_dma(reason="32 heads' scalars, one per partition"):
                sp.dma_start(head_col[:, 0:1], dt_bias.rearrange("o h -> h o")).then_inc(s_small, 16)
                sp.dma_start(head_col[:, 1:2], a_log.rearrange("o h -> h o")).then_inc(s_small, 16)
            ffn_loads(0)

            win = w_in[0].rearrange("(k p) m -> p k m", p=P)
            load(W["dt"], 0, win[:, 0:4, O_DT:O_DT + P], 4)
            load(W["dt"] + 1, 1, win[:, 4:8, O_DT:O_DT + P], 4)
            sp.wait_ge(freed[0], O[0]["dt"])
            sp.wait_ge(freed[1], O[1]["dt"])
            sp.dma_start(x_keep, xT[:]).then_inc(s_xkeep, 16)
            na = W["att"]
            with sp.Fori(0, PAIRS) as i:
                load(na + i * 4, 0, win[:, :, bass.ds(i * P + O_Q, P)], 8)
                load(na + i * 4 + 1, 1, win[:, :, bass.ds(i * P + O_K, P)], 8)
                load(na + i * 4 + 2, 0, win[:, 0:4, bass.ds(i * P + O_V, P)], 4)
                load(na + i * 4 + 3, 1, win[:, 4:8, bass.ds(i * P + O_V, P)], 4)
            with sp.Fori(0, 2) as i:
                for j in range(2):
                    load(W["gba"] + i * 2 + j, j, win[:, :, bass.ds((i * 2 + j) * P + O_G1, P)], 8)
            wao = w_att_out[0].rearrange("(k p) m -> p k m", p=P)
            with sp.Fori(0, 8) as i:
                load(W["ga"] + i * 2, 0, win[:, :, bass.ds(i * P + O_G0, P)], 8)
                load(W["ga"] + 1 + i * 2, 1, wao[:, :, bass.ds(i * P, P)], 6)

            def ssd_x(n, g):
                load(n, 0, win[:, :, bass.ds(g * 2 * P + O_X, P)], 8)
                load(n + 1, 1, win[:, :, bass.ds(g * 2 * P + O_X + P, P)], 8)
                load(n + 2, 0, win[:, :, bass.ds(g * P + O_B, P)], 8)
                load(n + 3, 1, win[:, :, bass.ds(g * P + O_C, P)], 8)

            def ssd_z(n, g):
                load(n, 0, win[:, :, bass.ds(g * 2 * P + O_Z, P)], 8)
                load(n + 1, 1, win[:, :, bass.ds(g * 2 * P + O_Z + P, P)], 8)

            ssd_x(W["ssdx"], 0)
            with sp.Fori(0, NG - 1) as g:
                ssd_x(W["ssd"] + g * 6, g + 1)
                ssd_z(W["ssd"] + g * 6 + 4, g)
            for j in range(4):
                load(W["ssd"] + (NG - 1) * 6 + j, j % 2, win[:, :, O_G1 + (4 + j) * P:O_G1 + (5 + j) * P], 8)
            ssd_z(W["ssd"] + (NG - 1) * 6 + 4, NG - 1)
            wso = w_ssd_out[0].rearrange("(k p) m -> p k m", p=P)
            load(W["yo"], 0, wso[:, 0:8, 0:P], 8)
            load(W["yo"] + 1, 1, wso[:, 8:16, 0:P], 8)
            past(sp, s_conv, 4 * NG)
            past(sp, s_conv_act, 4 * NG)
            for g in range(NG):
                if g == 0:
                    past(sp, s_yout, 16 * (NG - 1))
                    past(sp, s_ysq, 2 * (NG - 1))
                elif g == Y_EARLY:
                    for e in (pe_phase, act_phase, dve_phase, pool_phase):
                        sp.wait_ge(e, 2)
                    past(sp, s_yout, 16 * NG)
                sp.dma_start(y_raw[:, 2 * g:2 * g + 2, :], y_keep[g]).then_inc(s_yin[g], 16)
            sp.wait_ge(s_mg_out, 16 * 8)
            sp.wait_ge(s_ms, 3)
            sp.dma_start(merged[:], merged_keep.rearrange("d p t -> p d t")).then_inc(s_mg_in, 16)
            for s in s_gt_out:
                sp.wait_ge(s, 16 * 4)
            sp.dma_start(gate[:], gate_keep[0]).then_inc(s_gt_in, 16)
            with sp.Fori(1, 8) as i:
                for j in range(2):
                    load(W["yo"] + i * 2 + j, j, wso[:, 8 * j:8 * j + 8, bass.ds(i * P, P)], 8)
                sp.wait_ge(s_mg, i)
                sp.dma_start(gate[:], gate_keep[bass.ds(i, 1)].rearrange("o p t -> (o p) t")).then_inc(s_gt_in, 16)
            wmo = w_mix_out[0].rearrange("(k p) m -> p k m", p=P)
            load(W["mix"], 0, wmo[:, :, 0:P], 8)
            load(W["mix"] + 1, 1, wmo[:, :, P:2 * P], 8)
            sp.wait_ge(w_used, W["mix"])
            sp.wait_ge(s_xkeep, 16)
            sp.dma_start(xT[:], x_keep).then_inc(s_xback, 16)
            with sp.Fori(1, 4) as i:
                for j in range(2):
                    load(W["mix"] + i * 2 + j, j, wmo[:, :, bass.ds((i * 2 + j) * P, P)], 8)
            ffn_loads(1)
            sp.wait_ge(w_used, BLOCKS)
            sp.dma_start(w_final[:], final_norm_w.rearrange("(o d) -> o d", o=1).to_broadcast([P, D])).then_inc(s_wf, 16)
            for t in range(NT):
                sp.wait_ge(s_orow, 2 * (t + 1))
                sp.dma_start(out[0, t * P:(t + 1) * P, :], o_row[:, t % 2, :]).then_inc(s_out[t % 2], 16)
            for s in s_out:
                sp.wait_ge(s, 16 * NT // 2)

        @block.tensor
        def _(pe):
            mm = nc.tensor.matmul
            for s in (s_qk, s_tr, s_pv, s_otr, s_rot, s_vtr, s_tokT, s_cb, s_y, s_st):
                pe.sem_inc(s, CREDIT)

            def passes(out_, j, k, rh, rl, first, last):
                mm(out_, w_lo[:, j, k, :], rh, start=first, stop=False)
                mm(out_, w_hi[:, j, k, :], rl, start=False, stop=False)
                return mm(out_, w_hi[:, j, k, :], rh, start=False, stop=last)

            def product(n, j, b, m, hi, lo, kt, k_off=0, first=True, last=True, ready=None):
                pe.wait_ge(w_lo_done, n + 1)
                if first:
                    at_least(pe, freed[b], m)
                for k in range(kt):
                    if ready is not None:
                        ready(k)
                    for t in range(2):
                        cols = slice(512 * t, 512 * t + 512)
                        ins = passes(psG[:, b, t, :], j, k, hi[:, k_off + k, cols], lo[:, k_off + k, cols],
                                     first and k == 0, last and k == kt - 1)
                ins.then_inc(w_used, 1)

            def transpose(out_, in_, rows=P):
                return nc.tensor.transpose(out_, in_, ident[0:rows, 0:rows])

            def ada_sum(q):
                src, dst = ada_red, psO[:, 0:4]
                pe.wait_ge(s_ada_red, q + 1)
                at_least(pe, s_ada_done, q)
                for j in range(4):
                    ins = mm(dst[:, j:j + 1], src[:, j * P:(j + 1) * P], ones[:, 0:1], start=True, stop=True)
                ins.then_inc(s_ada_mm, 1)

            def h_ready(idx):
                def wait(k):
                    pe.wait_ge(s_hlo[k % 2], 4 * idx + k // 2 + 1)
                return wait

            def token_sums(src):
                for t in range(NT):
                    ins = mm(psT[:, t:t + 1], src[:, t * P:(t + 1) * P], ones[:, 0:1], start=True, stop=True)
                ins.then_inc(s_ms, 1)

            def spread(count, diag):
                pe.wait_ge(s_diag, count)
                for t in range(2):
                    ins = mm(psS[:, t, :], ones, diag[:, 512 * t:512 * t + 512], start=True, stop=True)
                ins.then_inc(s_spread, 1)

            def norm_sum(idx, count):
                pe.wait_ge(s_acc, 8 * (idx + 1))
                token_sums(acc)
                spread(count, rstd)

            def ffn(x, idx):
                for p, (f0, cnt) in enumerate(PARTS):
                    s = f"gu{x}{p}"
                    n0, a0, a1 = W[s], O[0][s], O[1][s]

                    def pair(i, ready=None):
                        if x == 0 and p < 2:
                            ada_sum_step(i, f0)
                        product(n0 + i * 2, 0, 0, a0 + i, h_hi, h_lo, 8, ready=ready)
                        product(n0 + 1 + i * 2, 1, 1, a1 + i, h_hi, h_lo, 8)

                    def ada_sum_step(i, f0):
                        if isinstance(i, int) and i + f0 == 0:
                            return
                        ada_sum(i + (f0 + ADA_FIRST - 1))

                    if p == 0:
                        pair(0, ready=h_ready(idx))
                        with pe.Fori(1, cnt) as i:
                            pair(i)
                    else:
                        with pe.Fori(0, cnt) as i:
                            pair(i)
                    if x == 0 and p == 1:
                        ada_sum(ADA_ALL - 1)
                    s = f"dn{x}{p}"
                    n0, a0, a1 = W[s], O[0][s], O[1][s]

                    def hidden(k, F=FT * x + f0, cnt=cnt):
                        if k in (0, cnt - 2, cnt - 1):
                            pe.wait_ge(s_hid_lo, F + max(k + 1, cnt - 2))
                    for j in range(2):
                        product(n0 + j, j, j, (a0, a1)[j], hid_hi, hid_lo, cnt, ready=hidden if j == 0 else None)
                    with pe.Fori(1, 4) as i:
                        for j in range(2):
                            product(n0 + i * 2 + j, j, j, (a0, a1)[j] + i, hid_hi, hid_lo, cnt)

            pe.wait_ge(s_table, 16)
            pe.wait_ge(s_rows, 16 * 8)
            transpose(psT[:, 0:R_P1], par1[0:R_P1, 0, :], R_P1)
            transpose(psT[:, R_CW:R_CW + P], par1[:, 1, :])
            transpose(psT[:, R_CB:R_CB + 32], par1[0:32, 2, :], 32).then_inc(s_par_ps, 1)
            for t in range(NT):
                pe.wait_ge(s_xin, 16 * (t // 4 + 1))
                for u in range(2):
                    i = 2 * t + u
                    at_least(pe, s_xt, i - 1)
                    for j in range(4):
                        ins = transpose(psS[:, u, j * P:(j + 1) * P], x_nat[:, t % 4, (4 * u + j) * P:(4 * u + j + 1) * P])
                    ins.then_inc(s_xtr, 1)
            for q in range(ADA_FIRST):
                ada_sum(q)
            pe.wait_ge(s_xt, 2 * NT)
            pe.wait_ge(s_par, 1)
            norm_sum(0, 1)
            ffn(0, 0)

            norm_sum(1, 2)
            product(W["dt"], 0, 0, O[0]["dt"], h_hi, h_lo, 4, 0, True, False, ready=h_ready(1))
            n = W["dt"] + 1
            pe.wait_ge(w_lo_done, n + 1)
            for k in range(4):
                h_ready(1)(4 + k)
                for t in range(2):
                    cols = slice(512 * t, 512 * t + 512)
                    ins = passes(psG[:, 0, t, :], 1, k, h_hi[:, 4 + k, cols], h_lo[:, 4 + k, cols], False, k == 3)
            ins.then_inc(w_used, 1)

            def att_half(i, j, k, t):
                n = W["att"] + i * 4 + j
                b = (0, 1, 0, 0)[j]
                m = (O[0]["att"] + i * 3, O[1]["att"] + i * 3, O[0]["att"] + i * 3 + 2, 0)[j]
                kk = k - 4 if j == 3 else k
                if kk == 0 and t == 0:
                    pe.wait_ge(w_lo_done, n + 1)
                    if j < 3:
                        pe.wait_ge(freed[b], m)
                cols = slice(512 * t, 512 * t + 512)
                ins = passes(psG[:, b, t, :], j % 2, kk, h_hi[:, k, cols], h_lo[:, k, cols], k == 0, k == 7)
                if t == 1 and kk == (3 if j > 1 else 7):
                    ins.then_inc(w_used, 1)

            def att_rot(i, b):
                m = O[b]["att"] + i * 3 + 1
                pe.wait_ge(freed[b], m)
                src = (q_st, k_st)[b]
                for t in range(2):
                    ins = mm(psG[:, b, t, :], rotm, src[:, 512 * t:512 * t + 512], start=True, stop=True)
                ins.then_inc(s_rot, 1)

            def att_vtr(i):
                pe.wait_ge(freed[1], O[1]["att"] + i * 3 + 2)
                pe.wait_ge(freed[0], O[0]["att"] + i * 3 + 3)
                for t in range(NT):
                    ins = transpose(psG[:, 1, t // 4, (t % 4) * P:(t % 4 + 1) * P], v_st[:, t * P:(t + 1) * P])
                ins.then_inc(s_vtr, 1)

            def gate_half(j, k, t):
                b = j % 2
                if k == 0 and t == 0:
                    pe.wait_ge(w_lo_done, W["gba"] + j + 1)
                    pe.wait_ge(freed[b], O[b]["gba"] + j // 2)
                cols = slice(512 * t, 512 * t + 512)
                ins = passes(psG[:, b, t, :], b, k, h_hi[:, k, cols], h_lo[:, k, cols], k == 0, k == 7)
                if t == 1 and k == 7:
                    ins.then_inc(w_used, 1)

            def att_event(i, e):
                if e[0] == "half":
                    att_half(i, *e[1:])
                elif e[0] == "rot":
                    att_rot(i, e[1])
                else:
                    gate_half(*e[1:])

            def att_iter(i, par_, att, gemm):
                S = i * NA
                TR = i * AGROUP0[NA]
                for s in range(NA + 3):
                    evs = step_events(s, gemm)
                    slots = [evs[0:1], evs[1:2], evs[2:3], evs[3:]]
                    r = s - 1
                    if att and 0 <= r < NA:
                        q, h = ASTEPS[r]
                        past(pe, s_exp, S + r + 1)
                        past(pe, s_pta, S + r)
                        past(pe, s_ptb, i * AGB0[NA] + AGB0[r])
                        for j in range(min(q + 1, 4)):
                            ins = transpose(psT[:, j * P:(j + 1) * P], prob[:, r % 2, j * P:(j + 1) * P])
                        ins.then_inc(s_tr, 1)
                    for e in slots[0]:
                        att_event(i + 1, e)
                    if att and s < NA:
                        q, h = ASTEPS[s]
                        rows = slice(HD * h, HD * h + HD)
                        if s == 0:
                            past(pe, s_roped, i * 2 + 2)
                        past(pe, s_masked, S + s)
                        past(pe, s_olo, i * NT + max(0, (s - 3) // 2))
                        width = (q + 1) * P
                        for t in range((width + 511) // 512):
                            c0, c1 = 512 * t, min(width, 512 * t + 512)
                            ins = mm(psS[:, t, 0:c1 - c0], qT[rows, par_, q * P:(q + 1) * P],
                                     kT[rows, par_, c0:c1], start=True, stop=True)
                        ins.then_inc(s_qk, 1)
                    if att and s == 1:
                        att_vtr(i)
                    for e in slots[1]:
                        att_event(i + 1, e)
                    if att and 0 <= r < NA and ASTEPS[r][0] >= 4:
                        q, h = ASTEPS[r]
                        past(pe, s_pta, S + r + 1)
                        for j in range(4, q + 1):
                            ins = transpose(psT[:, (j - 4) * P:(j - 3) * P], prob[:, r % 2, j * P:(j + 1) * P])
                        ins.then_inc(s_tr, 1)
                    for e in slots[2]:
                        att_event(i + 1, e)
                    r = s - 2
                    if att and 0 <= r < NA:
                        q, h = ASTEPS[r]
                        if r == 0:
                            past(pe, s_vtok, i + 1)
                        past(pe, s_pta, S + r + 1)
                        if q >= 4:
                            past(pe, s_ptb, i * AGB0[NA] + AGB0[r + 1])
                        past(pe, s_o, S + r)
                        for j in range(q + 1):
                            ins = mm(psO[:, 0:HD], probT[:, r % 2, j * P:(j + 1) * P],
                                     v_tok[:, par_, j, HD * h:HD * h + HD], start=(j == 0), stop=(j == q))
                        ins.then_inc(s_pv, 1)
                    for e in slots[3]:
                        att_event(i + 1, e)
                    r = s - 3
                    if att and 0 <= r < NA and r % 2 == 1:
                        q = ASTEPS[r][0]
                        past(pe, s_o, S + r + 1)
                        past(pe, s_masked, S + min(s + 1, NA))
                        transpose(psS[:, 0, 0:P], o_tok[:, q % 2, :]).then_inc(s_otr, 1)

            att_iter(-1, 0, False, True)
            pe.wait_ge(s_dt_cs, 1)
            pe.wait_ge(s_dt_ready, 1)
            for u, src in enumerate((csT, dtT, dteT)):
                for t in range(NT):
                    dst = psS[:, u // 2, (u % 2) * 256 + t * SH:(u % 2) * 256 + (t + 1) * SH]
                    ins = transpose(dst, src[0:SH, t * P:(t + 1) * P], SH)
            ins.then_inc(s_dt_tr, 1)
            pe.wait_ge(s_dt_tok, 1)
            with pe.Fori(0, PAIRS // 2 - 1) as i2:
                att_iter(i2 * 2, 0, True, True)
                att_iter(i2 * 2 + 1, 1, True, True)
            att_iter(PAIRS - 2, 0, True, True)
            att_iter(PAIRS - 1, 1, True, False)

            past(pe, s_olo, PAIRS * NT)
            with pe.Fori(0, 8) as i:
                product(W["ga"] + i * 2, 0, 0, O[0]["ga"] + i, h_hi, h_lo, 8)
                product(W["ga"] + 1 + i * 2, 1, 1, O[1]["ga"] + i, o_hi, o_lo, 6)
            for j in range(4):
                product(W["ssdx"] + j, j % 2, j % 2, O[j % 2]["ssdx"] + j // 2, h_hi, h_lo, 8)

            def ssd_front(i, p, c):
                n = i * NT + c
                tok = slice(c * P, (c + 1) * P)
                if c == 0:
                    past(pe, s_conv_act, i * 4 + 4)
                past(pe, s_xdte, n)
                past(pe, s_btok, n)
                for j in range(3):
                    ins = transpose(psT[:, j * P:(j + 1) * P], xbc[:, p, j, tok])
                ins.then_inc(s_tokT, 1)
                past(pe, s_wT, n)
                mm(psS[:, 0, 0:P], xbc[:, p, 2, tok], xbc[:, p, 3, tok], start=True, stop=True).then_inc(s_cb, 1)

            def ssd_back(i, p, c):
                n = i * NT + c
                past(pe, s_wT, n + 1)
                past(pe, s_xdte, n + 1)
                past(pe, s_cscaled, n + 1)
                past(pe, s_yev, n)
                if c > 0:
                    past(pe, s_state, i * (NT - 1) + c)
                for e in range(GH):
                    dst = psS[HD * (e % 2):HD * (e % 2) + HD, 1, (e // 2) * P:(e // 2 + 1) * P]
                    cols = slice(e * HD, (e + 1) * HD)
                    ins = mm(dst, xdt[:, c % 2, cols], wT[:, c % 2, e, :], start=True, stop=(c == 0))
                    if c > 0:
                        ins = mm(dst, state[:, (c - 1) % 2, cols], c_scaled[:, c % 2, e, :], start=False, stop=True)
                ins.then_inc(s_y, 1)
                if c < NT - 1:
                    past(pe, s_btok, n + 1)
                    past(pe, s_state, i * (NT - 1) + c)
                    mm(psO[:, 0:2 * P], b_tok[:, c % 2, :], xdte[:, c % 2, :], start=True, stop=True).then_inc(s_st, 1)

            def ssd_iter(i, p, gemm):
                n0 = W["ssd"] + i * 6
                halves = [(j, k) for j in range(6) for k in range(8)]
                per = len(halves) // NT

                def slice_(part):
                    for j, k in part:
                        n = n0 + j
                        b = j % 2
                        if k == 0:
                            pe.wait_ge(w_lo_done, n + 1)
                            pe.wait_ge(freed[b], O[b]["ssd"] + i * 3 + j // 2)
                        for t in range(2):
                            cols = slice(512 * t, 512 * t + 512)
                            ins = passes(psG[:, b, t, :], b, k, h_hi[:, k, cols], h_lo[:, k, cols], k == 0, k == 7)
                        if k == 7:
                            ins.then_inc(w_used, 1)

                for c in range(NT):
                    if gemm or c < NT - 1:
                        ssd_front(*following(i, p, c))
                    ssd_back(i, p, c)
                    slice_(halves[per * c:per * (c + 1)])

            pe.wait_ge(s_dec, 16)
            ssd_front(0, 0, 0)
            with pe.Fori(0, NG // 2 - 1) as i2:
                ssd_iter(i2 * 2, 0, True)
                ssd_iter(i2 * 2 + 1, 1, True)
            ssd_iter(NG - 2, 0, True)
            ssd_iter(NG - 1, 1, False)
            nc.tensor.drain().then_inc(pe_phase, 2)

            pe.wait_ge(freed[0], O[0]["yo"])
            for j in range(2):
                pe.wait_ge(w_lo_done, W["yo"] + j + 1)
                for k in range(8):
                    pe.wait_ge(s_ylo, 8 * j + k + 1)
                    for t in range(2):
                        cols = slice(512 * t, 512 * t + 512)
                        ins = passes(psG[:, 0, t, :], j, k, y_hi[:, 8 * j + k, cols], y_lo[:, 8 * j + k, cols],
                                     j == 0 and k == 0, j == 1 and k == 7)
                ins.then_inc(w_used, 1)
                if j == 0:
                    past(pe, s_yacc, NG * 2 + 1)
                    token_sums(y_acc)
            spread(3, y_rstd)

            def y_out(n, b, m):
                product(n, 0, b, m, y_hi, y_lo, 8, 0, True, False)
                product(n + 1, 1, b, m, y_hi, y_lo, 8, 8, False, True)

            y_out(W["yo"] + 2, 1, O[1]["yo"])
            with pe.Fori(1, 4) as i:
                y_out(W["yo"] + i * 4, 0, O[0]["yo"] + i)
                y_out(W["yo"] + 2 + i * 4, 1, O[1]["yo"] + i)

            def merged_ready(k):
                pe.wait_ge(s_mlo[k % 2], k // 2 + 1)
            for j in range(2):
                product(W["mix"] + j, j, j, O[j]["mix"], m_hi, m_lo, 8, ready=merged_ready if j == 0 else None)
            with pe.Fori(1, 4) as i:
                for j in range(2):
                    product(W["mix"] + i * 2 + j, j, j, O[j]["mix"] + i, m_hi, m_lo, 8)
            norm_sum(2, 4)
            ffn(1, 2)

            pe.wait_ge(s_acc, 8 * 4)
            token_sums(acc)
            for t in range(NT):
                for u in range(2):
                    i = 2 * t + u
                    at_least(pe, s_orow, i - 1)
                    for j in range(4):
                        ins = transpose(psS[:, u, j * P:(j + 1) * P], xT[:, 4 * u + j, t * P:(t + 1) * P])
                    ins.then_inc(s_ftr, 1)

        @block.scalar
        def _(act):
            ch = Chain(act, c_act_sem)
            for s in (s_exp, s_pta, s_ohi, s_conv_act, s_dec_exp, s_ecs, s_btok, s_ysq, s_yout):
                act.sem_inc(s, CREDIT)
            fn = nc.scalar.activation

            def split_at(base, i, rate, j):
                n = i * rate + base
                assert base % 2 == j and rate % 2 == 0
                act.wait_ge(w_loaded[j], i * (8 * rate) + 16 * (base // 2 + 1))
                at_least(act, w_used, n - 1)
                fn(w_hi[:, j], w_raw[:, j], ACT.Copy).then_inc(w_hi_done, 1)

            def norm_apply(idx, scale, shift, h_free):
                for d in range(8):
                    act.wait_ge(s_xr, 8 * idx + d + 1)
                    if d == 0 and h_free:
                        act.wait_ge(w_used, h_free)
                    shift_d = mod[:, shift + d:shift + d + 1]
                    if d % 2 == 0:
                        fn(h_hi[:, d], tmp[:, 0], ACT.Identity, bias=shift_d).then_inc(s_hhi, 1)
                    else:
                        ch.link(fn(tmp[:, 1], tmp[:, 1], ACT.Identity, bias=shift_d))
                        fn(h_hi[:, d], tmp[:, 1], ACT.Copy).then_inc(s_hhi, 1)

            def root(n, width):
                act.wait_ge(s_ms, n)
                fn(rcol[:], psT[:, 0:NT], ACT.Sqrt, scale=1.0 / width, bias=eps_col).then_inc(s_rt, 1)

            def square(count, src, j, xt_sem, xt_value):
                act.wait_ge(xt_sem, xt_value)
                at_least(act, s_acc, count - 1)
                fn(sq[:, j], src, ACT.Square).then_inc(s_sq, 1)

            def ffn(x, idx):
                for p, (f0, cnt) in enumerate(PARTS):
                    s = f"gu{x}{p}"
                    n0 = W[s]
                    F0 = FT * x + f0
                    U0 = O[1][s]
                    free_at = W[s] if p else (0 if x == 0 else None)

                    def body(i):
                        split_at(n0 + 2, i, 2, 0)
                        act.wait_ge(w_used, i * 2 + n0 + 1)
                        at_least(act, freed[1], i + U0)
                        fn(tmp[:, 0], psG[:, 0].rearrange("p a b -> p (a b)"), ACT.Silu).then_inc(freed[0], 1)
                        split_at(n0 + 3, i, 2, 1)
                        act.wait_ge(freed[1], i + U0 + 1)
                        if p:
                            act.wait_ge(w_used, n0)
                        fn(hid_hi[:, bass.ds(i, 1), :].rearrange("p o t -> p (o t)"), tmp[:, 1], ACT.Copy).then_inc(s_hid_hi, 1)
                    if p == 0:
                        body(0)
                        with ch.loop(1, cnt, 0) as i:
                            body(i)
                    else:
                        with ch.loop(0, cnt, 0) as i:
                            body(i)
                    s = f"dn{x}{p}"
                    n1 = W[s]

                    def down(i, tail=False):
                        for j in range(2):
                            if not tail:
                                split_at(n1 + 2 + j, i, 2, j)
                            if p == 3:
                                d = i * 2 + j
                                src = xT[:, bass.ds(d, 1), :].rearrange("p o t -> p (o t)")
                                square(d + 8 * (idx + 1), src, j, freed[j], O[j][s] + i + 1)
                    last = x == 1 and p == 3
                    with ch.loop(0, 3 if last else 4, 0) as i:
                        down(i)
                    if last:
                        down(3, True)

            act.wait_ge(s_par, 1)
            fn(c_act, par[:, R_C:R_C + 8], ACT.Silu).then_inc(s_cact, 1)
            for t in range(NT):
                for u in range(2):
                    act.wait_ge(s_xtr, 2 * t + u + 1)
                    fn(xT[:, 4 * u:4 * u + 4, t * P:(t + 1) * P], psS[:, u].rearrange("p (j t) -> p j t", j=4),
                       ACT.Copy).then_inc(s_xt, 1)
            for d in range(8):
                square(d, xT[:, d], d % 2, s_xt, 2 * NT)
            split_at(0, 0, 2, 0)
            split_at(1, 0, 2, 1)
            act.wait_ge(s_eps, 1)
            root(1, D)
            act.wait_ge(s_first_cols, 1)
            norm_apply(0, scale1, SH1, 0)
            ffn(0, 0)
            root(2, D)
            act.wait_ge(s_first_cols, 2)
            norm_apply(1, scale2, SH2, W["dn03"])

            split_at(W["dt"] + 2, 0, 2, 0)
            split_at(W["dt"] + 3, 0, 2, 1)
            act.wait_ge(s_dt_e, 1)
            ch.link(fn(dt_w[2][0:SH], dt_w[1][0:SH], ACT.Exp, scale=-1.0))
            ch.link(fn(head_col[:, 2:3], head_col[:, 1:2], ACT.Exp))
            fn(dt_w[3][0:SH], dt_w[2][0:SH], ACT.Ln, bias=1.0).then_inc(s_dt_ln, 1)
            act.wait_ge(s_dt_cs, 1)
            for t in range(NT):
                ins = fn(dteT[0:SH, t * P:(t + 1) * P], csT[0:SH, t * P:(t + 1) * P], ACT.Exp, scale=-1.0,
                         bias=csT[0:SH, (t + 1) * P - 1:(t + 1) * P])
            ins.then_inc(s_dt_dte, 1)
            ch.link(fn(dec_head, csT[0:SH, P - 1:T:P], ACT.Exp))
            act.dma_start(cs_keep, csT[0:SH]).then_inc(s_cs_kept, 16)
            act.dma_start(dec_keep, dec_head).then_inc(s_dec_kept, 16)
            act.wait_ge(s_dec_kept, 16)
            act.dma_start(dec_b[:], dec_keep.rearrange("h t -> (h t)")[None, :].to_broadcast([P, SH * NT])
                          .rearrange("p (h t) -> p h t", t=NT)).then_inc(s_dec, 16)
            act.wait_ge(s_ang, 1)
            fn(sinT[:], rt2[:], ACT.Sin).then_inc(s_trig, 1)
            act.wait_ge(s_ang, 2)
            fn(cosT[:], rt2[:], ACT.Sin).then_inc(s_trig, 1)

            def keep_gate(d, dst):
                b = d % 2
                at_least(act, s_gt_out[b], 16 * (d // 2))
                fn(dst, psG[:, b].rearrange("p a b -> p (a b)"), ACT.Copy).then_inc(freed[b], 1)
                m = O[b]["gba"] + d // 2 if d < 4 else O[b]["ssd"] + (NG - 1) * 3 + (d - 4) // 2
                act.wait_ge(freed[b], m + 1)
                act.dma_start(gate_keep[d], dst).then_inc(s_gt_out[b], 16)

            def att_done(i, e):
                if e[0] == "gate" and e[2:] == (7, 1):
                    j = e[1]
                    act.wait_ge(w_used, W["gba"] + j + 1)
                    if j == 0:
                        past(act, s_vtok, PAIRS)
                    keep_gate(j, (q_st, k_st)[j % 2][:])
                    split_at(W["gba"] + 2 + j, 0, 2, j % 2)
                if e[0] != "half" or e[3] == 0:
                    return
                j, k = e[1], e[2]
                if k != (7, 7, 3, 7)[j]:
                    return
                n = W["att"] + j
                act.wait_ge(w_used, i * 4 + n + 1)
                if j == 0:
                    past(act, s_vtok, i)
                    fn(q_st[:], psG[:, 0].rearrange("p a b -> p (a b)"), ACT.Copy, scale=-(HD ** -0.5)).then_inc(freed[0], 1)
                if j == 1:
                    past(act, s_roped, i * 2)
                    fn(k_st[:], psG[:, 1].rearrange("p a b -> p (a b)"), ACT.Copy).then_inc(freed[1], 1)
                if j == 3:
                    past(act, s_roped, i * 2 + 1)
                    fn(v_st[:], psG[:, 0].rearrange("p a b -> p (a b)"), ACT.Copy).then_inc(freed[0], 1)
                split_at(n + 2, i, 4, j % 2)

            def att_iter(i, par_, att, gemm):
                S = i * NA
                for s in range(NA + 3):
                    r = s - 1
                    if att and 0 <= r < NA:
                        q, h = ASTEPS[r]
                        past(act, s_tr, i * AGROUP0[NA] + AGROUP0[r] + 1)
                        past(act, s_pv, S + r - 1)
                        w = min(q + 1, 4) * P
                        fn(probT[:, r % 2, 0:w], psT[:, 0:w], ACT.Copy).then_inc(s_pta, 1)
                    if att and s < NA:
                        q, h = ASTEPS[s]
                        past(act, s_masked, S + s + 1)
                        past(act, s_o, S + s - 3)
                        fn(prob[:, s % 2, 0:(q + 1) * P], prob[:, s % 2, 0:(q + 1) * P], ACT.Exp, scale=-1.0,
                           bias=negmax[:, s % 2:s % 2 + 1], accum_out=den[:, s % 4:s % 4 + 1]).then_inc(s_exp, 1)
                    for e in step_events(s, gemm):
                        att_done(i + 1, e)
                    r = s - 3
                    if att and 0 <= r < NA and r % 2 == 1:
                        q = ASTEPS[r][0]
                        past(act, s_otr, i * NT + q + 1)
                        dst = o_hi[:, bass.ds(i, 1), q * P:(q + 1) * P].rearrange("p o t -> p (o t)")
                        fn(dst, psS[:, 0, 0:P], ACT.Copy).then_inc(s_ohi, 1)

            act.wait_ge(s_cs_kept, 16)
            att_iter(-1, 0, False, True)
            with ch.loop(0, PAIRS // 2 - 1, 0) as i2:
                att_iter(i2 * 2, 0, True, True)
                att_iter(i2 * 2 + 1, 1, True, True)
            att_iter(PAIRS - 2, 0, True, True)
            att_iter(PAIRS - 1, 1, True, False)
            nc.scalar.drain().then_inc(act_phase, 1)

            with ch.loop(0, 8, 0) as i:
                split_at(W["ga"] + 2, i, 2, 0)
                act.wait_ge(w_used, i * 2 + W["ga"] + 1)
                act.wait_ge(freed[1], i + O[1]["ga"])
                fn(tmp[:, 0], psG[:, 0].rearrange("p a b -> p (a b)"), ACT.Sigmoid).then_inc(freed[0], 1)
                split_at(W["ga"] + 3, i, 2, 1)
                act.wait_ge(freed[1], i + O[1]["ga"] + 1)
                act.dma_start(merged_keep[bass.ds(i, 1)].rearrange("o p t -> (o p) t"), tmp[:, 1]).then_inc(s_mg_out, 16)
            act.wait_ge(s_mg_out, 16 * 8)

            def load_cs(g, c):
                src = cs_keep.rearrange("(g e) (c l) -> g c e l", e=GH, l=P)[bass.ds(g, 1), c]
                act.dma_start(cs_b[:, c], src.to_broadcast([P, GH, P])).then_inc(s_csb[c], 16)

            def conv_out(base, i, rate, j, C):
                n = i * rate + base
                act.wait_ge(w_used, n + 1)
                past(act, s_conv, C - 1)
                fn(conv_in[:, j % 2, 4:4 + T], psG[:, j % 2].rearrange("p a b -> p (a b)"), ACT.Copy).then_inc(freed[j % 2], 1)

            def conv_act(i, p, j):
                past(act, s_conv, i * 4 + j + 1)
                t = conv_tile(i, j)
                ins = fn(xbc[:, p, j], xbc[:, p, j], ACT.Silu, bias=par[:, bass.ds(t + R_CB, 1)])
                ins.then_inc(s_conv_act, 1)

            def conv_tile(i, j):
                return (i * 2 + j) if j < 2 else i + (16 if j == 2 else 24)

            act.wait_ge(dve_phase, 1)
            act.wait_ge(pool_phase, 1)
            for c in range(NT):
                load_cs(0, c)
            for j in range(4):
                split_at(W["ssdx"] + 2 + j, 0, 2, j % 2)
                conv_out(W["ssdx"] + j, 0, 2, j, j)
                if j:
                    conv_act(0, 0, j - 1)
            conv_act(0, 0, 3)

            def ssd_prepare(i, p, c, refill=True):
                n = i * NT + c
                past(act, s_tokT, n + 1)
                past(act, s_st, i * (NT - 1) + max(c - 1, 0))
                fn(b_tok[:, c % 2], psT[:, 2 * P:3 * P], ACT.Copy).then_inc(s_btok, 1)
                act.wait_ge(s_csb[c], i * 16 + 16)
                past(act, s_cscaled, n - 1)
                fn(ecs[:, c % 2], cs_b[:, c], ACT.Exp).then_inc(s_ecs, 1)
                past(act, s_arg, n + 1)
                fn(decay[:, c % 2], decay[:, c % 2], ACT.Exp).then_inc(s_dec_exp, 1)
                if refill:
                    past(act, s_ecs, n + 1)
                    load_cs(i + 1, c)

            def ssd_iter(i, p, gemm, second_last=False):
                n0 = W["ssd"]

                def done(j):
                    base = n0 + j
                    split_at(base + 2, i, 6, j % 2)
                    act.wait_ge(w_used, i * 6 + base + 1)
                    if j < 4 and not gemm:
                        keep_gate(4 + j, tmp[:, j % 2])
                        return
                    if j == 0:
                        past(act, s_yout, i * 16)
                    if j < 4:
                        conv_out(base, i, 6, j, i * 4 + 4 + j)
                        if j:
                            conv_act(i + 1, 1 - p, j - 1)
                    else:
                        if j == 4 and gemm:
                            conv_act(i + 1, 1 - p, 3)
                        past(act, s_gated, i * 2 + j - 5)
                        fn(z_sil[:, j - 4], psG[:, j % 2].rearrange("p a b -> p (a b)"), ACT.Silu).then_inc(freed[j % 2], 1)

                for c in range(NT):
                    if gemm or c < NT - 1:
                        ssd_prepare(*following(i, p, c), refill=gemm and not (second_last and c == NT - 1))
                    for j in range(6):
                        if (8 * j + 7) // 6 == c:
                            done(j)
                for j in range(2):
                    past(act, s_gated, i * 2 + j + 1)
                    past(act, s_yacc, i * 2 + j + 1)
                    fn(y_sq[:], xbc[:, p, j], ACT.Square).then_inc(s_ysq, 1)
                act.dma_start(y_keep[bass.ds(i, 1)].rearrange("o p u t -> (o p) u t"), xbc[:, p, 0:2]).then_inc(s_yout, 16)

            ssd_prepare(0, 0, 0)
            with ch.loop(0, NG // 2 - 1, 0) as i2:
                ssd_iter(i2 * 2, 0, True)
                ssd_iter(i2 * 2 + 1, 1, True)
            ssd_iter(NG - 2, 0, True, second_last=True)
            ssd_iter(NG - 1, 1, False)
            nc.scalar.drain().then_inc(act_phase, 1)

            act.wait_ge(w_used, W["yo"])
            for k in range(16):
                act.wait_ge(s_yin[k // 2], 16)
                fn(y_hi[:, k], y_raw[:, k], ACT.Copy, scale=par[:, R_SN + k:R_SN + k + 1]).then_inc(s_yhi, 1)
            root(3, INNER)
            with ch.loop(0, 8, 0) as i:
                split_at(W["yo"] + 2, i, 2, 0)
                act.wait_ge(s_gt_in, i * 16 + 16)
                fn(gate[:], gate[:], ACT.Sigmoid).then_inc(s_gate, 1)
                split_at(W["yo"] + 3, i, 2, 1)
            for d in range(8):
                act.wait_ge(s_mg, d + 1)
                if d == 0:
                    act.wait_ge(w_used, W["mix"])
                fn(m_hi[:, d], merged[:, d], ACT.Copy).then_inc(s_mhi, 1)
            with ch.loop(0, 4, 0) as i:
                for j in range(2):
                    split_at(W["mix"] + 2 + j, i, 2, j)
                    d = i * 2 + j
                    src = xT[:, bass.ds(d, 1), :].rearrange("p o t -> p (o t)")
                    square(d + 16, src, j, freed[j], O[j]["mix"] + i + 1)
            root(4, D)
            norm_apply(2, scale3, SH3, W["gu10"])
            ffn(1, 2)
            root(5, D)

        @block.vector
        def _(dve):
            ch = Chain(dve, c_dve_sem)
            for s in (s_masked, s_ptb, s_o, s_olo, s_roped, s_vtok, s_conv, s_arg, s_xdte, s_wT, s_state, s_yev, s_gated):
                dve.sem_inc(s, CREDIT)
            v = nc.vector

            def flat(ps):
                return ps.rearrange("p a b -> p (a b)")

            def ada_reduce(q, src):
                dve.wait_ge(s_ada_mul, q + 1)
                at_least(dve, s_ada_mm, q)
                v.tensor_reduce(ada_red[:], src.rearrange("p k m -> p m k"), AXX, ALU.add).then_inc(s_ada_red, 1)

            def ada_finish(q):
                dve.wait_ge(s_ada_mm, q + 1)
                if isinstance(q, int):
                    cols = slice(4 * q, 4 * q + 4)
                else:
                    cols = bass.ds(q * 4, 4)
                v.tensor_tensor(mod[:, cols], psO[:, 0:4], par[:, cols], ALU.add).then_inc(s_ada_done, 1)

            def diagonal(n, dst):
                dve.wait_ge(s_rt, n)
                ch.link(v.reciprocal(rcol[:], rcol[:]))
                v.tensor_tensor(dst.rearrange("p (t c) -> p t c", t=NT), ident.unsqueeze(1).to_broadcast([P, NT, P]),
                                rcol[:].unsqueeze(2).to_broadcast([P, NT, P]), ALU.mult).then_inc(s_diag, 1)
                dve.wait_ge(s_spread, n)

            def norm_apply(idx, n, scale, shift):
                diagonal(n, rstd[:])

                def lo(d):
                    dve.wait_ge(s_hhi, 8 * idx + d + 1)
                    v.scalar_tensor_tensor(h_lo[:, d], tmp[:, 0], mod[:, shift + d:shift + d + 1],
                                           h_hi[:, d].bitcast(F32), ALU.add, ALU.subtract).then_inc(s_hlo[0], 1)
                for d in range(8):
                    if d % 2:
                        at_least(dve, s_hlo[1], 4 * idx + d // 2)
                    elif d:
                        lo(d - 2)
                        dve.wait_ge(s_hlo[0], 4 * idx + d // 2)
                    v.scalar_tensor_tensor(tmp[:, d % 2], xT[:, d], scale[:, d:d + 1], flat(psS[:]),
                                           ALU.mult, ALU.mult).then_inc(s_xr, 1)
                lo(6)

            def ffn(x):
                for p, (f0, cnt) in enumerate(PARTS):
                    s = f"gu{x}{p}"
                    n0, G0, U0, F0 = W[s], O[0][s], O[1][s], FT * x + f0

                    def body(i):
                        if x == 0 and p < 2:
                            if not (isinstance(i, int) and i + f0 == 0):
                                ada_finish(i + (f0 + ADA_FIRST - 1))
                            ada_reduce(i + (f0 + ADA_FIRST), ada[:])
                        dve.wait_ge(freed[0], i + G0 + 1)
                        dve.wait_ge(w_used, i * 2 + n0 + 2)
                        at_least(dve, s_hid_lo, i + F0)
                        v.tensor_tensor(tmp[:, 1], tmp[:, 0], flat(psG[:, 1]), ALU.mult).then_inc(freed[1], 1)
                    if p == 0:
                        body(0)
                        with ch.loop(1, cnt, 0) as i:
                            body(i)
                    else:
                        with ch.loop(0, cnt, 0) as i:
                            body(i)
                    if x == 0 and p == 0:
                        dve.wait_ge(s_ada_done, G1 // 4 + 2)
                        v.tensor_scalar(gate1, mod[:, G1:G1 + 8], 0.5, None, ALU.mult).then_inc(s_g1, 1)
                        dve.wait_ge(s_g1, 1)
                    if x == 0 and p == 1:
                        ada_finish(ADA_ALL - 1)
                        dve.wait_ge(s_ada_done, ADA_ALL)
                        ch.link(v.tensor_scalar(gate3, mod[:, G3:G3 + 8], 0.5, None, ALU.mult))
                        ch.link(v.scalar_tensor_tensor(scale3, mod[:, SC3:SC3 + 8], 1.0, par[:, R_N3:R_N3 + 8], ALU.add, ALU.mult))
                        v.scalar_tensor_tensor(scale2, mod[:, SC2:SC2 + 8], 1.0, par[:, R_N2:R_N2 + 8],
                                               ALU.add, ALU.mult).then_inc(s_first_cols, 1)
                    s = f"dn{x}{p}"
                    n1 = W[s]
                    g = gate1 if x == 0 else gate3
                    with ch.loop(0, 4, 0) as i:
                        for j in range(2):
                            d = i * 2 + j
                            dve.wait_ge(w_used, d + n1 + 1)
                            xd = xT[:, bass.ds(d, 1), :].rearrange("p o t -> p (o t)")
                            v.scalar_tensor_tensor(xd, flat(psG[:, j]), g[:, bass.ds(d, 1)], xd,
                                                   ALU.mult, ALU.add).then_inc(freed[j], 1)

            v.memset(eps_col, EPS).then_inc(s_eps, 1)
            dve.wait_ge(s_par_ps, 1)
            v.tensor_copy(par[:], psT[:, 0:R_ALL]).then_inc(s_par, 1)
            for q in range(ADA_FIRST):
                ada_reduce(q, (ada_a, ada_b)[q % 2][:])
                ada_finish(q)
            dve.wait_ge(s_ada_done, ADA_FIRST)
            v.scalar_tensor_tensor(scale1, mod[:, SC1:SC1 + 8], 1.0, par[:, R_N1:R_N1 + 8],
                                   ALU.add, ALU.mult).then_inc(s_first_cols, 1)
            norm_apply(0, 1, scale1, SH1)
            ffn(0)
            norm_apply(1, 2, scale2, SH2)

            dve.wait_ge(s_small, 16 * 3)
            for j in range(2):
                rows = slice(HD * j, HD * j + HD)
                ch.link(v.tensor_copy(d_col[rows], d_row[rows].rearrange("p (a b) -> p b a", b=2)[:, j]))
            dve.wait_ge(w_used, W["dt"] + 2)
            ch.link(v.tensor_scalar(dt_w[0][0:SH], flat(psG[0:SH, 0]), head_col[:, 0:1], None, ALU.add))
            dve.sem_inc(freed[0], 1)
            v.scalar_tensor_tensor(dt_w[1][0:SH], dt_w[0][0:SH], -1.0, dt_w[0][0:SH], ALU.mult, ALU.max).then_inc(s_dt_e, 1)
            dve.wait_ge(s_dt_ln, 1)
            ch.link(v.scalar_tensor_tensor(dtT[0:SH], dt_w[0][0:SH], 0.0, dt_w[3][0:SH], ALU.max, ALU.add))
            ch.link(v.tensor_scalar(dt_w[1][0:SH], dtT[0:SH], head_col[:, 2:3], -1.0, ALU.mult, ALU.mult))
            ch.link(v.memset(dt_w[2][0:SH], 1.0))
            for t in range(NT):
                tok = slice(t * P, (t + 1) * P)
                ins = v.tensor_tensor_scan(csT[0:SH, tok], dt_w[2][0:SH, tok], dt_w[1][0:SH, tok], 0.0, ALU.mult, ALU.add)
            ins.then_inc(s_dt_cs, 1)
            dve.wait_ge(s_dt_dte, 1)
            v.tensor_tensor(dteT[0:SH], dteT[0:SH], dtT[0:SH], ALU.mult).then_inc(s_dt_ready, 1)

            dve.wait_ge(s_pos, 16)
            two_pi = 2.0 * np.pi
            c1 = 6.28125
            c2 = float(np.float32(np.round((two_pi - c1) * 2 ** 19) / 2 ** 19))
            c3 = float(np.float32(two_pi - c1 - c2))
            magic = 1.5 * 2 ** 23
            ch.link(v.tensor_copy(rt1[:], pos_i[:]))
            ch.link(v.tensor_scalar(ang[:], rt1[:], invf, None, ALU.mult))
            for u, (turn, shift) in enumerate(((0.0, 0.0), (0.25, float(np.pi / 2)))):
                ch.link(v.tensor_scalar(rt1[:], ang[:], float(1 / two_pi), turn, ALU.mult, ALU.add))
                ch.link(v.tensor_scalar(rt1[:], rt1[:], magic, None, ALU.add))
                ch.link(v.tensor_scalar(rt1[:], rt1[:], magic, None, ALU.subtract))
                if u:
                    dve.wait_ge(s_trig, 1)
                ch.link(v.scalar_tensor_tensor(rt2[:], rt1[:], -c1, ang[:], ALU.mult, ALU.add))
                ch.link(v.scalar_tensor_tensor(rt2[:], rt1[:], -c2, rt2[:], ALU.mult, ALU.add))
                ch.link(v.scalar_tensor_tensor(rt2[:], rt1[:], -c3, rt2[:], ALU.mult, ALU.add))
                ch.link(v.tensor_scalar(rt2[:], rt2[:], shift, None, ALU.add))
                v.tensor_scalar(rt2[:], rt2[:], 3.1415925, -3.1415925, ALU.min, ALU.max).then_inc(s_ang, 1)

            def v_out(i, par_):
                past(dve, s_vtr, i + 1)
                v.tensor_copy(v_tok[:, par_].rearrange("p a b -> p (a b)"), flat(psG[:, 1])).then_inc(s_vtok, 1)
                past(dve, s_vtok, i + 1)
                dve.sem_inc(freed[1], 1)

            def att_done(i, par_, e):
                if e[0] != "rot":
                    return
                b = e[1]
                src, dst = (q_st, k_st)[b], (qT, kT)[b]
                past(dve, s_rot, i * 2 + b + 1)
                ch.link(v.tensor_tensor(dst[:, par_], src[:], cosT[:], ALU.mult))
                v.tensor_tensor(src[:], flat(psG[:, b]), sinT[:], ALU.mult).then_inc(freed[b], 1)
                dve.wait_ge(freed[b], i * 3 + O[b]["att"] + 2)
                v.tensor_tensor(dst[:, par_], dst[:, par_], src[:], ALU.add).then_inc(s_roped, 1)
                past(dve, s_roped, i * 2 + b + 1)

            def att_iter(i, par_, att, gemm):
                S = i * NA
                for s in range(NA + 3):
                    if att and s < NA:
                        q, h = ASTEPS[s]
                        w = (q + 1) * P
                        past(dve, s_qk, S + s + 1)
                        past(dve, s_tr, i * AGROUP0[NA] + (AGROUP0[s - 1] if s else -AGROUPS[NA - 1]))
                        dve.sem_inc(dve_turn, 1)
                        v.tensor_tensor_reduce(out=prob[:, s % 2, 0:w], in0=flat(psS)[:, 0:w], in1=mask[:, T - w:T],
                                               scale=1.0, scalar=3.0e38, op0=ALU.add, op1=ALU.min,
                                               accum_out=negmax[:, s % 2:s % 2 + 1]).then_inc(s_masked, 1)
                    if att and s == 1:
                        v_out(i, par_)
                    r = s - 1
                    if att and 0 <= r < NA and ASTEPS[r][0] >= 4:
                        q, h = ASTEPS[r]
                        past(dve, s_tr, i * AGROUP0[NA] + AGROUP0[r] + 2)
                        past(dve, s_pv, S + r - 1)
                        v.tensor_copy(probT[:, r % 2, 512:(q + 1) * P], psT[:, 0:(q - 3) * P]).then_inc(s_ptb, 1)
                    r = s - 2
                    if att and 0 <= r < NA:
                        q, h = ASTEPS[r]
                        ch.link(v.reciprocal(rden[:, r % 2:r % 2 + 1], den[:, r % 4:r % 4 + 1]))
                        past(dve, s_pv, S + r + 1)
                        if h == 0:
                            past(dve, s_otr, i * NT + q - 1)
                        v.tensor_scalar(o_tok[:, q % 2, HD * h:HD * h + HD], psO[:, 0:HD],
                                        rden[:, r % 2:r % 2 + 1], None, ALU.mult).then_inc(s_o, 1)
                    r = s - 3
                    if att and 0 <= r < NA and r % 2 == 1:
                        q = ASTEPS[r][0]
                        past(dve, s_ohi, i * NT + q + 1)
                        tok = slice(q * P, (q + 1) * P)
                        hi = o_hi[:, bass.ds(i, 1), tok].rearrange("p o t -> p (o t)").bitcast(F32)
                        lo = o_lo[:, bass.ds(i, 1), tok].rearrange("p o t -> p (o t)")
                        v.tensor_tensor(lo, psS[:, 0, 0:P], hi, ALU.subtract).then_inc(s_olo, 1)
                    for e in step_events(s, gemm):
                        att_done(i + 1, 1 - par_, e)

            dve.wait_ge(s_trig, 2)
            att_iter(-1, 1, False, True)
            dve.wait_ge(s_dt_tr, 1)
            dve.wait_ge(s_mask, 16)
            ch.link(v.tensor_copy(cs_tok[:].rearrange("p a b -> p (a b)"), psS[:, 0, 0:256]))
            ch.link(v.tensor_copy(dt_keep[:], psS[:, 0, 256:512]))
            v.tensor_copy(dte_tok[:].rearrange("p a b -> p (a b)"), psS[:, 1, 0:256]).then_inc(s_dt_tok, 1)
            dve.wait_ge(s_dt_tok, 1)
            with ch.loop(0, PAIRS // 2 - 1, 2 * NA + 4) as i2:
                att_iter(i2 * 2, 0, True, True)
                att_iter(i2 * 2 + 1, 1, True, True)
            att_iter(PAIRS - 2, 0, True, True)
            att_iter(PAIRS - 1, 1, True, False)
            past(dve, s_olo, PAIRS * NT)
            nc.vector.drain().then_inc(dve_phase, 1)

            def ga(i, first):
                dve.wait_ge(freed[0], i + O[0]["ga"] + 1)
                dve.wait_ge(w_used, i * 2 + W["ga"] + 2)
                if not first:
                    dve.wait_ge(s_mg_out, i * 16)
                v.tensor_tensor(tmp[:, 1], tmp[:, 0], flat(psG[:, 1]), ALU.mult).then_inc(freed[1], 1)
            dve.wait_ge(act_phase, 1)
            ga(0, True)
            with ch.loop(1, 8, 0) as i:
                ga(i, False)

            def conv(i, p, j, n):
                C = i * 4 + j
                dve.wait_ge(freed[j % 2], n)
                t = (i * 2 + j) if j < 2 else i + (16 if j == 2 else 24)
                for u in range(4):
                    tap = par[:, bass.ds(t + (R_CW + 32 * (3 - u)), 1)]
                    src = conv_in[:, j % 2, 4 - u:4 - u + T]
                    if u == 0:
                        ch.link(v.tensor_scalar(xbc[:, p, j], src, tap, None, ALU.mult))
                    else:
                        ins = v.scalar_tensor_tensor(xbc[:, p, j], src, tap, xbc[:, p, j], ALU.mult, ALU.add)
                        if u < 3:
                            ch.link(ins)
                ins.then_inc(s_conv, 1)

            dve.wait_ge(w_used, W["ssdx"])
            dve.wait_ge(s_dec, 16)
            for j in range(2):
                dve.wait_ge(s_gt_out[j], 16 * 2)
            ch.link(v.tensor_copy(dt_tok[:].rearrange("p a b -> p (a b)"), dt_keep[:]))
            for j in range(2):
                ch.link(v.memset(conv_in[:, j, 0:4], 0.0))
            for j in range(4):
                conv(0, 0, j, O[j % 2]["ssdx"] + j // 2 + 1)

            def ssd_arg(i, p, c):
                n = i * NT + c
                dve.wait_ge(s_csb[c], i * 16 + 16)
                past(dve, s_wT, n - 1)
                for e in range(GH):
                    ins = v.scalar_tensor_tensor(decay[:, c % 2, e], cs_b[:, c, e], cs_tok[:, c, bass.ds(i * GH + e, 1)],
                                                 causal, ALU.subtract, ALU.add)
                ins.then_inc(s_arg, 1)

            def ssd_weigh(i, p, c):
                n = i * NT + c
                heads = bass.ds(i * GH, GH)
                past(dve, s_tokT, n + 1)
                past(dve, s_btok, n + 1)
                past(dve, s_y, n - 1)
                past(dve, s_st, i * (NT - 1) + max(c - 1, 0))
                xt = psT[:, 0:2 * P].rearrange("p (e d) -> p e d", e=GH)
                v.tensor_tensor(xdt[:, c % 2].rearrange("p (e d) -> p e d", e=GH), xt,
                                dt_tok[:, c, heads].unsqueeze(2).to_broadcast([P, GH, HD]), ALU.mult)
                v.tensor_tensor(xdte[:, c % 2].rearrange("p (e d) -> p e d", e=GH), xt,
                                dte_tok[:, c, heads].unsqueeze(2).to_broadcast([P, GH, HD]), ALU.mult).then_inc(s_xdte, 1)
                past(dve, s_dec_exp, n + 1)
                past(dve, s_cb, n + 1)
                v.tensor_tensor(wT[:, c % 2], decay[:, c % 2],
                                psS[:, 0, 0:P].unsqueeze(1).to_broadcast([P, GH, P]), ALU.mult).then_inc(s_wT, 1)

            def ssd_iter(i, p, gemm):
                blocks = range(4) if gemm else ()
                for c in range(NT):
                    n = i * NT + c
                    heads = bass.ds(i * GH, GH)
                    more = gemm or c < NT - 1
                    if more:
                        ssd_arg(*following(i, p, c))
                    past(dve, s_y, n + 1)
                    for j in range(2):
                        tok = slice(c * P, (c + 1) * P)
                        ins = v.scalar_tensor_tensor(xbc[:, p, j, tok], xbc[:, p, j, tok], d_col[:, bass.ds(i * 2 + j, 1)],
                                                     psS[:, 1, j * P:(j + 1) * P], ALU.mult, ALU.add)
                    ins.then_inc(s_yev, 1)
                    if c < NT - 1:
                        past(dve, s_st, i * (NT - 1) + c + 1)
                        if c == 0:
                            v.tensor_copy(state[:, 0], psO[:, 0:2 * P]).then_inc(s_state, 1)
                        else:
                            dcol = dec_b[:, heads, c:c + 1].to_broadcast([P, GH, HD])
                            cur = state[:, c % 2].rearrange("p (e d) -> p e d", e=GH)
                            old = state[:, (c - 1) % 2].rearrange("p (e d) -> p e d", e=GH)
                            ch.link(v.tensor_tensor(cur, old, dcol, ALU.mult))
                            v.tensor_tensor(state[:, c % 2], state[:, c % 2], psO[:, 0:2 * P], ALU.add).then_inc(s_state, 1)
                        past(dve, s_state, i * (NT - 1) + c + 1)
                    if more:
                        ssd_weigh(*following(i, p, c))
                    for j in blocks:
                        if (8 * j + 7) // 6 == c:
                            conv(i + 1, 1 - p, j, i * 3 + O[j % 2]["ssd"] + j // 2 + 1)
                past(dve, s_yev, i * NT + NT)
                for j in range(2):
                    dve.wait_ge(freed[j], i * 3 + O[j]["ssd"] + 3)
                    v.tensor_tensor(xbc[:, p, j], xbc[:, p, j], z_sil[:, j], ALU.mult).then_inc(s_gated, 1)

            ssd_arg(0, 0, 0)
            ssd_weigh(0, 0, 0)
            with ch.loop(0, NG // 2 - 1, 2 * (6 + 12)) as i2:
                ssd_iter(i2 * 2, 0, True)
                ssd_iter(i2 * 2 + 1, 1, True)
            ssd_iter(NG - 2, 0, True)
            ssd_iter(NG - 1, 1, False)
            nc.vector.drain().then_inc(dve_phase, 1)
            for k in range(16):
                dve.wait_ge(s_yhi, k + 1)
                v.scalar_tensor_tensor(y_lo[:, k], y_raw[:, k], par[:, R_SN + k:R_SN + k + 1], y_hi[:, k].bitcast(F32),
                                       ALU.mult, ALU.subtract).then_inc(s_ylo, 1)
            diagonal(3, y_rstd[:])
            ch.link(v.tensor_copy(y_rstd[:], flat(psS[:])))
            dve.wait_ge(s_mg_in, 16)
            with ch.loop(0, 4, 2) as i:
                for j in range(2):
                    d = i * 2 + j
                    md = merged[:, bass.ds(d, 1), :].rearrange("p o t -> p (o t)")
                    dve.wait_ge(w_used, i * 4 + (W["yo"] + 2 * j + 2))
                    v.tensor_tensor(tmp[:, j], flat(psG[:, j]), y_rstd[:], ALU.mult).then_inc(freed[j], 1)
                    dve.wait_ge(freed[j], i + O[j]["yo"] + 1)
                    dve.wait_ge(s_gate, d + 1)
                    ch.link(v.tensor_tensor(tmp[:, j], tmp[:, j], gate[:], ALU.mult))
                    v.tensor_tensor(md, md, tmp[:, j], ALU.add).then_inc(s_mg, 1)
            for d in range(0, 8, 2):
                dve.wait_ge(s_mhi, d + 1)
                v.tensor_tensor(m_lo[:, d], merged[:, d], m_hi[:, d].bitcast(F32), ALU.subtract).then_inc(s_mlo[0], 1)
            dve.wait_ge(s_xback, 16)
            with ch.loop(0, 4, 0) as i:
                for j in range(2):
                    d = i * 2 + j
                    dve.wait_ge(w_used, d + W["mix"] + 1)
                    xd = xT[:, bass.ds(d, 1), :].rearrange("p o t -> p (o t)")
                    v.scalar_tensor_tensor(xd, flat(psG[:, j]), mod[:, bass.ds(d + G2, 1)], xd,
                                           ALU.mult, ALU.add).then_inc(freed[j], 1)
            norm_apply(2, 4, scale3, SH3)
            ffn(1)
            dve.wait_ge(s_rt, 5)
            ch.link(v.reciprocal(rcol[:], rcol[:]))
            dve.wait_ge(s_wf, 16)
            for t in range(NT):
                for u in range(2):
                    dve.wait_ge(s_ftr, 2 * t + u + 1)
                    if t >= 2 and u == 0:
                        dve.wait_ge(s_out[t % 2], 16 * (t // 2))
                    cols = slice(512 * u, 512 * u + 512)
                    v.scalar_tensor_tensor(o_row[:, t % 2, cols], psS[:, u, :], rcol[:, t:t + 1],
                                           w_final[:, cols], ALU.mult, ALU.mult).then_inc(s_orow, 1)

        @block.gpsimd
        def _(pool):
            ch = Chain(pool, c_pool_sem)
            for s in (s_cscaled, s_yacc):
                pool.sem_inc(s, CREDIT)
            g = nc.gpsimd

            def split(n, j):
                pool.wait_ge(w_hi_done, n + 1)
                g.tensor_tensor(w_lo[:, j], w_raw[:, j], w_hi[:, j].bitcast(F32), ALU.subtract).then_inc(w_lo_done, 1)

            def ada_mul(q, buf, loaded, value):
                pool.wait_ge(loaded, value)
                g.tensor_tensor(buf, buf, c_act.unsqueeze(2).to_broadcast([P, 8, ADA_W]), ALU.mult).then_inc(s_ada_mul, 1)

            def norm_apply(idx):
                for d in range(1, 8, 2):
                    pool.wait_ge(s_hhi, 8 * idx + d + 1)
                    g.tensor_tensor(h_lo[:, d], tmp[:, 1], h_hi[:, d].bitcast(F32), ALU.subtract).then_inc(s_hlo[1], 1)

            def add_square(count, j, first):
                pool.wait_ge(s_sq, count + 1)
                if first:
                    g.tensor_copy(acc[:], sq[:, j]).then_inc(s_acc, 1)
                else:
                    pool.wait_ge(s_acc, count)
                    g.tensor_tensor(acc[:], acc[:], sq[:, j], ALU.add).then_inc(s_acc, 1)

            def ffn(x, idx):
                for p, (f0, cnt) in enumerate(PARTS):
                    s = f"gu{x}{p}"
                    n0, F0 = W[s], FT * x + f0

                    def body(i):
                        if x == 0 and p < 2:
                            ada_mul(i + f0 + ADA_FIRST, ada[:], s_ada[2], i * 16 + (16 * f0 + 16))
                        split(i * 2 + (n0 + 2), 0)
                        split(n0 + 3 + i * 2, 1)
                        pool.wait_ge(s_hid_hi, i + F0 + 1)
                        at = hid_hi[:, bass.ds(i, 1), :].rearrange("p o t -> p (o t)").bitcast(F32)
                        to = hid_lo[:, bass.ds(i, 1), :].rearrange("p o t -> p (o t)")
                        g.tensor_tensor(to, tmp[:, 1], at, ALU.subtract).then_inc(s_hid_lo, 1)
                    if p == 0:
                        body(0)
                        with ch.loop(1, cnt, 0) as i:
                            body(i)
                    else:
                        with ch.loop(0, cnt, 0) as i:
                            body(i)
                    s = f"dn{x}{p}"
                    n1 = W[s]

                    def down(i, tail=False):
                        for j in range(2):
                            if not tail:
                                split(n1 + 2 + j + i * 2, j)
                            if p == 3:
                                add_square(i * 2 + j + 8 * (idx + 1), j, isinstance(i, int) and i == 0 and j == 0)
                    last = x == 1 and p == 3
                    down(0)
                    with ch.loop(1, 3 if last else 4, 0) as i:
                        down(i)
                    if last:
                        down(3, True)

            pool.wait_ge(s_cact, 1)
            for q in range(ADA_FIRST):
                ada_mul(q, (ada_a, ada_b)[q % 2][:], s_ada[q % 2], 16 * (q // 2 + 1))
            for d in range(8):
                add_square(d, d % 2, d == 0)
            split(0, 0)
            split(1, 1)
            norm_apply(0)
            ffn(0, 0)
            norm_apply(1)
            pool.wait_ge(s_xkeep, 16)
            g.dma_start(pos_i[:], positions.to_broadcast([P, T])).then_inc(s_pos, 16)
            g.dma_start(mask[:], table[:, K_MASK:K_MASK + T]).then_inc(s_mask, 16)
            split(W["dt"] + 2, 0)
            split(W["dt"] + 3, 1)
            with ch.loop(0, PAIRS, 0) as i:
                for j in range(4):
                    split(W["att"] + 2 + j + i * 4, j % 2)
            for j in range(4):
                split(W["gba"] + 2 + j, j % 2)
            nc.gpsimd.drain().then_inc(pool_phase, 1)
            with ch.loop(0, 8, 0) as i:
                for j in range(2):
                    split(W["ga"] + 2 + j + i * 2, j)
            g.memset(y_acc[:], 0.0).then_inc(s_yacc, 1)
            past(pool, s_yacc, 1)
            for j in range(4):
                split(W["ssdx"] + 2 + j, j % 2)

            def scale_c(i, p, c):
                n = i * NT + c
                if c == 0:
                    past(pool, s_conv_act, i * 4 + 4)
                past(pool, s_ecs, n + 1)
                past(pool, s_y, n - 1)
                g.tensor_tensor(c_scaled[:, c % 2], ecs[:, c % 2],
                                xbc[:, p, 3, c * P:(c + 1) * P].unsqueeze(1).to_broadcast([P, GH, P]),
                                ALU.mult).then_inc(s_cscaled, 1)

            def ssd_iter(i, p, gemm):
                for c in range(NT):
                    if gemm or c < NT - 1:
                        scale_c(*following(i, p, c))
                    for j in range(6):
                        if (8 * j + 7) // 6 == c:
                            split(W["ssd"] + 2 + j + i * 6, j % 2)
                for j in range(2):
                    past(pool, s_ysq, i * 2 + j + 1)
                    past(pool, s_yacc, i * 2 + j + 1)
                    g.tensor_tensor(y_acc[:], y_acc[:], y_sq[:], ALU.add).then_inc(s_yacc, 1)

            scale_c(0, 0, 0)
            with ch.loop(0, NG // 2 - 1, 0) as i2:
                ssd_iter(i2 * 2, 0, True)
                ssd_iter(i2 * 2 + 1, 1, True)
            ssd_iter(NG - 2, 0, True)
            ssd_iter(NG - 1, 1, False)
            nc.gpsimd.drain().then_inc(pool_phase, 1)
            with ch.loop(0, 8, 0) as i:
                for j in range(2):
                    split(W["yo"] + 2 + j + i * 2, j)
            for d in range(1, 8, 2):
                pool.wait_ge(s_mhi, d + 1)
                g.tensor_tensor(m_lo[:, d], merged[:, d], m_hi[:, d].bitcast(F32), ALU.subtract).then_inc(s_mlo[1], 1)

            def mix(i):
                for j in range(2):
                    split(W["mix"] + 2 + j + i * 2, j)
                    add_square(i * 2 + j + 16, j, isinstance(i, int) and i == 0 and j == 0)
            mix(0)
            with ch.loop(1, 4, 0) as i:
                mix(i)
            norm_apply(2)
            ffn(1, 2)


_INS = ["x", "c", "positions", "w_ada", "b_ada", "norm1_w", "ffn1_w_gu", "ffn1_w_down", "norm2_w", "w_in",
        "conv_w", "conv_b", "dt_bias", "a_log", "d_skip", "ssd_norm_w", "w_att_out", "w_ssd_out", "w_mix_out",
        "norm3_w", "ffn2_w_gu", "ffn2_w_down", "final_norm_w"]


def kernel(**inputs):
    import numpy as _np
    import concourse.bacc as _bacc
    from concourse import mybir as _mybir
    from concourse.bass_utils import run_bass_kernel_spmd as _run

    nc = _bacc.Bacc("TRN2", target_bir_lowering=False, num_devices=1)
    arrays, args = {}, []
    for name in _INS:
        a = _np.ascontiguousarray(inputs[name])
        arrays[f"in_{name}"] = a
        args.append(nc.dram_tensor(f"in_{name}", a.shape, _mybir.dt.from_np(a.dtype), kind="ExternalInput").ap())
    arrays["in_table"] = constants()
    args.append(nc.dram_tensor("in_table", arrays["in_table"].shape, F32, kind="ExternalInput").ap())
    shape = tuple(inputs["x"].shape)
    args.append(nc.dram_tensor("out_0", shape, F32, kind="ExternalOutput").ap())
    kernel_program(nc, *args)
    r = _run(nc, [arrays], core_ids=[0])
    return r.results[0]["out_0"]
```

```python
from contextlib import ExitStack, contextmanager

import numpy as np
import concourse.bass as bass
from concourse import mybir

F32 = mybir.dt.float32
F32R = mybir.dt.float32r
I32 = mybir.dt.int32
ALU = mybir.AluOpType
ACT = mybir.ActivationFunctionType
AXX = mybir.AxisListType.X

P = 128
D = 1024
T = 1024
DT_ = D // P
NT = T // P
FF = 2816
FT = FF // P
AH, HD = 12, 64
PAIRS = AH // 2
NG, GH = 8, 4
SH = NG * GH
INNER = 2 * D
AW = AH * HD
ROPE, THETA = HD // 4, 500000.0
O_Q, O_K, O_V = 0, AW, 2 * AW
O_Z = 3 * AW
O_X = O_Z + INNER
O_B = O_X + INNER
O_C = O_B + NG * P
O_DT = O_C + NG * P
O_G0 = O_DT + SH
O_G1 = O_G0 + D
EPS = 1e-6
NEG = -1e30
PATTERNS = ((128, 1), (512, 4), (2048, 16))

PARTS = ((0, 7), (7, 7), (14, 4), (18, 4))
ADA_W = 512
ADA_FIRST = 2 * D // ADA_W
ADA_ALL = 9 * D // ADA_W
assert PARTS[0][1] + PARTS[1][1] == ADA_ALL - ADA_FIRST

K_ID, K_ONE, K_NEG, K_ROT, K_INVF = 0, P, 2 * P, 3 * P, 4 * P
K_PERSIST = 4 * P + 1
K_MASK = K_PERSIST
K_ALL = K_MASK + T

R_ADA, R_N1, R_N2, R_N3, R_SN, R_C, R_FN = 0, 72, 80, 88, 96, 112, 120
R_P1 = 128
R_CW = R_P1
R_CB = R_CW + 4 * 32
R_ALL = R_CB + 32


def constants():
    k = np.zeros((P, K_ALL), np.float32)
    k[:, K_ID:K_ID + P] = np.eye(P)
    k[:, K_ONE:K_ONE + P] = 1.0
    s, l = np.arange(P)[:, None], np.arange(P)[None, :]
    k[:, K_NEG:K_NEG + P] = np.where(s <= l, 0.0, NEG)
    half = ROPE // 2
    for h in (0, HD):
        for m in range(half):
            k[h + m + half, K_ROT + h + m] = -1.0
            k[h + m, K_ROT + h + m + half] = 1.0
        inv = np.float32(THETA) ** (-np.arange(0, ROPE, 2, dtype=np.float32) / np.float32(ROPE))
        k[h:h + half, K_INVF] = inv
        k[h + half:h + ROPE, K_INVF] = inv
    dist = np.arange(P)[:, None] - np.arange(T)[None, :] + (T - P)
    n = sum(((dist >= 0) & (dist <= w) & (dist % r == 0)).astype(int) for w, r in PATTERNS)
    k[:, K_MASK:] = np.where(n > 0, -np.log(np.maximum(n, 1)), -NEG)
    return k


class Chain:

    def __init__(self, eng, sem):
        self.eng, self.sem, self.base, self.term, self.count = eng, sem, 0, None, 0

    def value(self):
        v = self.base + self.count
        return v if self.term is None else self.term + v

    def link(self, instruction):
        self.count += 1
        instruction.then_inc(self.sem, 1)
        self.eng.wait_ge(self.sem, self.value())

    @contextmanager
    def loop(self, start, end, rate):
        base = self.base + self.count
        with self.eng.Fori(start, end) as i:
            self.base, self.count, self.term = base - start * rate, 0, i * rate if rate else None
            yield i
            assert self.count == rate, (self.count, rate)
        self.base, self.count, self.term = base + (end - start) * rate, 0, None


def at_least(eng, sem, value):
    if not (isinstance(value, int) and value <= 0):
        eng.wait_ge(sem, value)


CREDIT = 64


def past(eng, sem, value):
    eng.wait_ge(sem, value + CREDIT)


def plan():
    w, o0, o1 = {}, {}, {}
    n, m0, m1 = 0, 0, 0

    def section(name, blocks, outs0, outs1):
        nonlocal n, m0, m1
        w[name], o0[name], o1[name] = n, m0, m1
        n, m0, m1 = n + blocks, m0 + outs0, m1 + outs1

    def ffn(x):
        for p, (_, cnt) in enumerate(PARTS):
            section(f"gu{x}{p}", 2 * cnt, cnt, cnt)
            section(f"dn{x}{p}", 8, 4, 4)

    ffn(0)
    section("dt", 2, 1, 0)
    section("att", 4 * PAIRS, 3 * PAIRS, 3 * PAIRS)
    section("gba", 4, 2, 2)
    section("ga", 16, 8, 8)
    section("ssdx", 4, 2, 2)
    section("ssd", 6 * NG, 3 * NG, 3 * NG)
    section("yo", 16, 4, 4)
    section("mix", 8, 4, 4)
    ffn(1)
    section("end", 0, 0, 0)
    return w, (o0, o1)


CONV_AT = (1, 3, 4, 5)


def following(i, p, c):
    return (i, p, c + 1) if c < NT - 1 else (i + 1, 1 - p, 0)


W, O = plan()
BLOCKS = W["end"]

ASTEPS = [(q, h) for q in range(NT) for h in range(2)]
AGROUPS = [1 + (q >= 4) for q, _ in ASTEPS]
AGROUP0 = [sum(AGROUPS[:s]) for s in range(len(ASTEPS) + 1)]
AGB0 = [sum(g - 1 for g in AGROUPS[:s]) for s in range(len(ASTEPS) + 1)]
NA = len(ASTEPS)


def att_events():
    ev = [("half", 0, k, t) for k in range(8) for t in range(2)]
    ev += [("half", 1, k, t) for k in range(4) for t in range(2)]
    ev += [("rot", 0)]
    ev += [("half", 1, k, t) for k in range(4, 8) for t in range(2)]
    ev += [("half", 2, k, t) for k in range(4) for t in range(2)]
    ev += [("rot", 1)]
    ev += [("half", 3, k, t) for k in range(4, 8) for t in range(2)]
    return ev


AEV = att_events()
A_PER_STEP = 3
GEV = [("gate", j, k, t) for j in range(4) for k in range(8) for t in range(2)]
G_PER_STEP = 4


def step_events(s, gemm):
    ev, per = (AEV, A_PER_STEP) if gemm else (GEV, G_PER_STEP)
    return ev[s * per:(s + 1) * per]


def kernel_program(nc, x, c, positions, w_ada, b_ada, norm1_w, ffn1_w_gu, ffn1_w_down, norm2_w, w_in,
                   conv_w, conv_b, dt_bias, a_log, d_skip, ssd_norm_w, w_att_out, w_ssd_out, w_mix_out,
                   norm3_w, ffn2_w_gu, ffn2_w_down, final_norm_w, table, out):
    ctx = ExitStack()
    with ctx:
        def dram(name, shape):
            return nc.dram_tensor(name, shape, F32, kind="Internal").ap()

        x_keep = dram("x_keep", (P, DT_, T))
        merged_keep = dram("merged_keep", (DT_, P, T))
        gate_keep = dram("gate_keep", (DT_, P, T))
        y_keep = dram("y_keep", (NG, P, 2, T))
        cs_keep = dram("cs_keep", (SH, T))
        dec_keep = dram("dec_keep", (SH, NT))

        SLAB_KB = 207.125
        origin = 16512
        ctx.enter_context(nc.sbuf_tensor("slab", [P, int(SLAB_KB * 256)], F32))

        def sb(name, kb, shape, dt=F32):
            size = int(np.prod(shape)) * 4
            assert kb * 1024 + size <= SLAB_KB * 1024, name
            return nc.alloc_sbuf_tensor_at(name, [P, *shape], dt, offset=origin + int(kb * 1024))

        w_raw = sb("w_raw", 0, [2, 8, P])
        w_hi = sb("w_hi", 8, [2, 8, P], F32R)
        w_lo = sb("w_lo", 16, [2, 8, P], F32R)
        h_hi = sb("h_hi", 24, [8, T], F32R)
        h_lo = sb("h_lo", 56, [8, T], F32R)
        xT = sb("xT", 88, [8, T])
        hid_hi = sb("hid_hi", 120, [7, T], F32R)
        hid_lo = sb("hid_lo", 148, [7, T], F32R)
        ada = sb("ada", 176, [8, ADA_W])
        acc = sb("acc", 176, [T])
        rstd = sb("rstd", 180, [T])
        sq = sb("sq", 184, [2, T])
        tmp = sb("tmp", 192, [2, T])
        xs = sb("xs", 184, [4, T])
        x_nat = sb("x_nat", 120, [NT, D])
        ada_start = sb("ada_start", 24, [ADA_FIRST, 8, ADA_W])
        mod_row = sb("mod_row", 152, [ADA_FIRST, ADA_W])
        par1 = sb("par1", 168, [3, P])
        x_w = sb("x_w", 24, [8, T])
        o_row = sb("o_row", 120, [NT, D])
        cosT = sb("cosT", 88, [T])
        sinT = sb("sinT", 92, [T])
        q_st = sb("q_st", 96, [T])
        k_st = sb("k_st", 100, [T])
        v_st = sb("v_st", 96, [T])
        dt_keep = sb("dt_keep", 104, [NT * SH])
        den_diag = sb("den_diag", 105, [2, P])
        o_T = sb("o_T", 106, [P])
        qT = sb("qT", 108, [2, T])
        kT = sb("kT", 116, [2, T])
        v_tok = sb("v_tok", 124, [2, NT, P])
        prob = sb("prob", 132, [2, T])
        mask = sb("mask", 140, [T])
        o_hi = sb("o_hi", 144, [PAIRS, T], F32R)
        o_lo = sb("o_lo", 168, [PAIRS, T], F32R)
        probT = sb("probT", 192, [2, T])
        sin_w = sb("sin_w", 136, [T])
        pos_i = sb("pos_i", 140, [T], I32)
        ang = sb("ang", 144, [T])
        rt1 = sb("rt1", 164, [T])
        rt2 = sb("rt2", 168, [T])
        cos_w = sb("cos_w", 172, [T])
        dt_w = [sb(f"dt_w{j}", 144 + 4 * j, [T]) for j in range(4)]
        dtT = sb("dtT", 160, [T])
        csT = sb("csT", 164, [T])
        dteT = sb("dteT", 168, [T])
        conv_in = sb("conv_in", 88, [2, T + 4])
        xbc = sb("xbc", 97, [2, 4, T])
        z_sil = sb("z_sil", 129, [2, T])
        cs_b = sb("cs_b", 137, [NT, GH, P])
        decay = sb("decay", 153, [2, GH, P])
        wT = sb("wT", 157, [2, GH, P])
        c_scaled = sb("c_scaled", 161, [2, GH, P])
        ecs = sb("ecs", 165, [2, GH, P])
        xdt = sb("xdt", 169, [2, 2 * P])
        xdte = sb("xdte", 171, [2, 2 * P])
        b_tok = sb("b_tok", 173, [2, P])
        state = sb("state", 174, [2, 2 * P])
        y_sq = sb("y_sq", 176, [T])
        y_acc = sb("y_acc", 180, [T])
        y_hi = sb("y_hi", 24, [16, T], F32R)
        y_lo = sb("y_lo", 88, [16, T], F32R)
        y_raw = sb("y_raw", 88, [16, T])
        merged = sb("merged", 152, [8, T])
        y_rstd = sb("y_rstd", 184, [T])
        gate = sb("gate", 188, [T])
        m_hi = sb("m_hi", 24, [8, T], F32R)
        m_lo = sb("m_lo", 56, [8, T], F32R)
        kst = sb("kst", 200, [K_PERSIST + 1])
        par = sb("par", 202.125, [R_ALL])
        mod = sb("mod", 203.25, [72])
        small = sb("small", 203.5625, [112])
        rcol = sb("rcol", 207, [NT])
        ada_red = sb("ada_red", 204, [ADA_W])
        cs_tok = sb("cs_tok", 204, [NT, SH])
        dte_tok = sb("dte_tok", 205, [NT, SH])
        dec_b = sb("dec_b", 206, [SH, NT])
        dt_tok = sb("dt_tok", 191, [NT, SH])
        assert K_PERSIST + 1 <= 544 and R_ALL <= 288 and 202.125 + R_ALL / 256 <= 203.25

        Y_EARLY = 3
        assert 88 + 8 * Y_EARLY <= 97 + 16

        ident = kst[:, K_ID:K_ID + P]
        ones = kst[:, K_ONE:K_ONE + P]
        causal = kst[:, K_NEG:K_NEG + P]
        rotm = kst[:, K_ROT:K_ROT + P]
        invf = kst[:, K_INVF:K_INVF + 1]
        c_act = small[:, 0:8]
        scale1, scale2, scale3 = (small[:, 8 + 8 * j:16 + 8 * j] for j in range(3))
        gate1, gate3 = small[:, 32:40], small[:, 40:48]
        d_col = small[:, 48:64]
        negmax = small[:, 64:66]
        den = small[:, 74:78]
        rden = small[:, 68:70]
        head_col = small[0:SH, 70:73]
        d_row = small[:, 78:110]
        eps_col = small[:, 110:111]
        dec_head = dt_w[3][0:SH, 0:NT]
        SH1, SC1, G1, SH2, SC2, G2, SH3, SC3, G3 = (8 * j for j in range(9))

        psG = ctx.enter_context(nc.psum_tensor("psG", [P, 2, 2, 512], F32))
        psS = ctx.enter_context(nc.psum_tensor("psS", [P, 2, 512], F32))
        psT = ctx.enter_context(nc.psum_tensor("psT", [P, 512], F32))
        psO = ctx.enter_context(nc.psum_tensor("psO", [P, 512], F32))

        def sem(name):
            return ctx.enter_context(nc.semaphore(name))

        w_loaded = [sem("w_loaded0"), sem("w_loaded1")]
        w_hi_done, w_lo_done, w_used = sem("w_hi_done"), sem("w_lo_done"), sem("w_used")
        freed = [sem("psum0_read"), sem("psum1_read")]
        s_table, s_rows, s_small, s_xin, s_xtr, s_xt = (sem(n) for n in (
            "table_loaded", "rows_loaded", "small_loaded", "x_loaded", "x_transposed", "xT_written"))
        s_par_ps, s_par, s_cact = sem("par_transposed"), sem("par_written"), sem("c_act_done")
        s_ada = [sem(f"ada_loaded{j}") for j in range(ADA_FIRST + 1)]
        s_ada_mul, s_ada_red, s_ada_mm, s_ada_done = (sem(n) for n in (
            "ada_scaled", "ada_reduced", "ada_summed", "mod_written"))
        s_row, s_row_out = sem("mod_row_summed"), sem("mod_row_done")
        s_first_cols, s_g1 = sem("scale_columns"), sem("gate1_column")
        s_sq, s_acc, s_ms, s_rt, s_diag, s_spread, s_xr, s_hhi = (sem(n) for n in (
            "squared", "squares_added", "square_sums", "root_done", "diagonals", "rstd_spread", "x_scaled",
            "h_hi_done"))
        s_hlo, s_eps = [sem("h_lo_even"), sem("h_lo_odd")], sem("eps_written")
        s_hid_hi, s_hid_lo = sem("hid_hi_done"), sem("hid_lo_done")
        s_xkeep, s_xback = sem("x_kept"), sem("x_back")
        s_dt_e, s_dt_ln, s_dt_cs, s_dt_dte, s_dt_ready, s_dt_tr, s_dt_tok = (sem(n) for n in (
            "dt_abs", "dt_log", "cs_done", "dte_exp", "dte_done", "dt_transposed", "dt_tok_done"))
        s_cs_kept, s_dec, s_dec_kept = sem("cs_kept"), sem("dec_loaded"), sem("dec_kept")
        s_pos, s_mask, s_ang, s_trig = sem("pos_loaded"), sem("mask_loaded"), sem("angle_done"), sem("trig_done")
        s_trig_in = sem("trig_moved")
        s_qk, s_masked, s_exp, s_tr, s_pta, s_ptb, s_dd, s_pv, s_o, s_ohi, s_olo = (sem(n) for n in (
            "qk_done", "masked", "exp_done", "prob_transposed", "probT_a", "probT_b", "den_diagonal",
            "pv_done", "o_scaled", "o_hi_done", "o_lo_done"))
        s_rot, s_cosed, s_roped, s_vtr, s_vtok = sem("rot_done"), sem("cos_part_done"), sem("roped"), sem("v_transposed"), sem("v_tok_done")
        s_mg_out, s_gt_out = sem("merged_kept"), [sem("gate_kept0"), sem("gate_kept1")]
        s_conv, s_conv_act = sem("conv_done"), sem("conv_act_done")
        s_csb = [sem(f"cs_b_loaded{j}") for j in range(NT)]
        s_arg, s_dec_exp, s_ecs, s_cscaled, s_tokT, s_cb, s_btok, s_xdte, s_wT, s_y, s_st, s_state, s_yev = (
            sem(n) for n in ("decay_arg", "decay_exp", "ecs_done", "c_scaled_done", "tok_transposed", "cb_done",
                             "b_tok_done", "xdte_done", "wT_done", "y_done", "state_mm", "state_done", "y_evac"))
        s_gated, s_ysq, s_yacc, s_yout = sem("y_gated"), sem("y_squared"), sem("y_sq_added"), sem("y_kept")
        s_yin = [sem(f"y_loaded{g}") for g in range(NG)]
        s_yhi, s_ylo = sem("y_hi_done"), sem("y_lo_done")
        s_mg_in, s_gt_in, s_gate = sem("merged_loaded"), sem("gate_loaded"), sem("gate_done")
        s_mg, s_mhi = sem("merged_done"), sem("m_hi_done")
        s_mlo = [sem("m_lo_even"), sem("m_lo_odd")]
        s_xw, s_ftr, s_rinv, s_out = (sem(n) for n in ("x_weighted", "final_transposed", "final_rstd", "out_written"))
        s_orow = [sem("row_half0"), sem("row_half1")]
        pe_phase, act_phase, dve_phase, pool_phase = (sem(n) for n in (
            "pe_phase", "act_phase", "dve_phase", "pool_phase"))
        sp_turn, dve_turn = sem("sp_turn"), sem("dve_turn")
        c_act_sem, c_dve_sem, c_pool_sem = sem("act_chain"), sem("dve_chain"), sem("pool_chain")
        block = ctx.enter_context(nc.Block())

        def final_bank(t, u):
            b = t % 3
            return psS[:, u, :] if b == 2 else psG[:, b, u, :]

        def gu_cols(w, col):
            return w[0].rearrange("(k p) m -> p k m", p=P)[:, :, bass.ds(col, P)]

        ffn_w = ((ffn1_w_gu, ffn1_w_down), (ffn2_w_gu, ffn2_w_down))

        @block.sync
        def _(sp):
            def load(n, j, src, kt):
                at_least(sp, w_lo_done, n - 1)
                sp.sem_inc(sp_turn, 1)
                sp.dma_start(w_raw[:, j, 0:kt, :], src).then_inc(w_loaded[j], 16)

            def load_ada(chunk, dst, which):
                src = w_ada[0].rearrange("(k p) m -> p k m", p=P)[:, :, bass.ds(chunk * ADA_W, ADA_W)]
                sp.dma_start(dst, src).then_inc(s_ada[which], 16)

            def ffn_loads(x, after_first=None):
                w_gu, w_dn = ffn_w[x]
                for p, (f0, cnt) in enumerate(PARTS):
                    n0 = W[f"gu{x}{p}"]

                    def pair(i, n0=n0, f0=f0):
                        load(n0 + i * 2, 0, gu_cols(w_gu, (i + f0) * P), 8)
                        load(n0 + 1 + i * 2, 1, gu_cols(w_gu, (i + f0) * P + FF), 8)
                        if x == 0 and p < 2:
                            q = i + f0
                            at_least(sp, s_ada_red, q)
                            if isinstance(i, int) and q == 0:
                                for s_ in s_hlo:
                                    sp.wait_ge(s_, 4)
                            load_ada(q + ADA_FIRST, ada[:], ADA_FIRST)
                    if p == 0:
                        pair(0)
                        with sp.Fori(1, cnt) as i:
                            pair(i)
                    else:
                        with sp.Fori(0, cnt) as i:
                            pair(i)
                    n1 = W[f"dn{x}{p}"]
                    rows = w_dn[0][f0 * P:(f0 + cnt) * P, :].rearrange("(k p) m -> p k m", p=P)
                    with sp.Fori(0, 4) as i:
                        for j in range(2):
                            load(n1 + i * 2 + j, j, rows[:, :, bass.ds((i * 2 + j) * P, P)], cnt)

            sp.dma_start(kst[:, 0:K_PERSIST], table[:, 0:K_PERSIST]).then_inc(s_table, 16)
            x_rows = x[0].rearrange("(h q p) d -> h p q d", h=2, p=P)
            sp.dma_start(x_nat[:, 0:4], x_rows[0]).then_inc(s_xin, 16)
            sp.dma_start(par1[0:72, 0, :], b_ada.rearrange("o (r p) -> (o r) p", p=P)).then_inc(s_rows, 16)
            for r0, v in ((R_N1, norm1_w), (R_N2, norm2_w), (R_N3, norm3_w), (R_SN, ssd_norm_w), (R_C, c)):
                rows = v.shape[1] // P
                sp.dma_start(par1[r0:r0 + rows, 0, :], v.rearrange("o (r p) -> (o r) p", p=P)).then_inc(s_rows, 16)
            sp.dma_start(par1[R_FN:R_FN + 8, 0, :], final_norm_w.rearrange("(r p) -> r p", p=P)).then_inc(s_rows, 16)
            sp.dma_start(par1[:, 1, :], conv_w[0].rearrange("j (r p) -> (j r) p", p=P)).then_inc(s_rows, 16)
            sp.dma_start(par1[0:32, 2, :], conv_b.rearrange("o (r p) -> (o r) p", p=P)).then_inc(s_rows, 16)
            sp.wait_ge(s_xin, 16)
            sp.dma_start(x_nat[:, 4:8], x_rows[1]).then_inc(s_xin, 16)
            for q in range(ADA_FIRST):
                load_ada(q, ada_start[:, q], q)
            sp.dma_start(d_row, d_skip.to_broadcast([P, SH])).then_inc(s_small, 16)
            with nc.allow_non_contiguous_dma(reason="32 heads' scalars, one per partition"):
                sp.dma_start(head_col[:, 0:1], dt_bias.rearrange("o h -> h o")).then_inc(s_small, 16)
                sp.dma_start(head_col[:, 1:2], a_log.rearrange("o h -> h o")).then_inc(s_small, 16)
            ffn_loads(0)

            win = w_in[0].rearrange("(k p) m -> p k m", p=P)
            load(W["dt"], 0, win[:, 0:4, O_DT:O_DT + P], 4)
            load(W["dt"] + 1, 1, win[:, 4:8, O_DT:O_DT + P], 4)
            sp.wait_ge(freed[0], O[0]["dt"])
            sp.wait_ge(freed[1], O[1]["dt"])
            sp.dma_start(x_keep, xT[:]).then_inc(s_xkeep, 16)
            na = W["att"]
            with sp.Fori(0, PAIRS) as i:
                load(na + i * 4, 0, win[:, :, bass.ds(i * P + O_Q, P)], 8)
                load(na + i * 4 + 1, 1, win[:, :, bass.ds(i * P + O_K, P)], 8)
                load(na + i * 4 + 2, 0, win[:, 0:4, bass.ds(i * P + O_V, P)], 4)
                load(na + i * 4 + 3, 1, win[:, 4:8, bass.ds(i * P + O_V, P)], 4)
            with sp.Fori(0, 2) as i:
                for j in range(2):
                    load(W["gba"] + i * 2 + j, j, win[:, :, bass.ds((i * 2 + j) * P + O_G1, P)], 8)
            wao = w_att_out[0].rearrange("(k p) m -> p k m", p=P)
            with sp.Fori(0, 8) as i:
                load(W["ga"] + i * 2, 0, win[:, :, bass.ds(i * P + O_G0, P)], 8)
                load(W["ga"] + 1 + i * 2, 1, wao[:, :, bass.ds(i * P, P)], 6)

            def ssd_x(n, g):
                load(n, 0, win[:, :, bass.ds(g * 2 * P + O_X, P)], 8)
                load(n + 1, 1, win[:, :, bass.ds(g * 2 * P + O_X + P, P)], 8)
                load(n + 2, 0, win[:, :, bass.ds(g * P + O_B, P)], 8)
                load(n + 3, 1, win[:, :, bass.ds(g * P + O_C, P)], 8)

            def ssd_z(n, g):
                load(n, 0, win[:, :, bass.ds(g * 2 * P + O_Z, P)], 8)
                load(n + 1, 1, win[:, :, bass.ds(g * 2 * P + O_Z + P, P)], 8)

            ssd_x(W["ssdx"], 0)
            with sp.Fori(0, NG - 1) as g:
                ssd_x(W["ssd"] + g * 6, g + 1)
                ssd_z(W["ssd"] + g * 6 + 4, g)
            for j in range(4):
                load(W["ssd"] + (NG - 1) * 6 + j, j % 2, win[:, :, O_G1 + (4 + j) * P:O_G1 + (5 + j) * P], 8)
            ssd_z(W["ssd"] + (NG - 1) * 6 + 4, NG - 1)
            wso = w_ssd_out[0].rearrange("(k p) m -> p k m", p=P)
            load(W["yo"], 0, wso[:, 0:8, 0:P], 8)
            load(W["yo"] + 1, 1, wso[:, 8:16, 0:P], 8)
            past(sp, s_conv, 4 * NG)
            past(sp, s_conv_act, 4 * NG)
            for g in range(NG):
                if g == 0:
                    past(sp, s_yout, 16 * (NG - 1))
                    past(sp, s_ysq, 2 * (NG - 1))
                elif g == Y_EARLY:
                    for e in (pe_phase, act_phase, dve_phase, pool_phase):
                        sp.wait_ge(e, 2)
                    past(sp, s_yout, 16 * NG)
                sp.dma_start(y_raw[:, 2 * g:2 * g + 2, :], y_keep[g]).then_inc(s_yin[g], 16)
            for j in range(2):
                load(W["yo"] + 2 + j, j, wso[:, 8 * j:8 * j + 8, P:2 * P], 8)
            sp.wait_ge(s_mg_out, 16 * 8)
            sp.wait_ge(s_ms, 3)
            sp.dma_start(merged[:], merged_keep.rearrange("d p t -> p d t")).then_inc(s_mg_in, 16)
            for s in s_gt_out:
                sp.wait_ge(s, 16 * 4)
            sp.dma_start(gate[:], gate_keep[0]).then_inc(s_gt_in, 16)

            def load_gate(i):
                sp.wait_ge(s_mg, i)
                sp.dma_start(gate[:], gate_keep[bass.ds(i, 1)].rearrange("o p t -> (o p) t")).then_inc(s_gt_in, 16)
            with sp.Fori(2, 8) as i:
                for j in range(2):
                    load(W["yo"] + i * 2 + j, j, wso[:, 8 * j:8 * j + 8, bass.ds(i * P, P)], 8)
                load_gate(i - 1)
            load_gate(7)
            wmo = w_mix_out[0].rearrange("(k p) m -> p k m", p=P)
            load(W["mix"], 0, wmo[:, :, 0:P], 8)
            load(W["mix"] + 1, 1, wmo[:, :, P:2 * P], 8)
            sp.wait_ge(w_used, W["mix"])
            sp.wait_ge(s_xkeep, 16)
            sp.dma_start(xT[:], x_keep).then_inc(s_xback, 16)
            with sp.Fori(1, 4) as i:
                for j in range(2):
                    load(W["mix"] + i * 2 + j, j, wmo[:, :, bass.ds((i * 2 + j) * P, P)], 8)
            ffn_loads(1)
            for t in range(NT):
                for s_ in s_orow:
                    sp.wait_ge(s_, t + 1)
                sp.dma_start(out[0, t * P:(t + 1) * P, :], o_row[:, t, :]).then_inc(s_out, 16)
            sp.wait_ge(s_out, 16 * NT)

        @block.tensor
        def _(pe):
            mm = nc.tensor.matmul
            for s in (s_qk, s_tr, s_pv, s_rot, s_vtr, s_tokT, s_cb, s_y, s_st):
                pe.sem_inc(s, CREDIT)

            def passes(out_, j, k, rh, rl, first, last):
                mm(out_, w_lo[:, j, k, :], rh, start=first, stop=False)
                mm(out_, w_hi[:, j, k, :], rl, start=False, stop=False)
                return mm(out_, w_hi[:, j, k, :], rh, start=False, stop=last)

            def product(n, j, b, m, hi, lo, kt, k_off=0, first=True, last=True, ready=None):
                pe.wait_ge(w_lo_done, n + 1)
                if first:
                    at_least(pe, freed[b], m)
                for k in range(kt):
                    if ready is not None:
                        ready(k)
                    for t in range(2):
                        cols = slice(512 * t, 512 * t + 512)
                        ins = passes(psG[:, b, t, :], j, k, hi[:, k_off + k, cols], lo[:, k_off + k, cols],
                                     first and k == 0, last and k == kt - 1)
                ins.then_inc(w_used, 1)

            def transpose(out_, in_, rows=P):
                return nc.tensor.transpose(out_, in_, ident[0:rows, 0:rows])

            def ada_sum(q):
                src, dst = ada_red, psO[:, 0:4]
                pe.wait_ge(s_ada_red, q - ADA_FIRST + 1)
                at_least(pe, s_ada_done, q)
                for j in range(4):
                    ins = mm(dst[:, j:j + 1], src[:, j * P:(j + 1) * P], ones[:, 0:1], start=True, stop=True)
                ins.then_inc(s_ada_mm, 1)

            def h_ready(idx):
                def wait(k):
                    pe.wait_ge(s_hlo[k % 2], 4 * idx + k // 2 + 1)
                return wait

            def token_sums(src):
                for t in range(NT):
                    ins = mm(psT[:, t:t + 1], src[:, t * P:(t + 1) * P], ones[:, 0:1], start=True, stop=True)
                ins.then_inc(s_ms, 1)

            def spread(count, diag):
                pe.wait_ge(s_diag, count)
                for t in range(2):
                    ins = mm(psS[:, t, :], ones, diag[:, 512 * t:512 * t + 512], start=True, stop=True)
                ins.then_inc(s_spread, 1)

            def norm_sum(idx, count):
                pe.wait_ge(s_acc, 8 * (idx + 1))
                token_sums(acc)
                spread(count, rstd)

            def ffn(x, idx):
                for p, (f0, cnt) in enumerate(PARTS):
                    s = f"gu{x}{p}"
                    n0, a0, a1 = W[s], O[0][s], O[1][s]

                    def pair(i, ready=None):
                        product(n0 + i * 2, 0, 0, a0 + i, h_hi, h_lo, 8, ready=ready)
                        if x == 0 and p < 2:
                            ada_sum_step(i, f0)
                        product(n0 + 1 + i * 2, 1, 1, a1 + i, h_hi, h_lo, 8)

                    def ada_sum_step(i, f0):
                        if isinstance(i, int) and i + f0 == 0:
                            return
                        ada_sum(i + (f0 + ADA_FIRST - 1))

                    if p == 0:
                        pair(0, ready=h_ready(idx))
                        with pe.Fori(1, cnt) as i:
                            pair(i)
                    else:
                        with pe.Fori(0, cnt) as i:
                            pair(i)
                    s = f"dn{x}{p}"
                    n0, a0, a1 = W[s], O[0][s], O[1][s]

                    def hidden(k, F=FT * x + f0, cnt=cnt):
                        if k in (0, cnt - 2, cnt - 1):
                            pe.wait_ge(s_hid_lo, F + max(k + 1, cnt - 2))
                    for j in range(2):
                        product(n0 + j, j, j, (a0, a1)[j], hid_hi, hid_lo, cnt, ready=hidden if j == 0 else None)
                        if x == 0 and p == 1 and j == 0:
                            ada_sum(ADA_ALL - 1)
                    with pe.Fori(1, 4) as i:
                        for j in range(2):
                            product(n0 + i * 2 + j, j, j, (a0, a1)[j] + i, hid_hi, hid_lo, cnt)

            pe.wait_ge(s_table, 16)
            pe.wait_ge(s_rows, 16 * 9)
            transpose(psT[:, 0:R_P1], par1[0:R_P1, 0, :], R_P1)
            transpose(psT[:, R_CW:R_CW + P], par1[:, 1, :])
            transpose(psT[:, R_CB:R_CB + 32], par1[0:32, 2, :], 32).then_inc(s_par_ps, 1)
            for t in range(NT):
                pe.wait_ge(s_xin, 16 * (t // 4 + 1))
                for u in range(2):
                    i = 2 * t + u
                    at_least(pe, s_xt, i - 1)
                    for j in range(4):
                        ins = transpose(psS[:, u, j * P:(j + 1) * P], x_nat[:, t, (4 * u + j) * P:(4 * u + j + 1) * P])
                    ins.then_inc(s_xtr, 1)
            pe.wait_ge(s_cact, 1)

            def mod_row_product(q):
                pe.wait_ge(s_ada[q], 16)
                for k in range(8):
                    ins = mm(psG[0:1, q // 2, q % 2, :], c_act[:, k:k + 1], ada_start[:, q, k, :],
                             start=(k == 0), stop=(k == 7))
                ins.then_inc(s_row, 1)

            def mod_columns(q):
                pe.wait_ge(s_row_out, q + 1)
                for m in range(4):
                    ins = mm(psO[:, 4 * q + m:4 * q + m + 1], mod_row[0:1, q, m * P:(m + 1) * P], ones[0:1, 0:1],
                             start=True, stop=True)
                return ins
            for q in range(ADA_FIRST):
                if q == ADA_FIRST - 1:
                    pe.wait_ge(s_acc, 8)
                    token_sums(acc)
                mod_row_product(q)
                if q:
                    mod_columns(q - 1)
            mod_columns(ADA_FIRST - 1).then_inc(s_ada_mm, ADA_FIRST)
            spread(1, rstd)
            ffn(0, 0)

            norm_sum(1, 2)
            product(W["dt"], 0, 0, O[0]["dt"], h_hi, h_lo, 4, 0, True, False, ready=h_ready(1))
            n = W["dt"] + 1
            pe.wait_ge(w_lo_done, n + 1)
            for k in range(4):
                h_ready(1)(4 + k)
                for t in range(2):
                    cols = slice(512 * t, 512 * t + 512)
                    ins = passes(psG[:, 0, t, :], 1, k, h_hi[:, 4 + k, cols], h_lo[:, 4 + k, cols], False, k == 3)
            ins.then_inc(w_used, 1)

            def att_half(i, j, k, t):
                n = W["att"] + i * 4 + j
                b = (0, 1, 0, 0)[j]
                m = (O[0]["att"] + i * 3, O[1]["att"] + i * 3, O[0]["att"] + i * 3 + 2, 0)[j]
                kk = k - 4 if j == 3 else k
                if kk == 0 and t == 0:
                    pe.wait_ge(w_lo_done, n + 1)
                    if j < 3:
                        pe.wait_ge(freed[b], m)
                cols = slice(512 * t, 512 * t + 512)
                ins = passes(psG[:, b, t, :], j % 2, kk, h_hi[:, k, cols], h_lo[:, k, cols], k == 0, k == 7)
                if t == 1 and kk == (3 if j > 1 else 7):
                    ins.then_inc(w_used, 1)

            def att_rot(i, b):
                m = O[b]["att"] + i * 3 + 1
                pe.wait_ge(freed[b], m)
                src = (q_st, k_st)[b]
                for t in range(2):
                    ins = mm(psG[:, b, t, :], rotm, src[:, 512 * t:512 * t + 512], start=True, stop=True)
                ins.then_inc(s_rot, 1)

            def att_vtr(i):
                pe.wait_ge(freed[1], O[1]["att"] + i * 3 + 2)
                pe.wait_ge(freed[0], O[0]["att"] + i * 3 + 3)
                for t in range(NT):
                    ins = transpose(psG[:, 1, t // 4, (t % 4) * P:(t % 4 + 1) * P], v_st[:, t * P:(t + 1) * P])
                ins.then_inc(s_vtr, 1)

            def gate_half(j, k, t):
                b = j % 2
                if k == 0 and t == 0:
                    pe.wait_ge(w_lo_done, W["gba"] + j + 1)
                    pe.wait_ge(freed[b], O[b]["gba"] + j // 2)
                cols = slice(512 * t, 512 * t + 512)
                ins = passes(psG[:, b, t, :], b, k, h_hi[:, k, cols], h_lo[:, k, cols], k == 0, k == 7)
                if t == 1 and k == 7:
                    ins.then_inc(w_used, 1)

            def att_event(i, e):
                if e[0] == "half":
                    att_half(i, *e[1:])
                elif e[0] == "rot":
                    att_rot(i, e[1])
                else:
                    gate_half(*e[1:])

            def att_iter(i, par_, att, gemm):
                S = i * NA
                TR = i * AGROUP0[NA]
                for s in range(NA + 2):
                    evs = step_events(s, gemm)
                    slots = [evs[0:1], evs[1:2], evs[2:3], evs[3:]]
                    for e in slots[0]:
                        att_event(i + 1, e)
                    r = s - 1
                    if att and 0 <= r < NA:
                        q, h = ASTEPS[r]
                        past(pe, s_exp, S + r + 1)
                        past(pe, s_pta, S + r)
                        past(pe, s_ptb, i * AGB0[NA] + AGB0[r])
                        for j in range(min(q + 1, 4)):
                            ins = transpose(psT[:, j * P:(j + 1) * P], prob[:, r % 2, j * P:(j + 1) * P])
                        ins.then_inc(s_tr, 1)
                    r = s - 2
                    if att and 0 <= r < NA and r % 2 == 1:
                        q = ASTEPS[r][0]
                        if r == 1:
                            past(pe, s_vtok, i + 1)
                        past(pe, s_pta, S + r + 1)
                        if q >= 4:
                            past(pe, s_ptb, i * AGB0[NA] + AGB0[r + 1])
                        past(pe, s_o, i * NT + q)
                        for j in range(q + 1):
                            for h in range(2):
                                mm(psO[HD * h:HD * h + HD, 0:P], v_tok[:, par_, j, HD * h:HD * h + HD],
                                   probT[:, h, j * P:(j + 1) * P], start=(j == 0), stop=(j == q))
                        past(pe, s_dd, S + r + 1)
                        for h in range(2):
                            ins = mm(psO[HD * h:HD * h + HD, P:2 * P], ones[:, 0:HD], den_diag[:, h, :],
                                     start=True, stop=True)
                        ins.then_inc(s_pv, 1)
                    if att and s < NA:
                        q, h = ASTEPS[s]
                        rows = slice(HD * h, HD * h + HD)
                        if s == 0:
                            past(pe, s_roped, i * 2 + 2)
                        past(pe, s_masked, S + s)
                        width = (q + 1) * P
                        for t in range((width + 511) // 512):
                            c0, c1 = 512 * t, min(width, 512 * t + 512)
                            ins = mm(psS[:, t, 0:c1 - c0], qT[rows, par_, q * P:(q + 1) * P],
                                     kT[rows, par_, c0:c1], start=True, stop=True)
                        ins.then_inc(s_qk, 1)
                    if att and s == 1:
                        att_vtr(i)
                    for e in slots[1]:
                        att_event(i + 1, e)
                    r = s - 1
                    if att and 0 <= r < NA and ASTEPS[r][0] >= 4:
                        q, h = ASTEPS[r]
                        past(pe, s_pta, S + r + 1)
                        for j in range(4, q + 1):
                            ins = transpose(psT[:, (j - 4) * P:(j - 3) * P], prob[:, r % 2, j * P:(j + 1) * P])
                        ins.then_inc(s_tr, 1)
                    for e in slots[2]:
                        att_event(i + 1, e)
                    for e in slots[3]:
                        att_event(i + 1, e)

            att_iter(-1, 0, False, True)
            pe.wait_ge(s_dt_cs, 1)
            pe.wait_ge(s_dt_ready, 1)
            for u, src in enumerate((csT, dtT, dteT)):
                for t in range(NT):
                    dst = psS[:, u // 2, (u % 2) * 256 + t * SH:(u % 2) * 256 + (t + 1) * SH]
                    ins = transpose(dst, src[0:SH, t * P:(t + 1) * P], SH)
            ins.then_inc(s_dt_tr, 1)
            pe.wait_ge(s_dt_tok, 1)
            with pe.Fori(0, PAIRS // 2 - 1) as i2:
                att_iter(i2 * 2, 0, True, True)
                att_iter(i2 * 2 + 1, 1, True, True)
            att_iter(PAIRS - 2, 0, True, True)
            att_iter(PAIRS - 1, 1, True, False)

            past(pe, s_olo, PAIRS * NT)
            with pe.Fori(0, 8) as i:
                product(W["ga"] + i * 2, 0, 0, O[0]["ga"] + i, h_hi, h_lo, 8)
                product(W["ga"] + 1 + i * 2, 1, 1, O[1]["ga"] + i, o_hi, o_lo, 6)
            for j in range(4):
                product(W["ssdx"] + j, j % 2, j % 2, O[j % 2]["ssdx"] + j // 2, h_hi, h_lo, 8)

            def ssd_front(i, p, c):
                n = i * NT + c
                tok = slice(c * P, (c + 1) * P)
                if c == 0:
                    past(pe, s_conv_act, i * 4 + 4)
                past(pe, s_xdte, n)
                past(pe, s_btok, n)
                for j in range(3):
                    ins = transpose(psT[:, j * P:(j + 1) * P], xbc[:, p, j, tok])
                ins.then_inc(s_tokT, 1)
                past(pe, s_wT, n)
                mm(psS[:, 0, 0:P], xbc[:, p, 2, tok], xbc[:, p, 3, tok], start=True, stop=True).then_inc(s_cb, 1)

            def ssd_back(i, p, c):
                n = i * NT + c
                past(pe, s_wT, n + 1)
                past(pe, s_xdte, n + 1)
                past(pe, s_cscaled, n + 1)
                past(pe, s_yev, n)
                if c > 0:
                    past(pe, s_state, i * (NT - 1) + c)
                for e in range(GH):
                    dst = psS[HD * (e % 2):HD * (e % 2) + HD, 1, (e // 2) * P:(e // 2 + 1) * P]
                    cols = slice(e * HD, (e + 1) * HD)
                    ins = mm(dst, xdt[:, c % 2, cols], wT[:, c % 2, e, :], start=True, stop=(c == 0))
                    if c > 0:
                        ins = mm(dst, state[:, (c - 1) % 2, cols], c_scaled[:, c % 2, e, :], start=False, stop=True)
                ins.then_inc(s_y, 1)
                if c < NT - 1:
                    past(pe, s_btok, n + 1)
                    past(pe, s_state, i * (NT - 1) + c)
                    mm(psO[:, 0:2 * P], b_tok[:, c % 2, :], xdte[:, c % 2, :], start=True, stop=True).then_inc(s_st, 1)

            def ssd_iter(i, p, gemm):
                n0 = W["ssd"] + i * 6
                halves = [(j, k) for j in range(6) for k in range(8)]

                def slice_(part):
                    for j, k in part:
                        n = n0 + j
                        b = j % 2
                        if k == 0:
                            pe.wait_ge(w_lo_done, n + 1)
                            pe.wait_ge(freed[b], O[b]["ssd"] + i * 3 + j // 2)
                        for t in range(2):
                            cols = slice(512 * t, 512 * t + 512)
                            ins = passes(psG[:, b, t, :], b, k, h_hi[:, k, cols], h_lo[:, k, cols], k == 0, k == 7)
                        if k == 7:
                            ins.then_inc(w_used, 1)

                for c in range(NT):
                    if gemm or c < NT - 1:
                        ssd_front(*following(i, p, c))
                    ssd_back(i, p, c)
                    slice_(halves[6 * c:6 * (c + 1)])

            pe.wait_ge(s_dec, 16)
            ssd_front(0, 0, 0)
            ssd_iter(0, 0, True)
            with pe.Fori(0, NG // 2 - 1) as i2:
                ssd_iter(i2 * 2 + 1, 1, True)
                ssd_iter(i2 * 2 + 2, 0, True)
            ssd_iter(NG - 1, 1, False)
            nc.tensor.drain().then_inc(pe_phase, 2)

            pe.wait_ge(freed[0], O[0]["yo"])
            for j in range(2):
                pe.wait_ge(w_lo_done, W["yo"] + j + 1)
                for k in range(8):
                    pe.wait_ge(s_ylo, 8 * j + k + 1)
                    for t in range(2):
                        cols = slice(512 * t, 512 * t + 512)
                        ins = passes(psG[:, 0, t, :], j, k, y_hi[:, 8 * j + k, cols], y_lo[:, 8 * j + k, cols],
                                     j == 0 and k == 0, j == 1 and k == 7)
                ins.then_inc(w_used, 1)
                if j == 0:
                    past(pe, s_yacc, NG * 2 + 1)
                    token_sums(y_acc)
            spread(3, y_rstd)

            def y_out(n, b, m):
                product(n, 0, b, m, y_hi, y_lo, 8, 0, True, False)
                product(n + 1, 1, b, m, y_hi, y_lo, 8, 8, False, True)

            y_out(W["yo"] + 2, 1, O[1]["yo"])
            with pe.Fori(1, 4) as i:
                y_out(W["yo"] + i * 4, 0, O[0]["yo"] + i)
                y_out(W["yo"] + 2 + i * 4, 1, O[1]["yo"] + i)

            def merged_ready(k):
                pe.wait_ge(s_mlo[k % 2], k // 2 + 1)
            for j in range(2):
                product(W["mix"] + j, j, j, O[j]["mix"], m_hi, m_lo, 8, ready=merged_ready if j == 0 else None)
            with pe.Fori(1, 4) as i:
                for j in range(2):
                    product(W["mix"] + i * 2 + j, j, j, O[j]["mix"] + i, m_hi, m_lo, 8)
            norm_sum(2, 4)
            ffn(1, 2)

            pe.wait_ge(s_xw, 8)
            for t in range(NT):
                if t == 3:
                    pe.wait_ge(s_acc, 8 * 4)
                    token_sums(acc)
                for u in range(2):
                    at_least(pe, s_orow[u], t - 2)
                    for j in range(4):
                        ins = transpose(final_bank(t, u)[:, j * P:(j + 1) * P], x_w[:, 4 * u + j, t * P:(t + 1) * P])
                    ins.then_inc(s_ftr, 1)

        @block.scalar
        def _(act):
            ch = Chain(act, c_act_sem)
            for s in (s_exp, s_pta, s_ohi, s_conv_act, s_dec_exp, s_ecs, s_btok, s_ysq, s_yout):
                act.sem_inc(s, CREDIT)
            fn = nc.scalar.activation

            def split_at(base, i, rate, j):
                n = i * rate + base
                assert base % 2 == j and rate % 2 == 0
                act.wait_ge(w_loaded[j], i * (8 * rate) + 16 * (base // 2 + 1))
                at_least(act, w_used, n - 1)
                fn(w_hi[:, j], w_raw[:, j], ACT.Copy).then_inc(w_hi_done, 1)

            def norm_apply(idx, scale, shift, h_free):
                for d in range(8):
                    act.wait_ge(s_xr, 8 * idx + d + 1)
                    if d == 0 and h_free:
                        act.wait_ge(w_used, h_free)
                    shift_d = mod[:, shift + d:shift + d + 1]
                    if d % 2 == 0:
                        fn(h_hi[:, d], xs[:, d % 4], ACT.Identity, bias=shift_d).then_inc(s_hhi, 1)
                    else:
                        ch.link(fn(xs[:, d % 4], xs[:, d % 4], ACT.Identity, bias=shift_d))
                        fn(h_hi[:, d], xs[:, d % 4], ACT.Copy).then_inc(s_hhi, 1)

            def root(n, width):
                act.wait_ge(s_ms, n)
                fn(rcol[:], psT[:, 0:NT], ACT.Sqrt, scale=1.0 / width, bias=eps_col).then_inc(s_rt, 1)

            def square(count, src, j, xt_sem, xt_value):
                act.wait_ge(xt_sem, xt_value)
                at_least(act, s_acc, count - 1)
                fn(sq[:, j], src, ACT.Square).then_inc(s_sq, 1)

            def ffn(x, idx):
                for p, (f0, cnt) in enumerate(PARTS):
                    s = f"gu{x}{p}"
                    n0 = W[s]
                    F0 = FT * x + f0
                    U0 = O[1][s]

                    def body(i):
                        split_at(n0 + 2, i, 2, 0)
                        act.wait_ge(w_used, i * 2 + n0 + 1)
                        at_least(act, freed[1], i + U0)
                        fn(tmp[:, 0], psG[:, 0].rearrange("p a b -> p (a b)"), ACT.Silu).then_inc(freed[0], 1)
                        split_at(n0 + 3, i, 2, 1)
                        act.wait_ge(freed[1], i + U0 + 1)
                        if p:
                            act.wait_ge(w_used, n0)
                        fn(hid_hi[:, bass.ds(i, 1), :].rearrange("p o t -> p (o t)"), tmp[:, 1], ACT.Copy).then_inc(s_hid_hi, 1)
                    if p == 0:
                        body(0)
                        with ch.loop(1, cnt, 0) as i:
                            body(i)
                    else:
                        with ch.loop(0, cnt, 0) as i:
                            body(i)
                    if x == 0 and p >= 2:
                        act.wait_ge(s_ang, p - 1)
                        fn((sin_w, cos_w)[p - 2][:], rt2[:], ACT.Sin).then_inc(s_trig, 1)
                    s = f"dn{x}{p}"
                    n1 = W[s]

                    def down(i, tail=False):
                        for j in range(2):
                            if not tail:
                                split_at(n1 + 2 + j, i, 2, j)
                            if p == 3:
                                d = i * 2 + j
                                src = xT[:, bass.ds(d, 1), :].rearrange("p o t -> p (o t)")
                                square(d + 8 * (idx + 1), src, j, freed[j], O[j][s] + i + 1)
                    last = x == 1 and p == 3
                    with ch.loop(0, 3 if last else 4, 0) as i:
                        down(i)
                    if last:
                        down(3, True)

            act.wait_ge(s_par, 1)
            fn(c_act, par[:, R_C:R_C + 8], ACT.Silu).then_inc(s_cact, 1)
            for t in range(NT):
                for u in range(2):
                    act.wait_ge(s_xtr, 2 * t + u + 1)
                    fn(xT[:, 4 * u:4 * u + 4, t * P:(t + 1) * P], psS[:, u].rearrange("p (j t) -> p j t", j=4),
                       ACT.Copy).then_inc(s_xt, 1)
            for d in range(8):
                square(d, xT[:, d], d % 2, s_xt, 2 * NT)
            act.wait_ge(s_eps, 1)
            root(1, D)
            split_at(0, 0, 2, 0)
            split_at(1, 0, 2, 1)
            act.wait_ge(s_first_cols, 1)
            norm_apply(0, scale1, SH1, 0)
            ffn(0, 0)
            root(2, D)
            act.wait_ge(s_first_cols, 2)
            norm_apply(1, scale2, SH2, W["dn03"])

            split_at(W["dt"] + 2, 0, 2, 0)
            split_at(W["dt"] + 3, 0, 2, 1)
            act.wait_ge(s_dt_e, 1)
            ch.link(fn(dt_w[2][0:SH], dt_w[1][0:SH], ACT.Exp, scale=-1.0))
            ch.link(fn(head_col[:, 2:3], head_col[:, 1:2], ACT.Exp))
            fn(dt_w[3][0:SH], dt_w[2][0:SH], ACT.Ln, bias=1.0).then_inc(s_dt_ln, 1)
            act.wait_ge(s_dt_cs, 1)
            for t in range(NT):
                ins = fn(dteT[0:SH, t * P:(t + 1) * P], csT[0:SH, t * P:(t + 1) * P], ACT.Exp, scale=-1.0,
                         bias=csT[0:SH, (t + 1) * P - 1:(t + 1) * P])
            ins.then_inc(s_dt_dte, 1)
            ch.link(fn(dec_head, csT[0:SH, P - 1:T:P], ACT.Exp))
            act.dma_start(cs_keep, csT[0:SH]).then_inc(s_cs_kept, 16)
            act.dma_start(dec_keep, dec_head).then_inc(s_dec_kept, 16)
            def keep_gate(d, dst):
                b = d % 2
                at_least(act, s_gt_out[b], 16 * (d // 2))
                fn(dst, psG[:, b].rearrange("p a b -> p (a b)"), ACT.Copy).then_inc(freed[b], 1)
                m = O[b]["gba"] + d // 2 if d < 4 else O[b]["ssd"] + (NG - 1) * 3 + (d - 4) // 2
                act.wait_ge(freed[b], m + 1)
                act.dma_start(gate_keep[d], dst).then_inc(s_gt_out[b], 16)

            def att_done(i, e):
                if e[0] == "gate" and e[2:] == (7, 1):
                    j = e[1]
                    act.wait_ge(w_used, W["gba"] + j + 1)
                    if j == 0:
                        past(act, s_vtok, PAIRS)
                    keep_gate(j, (q_st, k_st)[j % 2][:])
                    split_at(W["gba"] + 2 + j, 0, 2, j % 2)
                if e[0] != "half" or e[3] == 0:
                    return
                j, k = e[1], e[2]
                if k != (7, 7, 3, 7)[j]:
                    return
                n = W["att"] + j
                act.wait_ge(w_used, i * 4 + n + 1)
                if j == 0:
                    past(act, s_vtok, i)
                    fn(q_st[:], psG[:, 0].rearrange("p a b -> p (a b)"), ACT.Copy, scale=-(HD ** -0.5)).then_inc(freed[0], 1)
                if j == 1:
                    past(act, s_roped, i * 2)
                    fn(k_st[:], psG[:, 1].rearrange("p a b -> p (a b)"), ACT.Copy).then_inc(freed[1], 1)
                if j == 3:
                    past(act, s_roped, i * 2 + 1)
                    fn(v_st[:], psG[:, 0].rearrange("p a b -> p (a b)"), ACT.Copy).then_inc(freed[0], 1)
                split_at(n + 2, i, 4, j % 2)

            def att_iter(i, par_, att, gemm):
                S = i * NA
                for s in range(NA + 2):
                    r = s - 1
                    if att and 0 <= r < NA:
                        q, h = ASTEPS[r]
                        past(act, s_tr, i * AGROUP0[NA] + AGROUP0[r] + 1)
                        past(act, s_pv, i * NT + q)
                        w = min(q + 1, 4) * P
                        fn(probT[:, r % 2, 0:w], psT[:, 0:w], ACT.Copy).then_inc(s_pta, 1)
                    if att and s < NA:
                        q, h = ASTEPS[s]
                        past(act, s_masked, S + s + 1)
                        past(act, s_dd, S + s - 3)
                        fn(prob[:, s % 2, 0:(q + 1) * P], prob[:, s % 2, 0:(q + 1) * P], ACT.Exp, scale=-1.0,
                           bias=negmax[:, s % 2:s % 2 + 1], accum_out=den[:, s % 4:s % 4 + 1]).then_inc(s_exp, 1)
                    for e in step_events(s, gemm):
                        att_done(i + 1, e)
                    r = s - 2
                    if att and 0 <= r < NA and r % 2 == 1:
                        q = ASTEPS[r][0]
                        past(act, s_o, i * NT + q + 1)
                        dst = o_hi[:, bass.ds(i, 1), q * P:(q + 1) * P].rearrange("p o t -> p (o t)")
                        fn(dst, o_T[:], ACT.Copy).then_inc(s_ohi, 1)

            att_iter(-1, 0, False, True)
            act.wait_ge(s_cs_kept, 16)
            act.wait_ge(s_dec_kept, 16)
            act.dma_start(dec_b[:], dec_keep.rearrange("h t -> (h t)")[None, :].to_broadcast([P, SH * NT])
                          .rearrange("p (h t) -> p h t", t=NT)).then_inc(s_dec, 16)
            with ch.loop(0, PAIRS // 2 - 1, 0) as i2:
                att_iter(i2 * 2, 0, True, True)
                att_iter(i2 * 2 + 1, 1, True, True)
            att_iter(PAIRS - 2, 0, True, True)
            att_iter(PAIRS - 1, 1, True, False)
            nc.scalar.drain().then_inc(act_phase, 1)

            with ch.loop(0, 8, 0) as i:
                split_at(W["ga"] + 2, i, 2, 0)
                act.wait_ge(w_used, i * 2 + W["ga"] + 1)
                act.wait_ge(freed[1], i + O[1]["ga"])
                fn(tmp[:, 0], psG[:, 0].rearrange("p a b -> p (a b)"), ACT.Sigmoid).then_inc(freed[0], 1)
                split_at(W["ga"] + 3, i, 2, 1)
                act.wait_ge(freed[1], i + O[1]["ga"] + 1)
                act.dma_start(merged_keep[bass.ds(i, 1)].rearrange("o p t -> (o p) t"), tmp[:, 1]).then_inc(s_mg_out, 16)
            act.wait_ge(s_mg_out, 16 * 8)

            def load_cs(g, c):
                src = cs_keep.rearrange("(g e) (c l) -> g c e l", e=GH, l=P)[bass.ds(g, 1), c]
                act.dma_start(cs_b[:, c], src.to_broadcast([P, GH, P])).then_inc(s_csb[c], 16)

            def conv_out(base, i, rate, j, C):
                n = i * rate + base
                act.wait_ge(w_used, n + 1)
                past(act, s_conv, C - 1)
                fn(conv_in[:, j % 2, 4:4 + T], psG[:, j % 2].rearrange("p a b -> p (a b)"), ACT.Copy).then_inc(freed[j % 2], 1)

            def conv_act(i, p, j):
                past(act, s_conv, i * 4 + j + 1)
                t = conv_tile(i, j)
                ins = fn(xbc[:, p, j], xbc[:, p, j], ACT.Silu, bias=par[:, bass.ds(t + R_CB, 1)])
                ins.then_inc(s_conv_act, 1)

            def conv_tile(i, j):
                return (i * 2 + j) if j < 2 else i + (16 if j == 2 else 24)

            act.wait_ge(dve_phase, 1)
            act.wait_ge(pool_phase, 1)
            for c in range(NT):
                load_cs(0, c)
            for j in range(4):
                split_at(W["ssdx"] + 2 + j, 0, 2, j % 2)
                conv_out(W["ssdx"] + j, 0, 2, j, j)
                if j:
                    conv_act(0, 0, j - 1)
            conv_act(0, 0, 3)

            def refill_cs(i, c):
                past(act, s_arg, i * NT + c + 1)
                past(act, s_ecs, i * NT + c + 1)
                load_cs(i + 1, c)

            def ssd_prepare(i, p, c, refill=True):
                n = i * NT + c
                past(act, s_tokT, n + 1)
                past(act, s_st, i * (NT - 1) + max(c - 1, 0))
                fn(b_tok[:, c % 2], psT[:, 2 * P:3 * P], ACT.Copy).then_inc(s_btok, 1)
                act.wait_ge(s_csb[c], i * 16 + 16)
                past(act, s_cscaled, n - 1)
                fn(ecs[:, c % 2], cs_b[:, c], ACT.Exp).then_inc(s_ecs, 1)
                past(act, s_arg, n + 1)
                fn(decay[:, c % 2], decay[:, c % 2], ACT.Exp).then_inc(s_dec_exp, 1)
                if refill:
                    refill_cs(i, c)

            def y_split(k):
                act.wait_ge(w_used, W["yo"])
                act.wait_ge(s_yin[k // 2], 16)
                fn(y_hi[:, k], y_raw[:, k], ACT.Copy, scale=par[:, R_SN + k:R_SN + k + 1]).then_inc(s_yhi, 1)

            def finish(i, p):
                past(act, s_gated, i * 2 + 2)
                act.dma_start(y_keep[bass.ds(i, 1)].rearrange("o p u t -> (o p) u t"), xbc[:, p, 0:2]).then_inc(s_yout, 16)
                for j in range(2):
                    past(act, s_yacc, i * 2 + j + 1)
                    fn(y_sq[:], xbc[:, p, j], ACT.Square).then_inc(s_ysq, 1)

            def ssd_iter(i, p, gemm):
                n0 = W["ssd"]

                def done(j):
                    base = n0 + j
                    split_at(base + 2, i, 6, j % 2)
                    act.wait_ge(w_used, i * 6 + base + 1)
                    if j < 4 and not gemm:
                        keep_gate(4 + j, tmp[:, j % 2])
                        return
                    if j == 0:
                        past(act, s_yout, i * 16)
                    if j < 4:
                        conv_out(base, i, 6, j, i * 4 + 4 + j)
                    else:
                        past(act, s_gated, i * 2 + j - 5)
                        fn(z_sil[:, j - 4], psG[:, j % 2].rearrange("p a b -> p (a b)"), ACT.Silu).then_inc(freed[j % 2], 1)

                for c in range(NT):
                    if gemm and c == 0:
                        refill_cs(i, 0)
                    if gemm or c < NT - 1:
                        ssd_prepare(*following(i, p, c), refill=gemm and c < NT - 1)
                    if c == 0 and not (isinstance(i, int) and i == 0):
                        finish(i - 1, 1 - p)
                    for j in range(6):
                        if (8 * j + 7) // 6 == c:
                            done(j)
                        if gemm and j < 4 and CONV_AT[j] == c - 1:
                            conv_act(i + 1, 1 - p, j)
            ssd_prepare(0, 0, 0, refill=False)
            ssd_iter(0, 0, True)
            with ch.loop(0, NG // 2 - 1, 0) as i2:
                ssd_iter(i2 * 2 + 1, 1, True)
                ssd_iter(i2 * 2 + 2, 0, True)
            ssd_iter(NG - 1, 1, False)
            y_split(0)
            y_split(1)
            finish(NG - 1, 1)
            nc.scalar.drain().then_inc(act_phase, 1)

            for k in range(2, 16):
                y_split(k)
            root(3, INNER)
            with ch.loop(0, 8, 0) as i:
                split_at(W["yo"] + 2, i, 2, 0)
                act.wait_ge(s_gt_in, i * 16 + 16)
                fn(gate[:], gate[:], ACT.Sigmoid).then_inc(s_gate, 1)
                split_at(W["yo"] + 3, i, 2, 1)
            for d in range(8):
                act.wait_ge(s_mg, d + 1)
                if d == 0:
                    act.wait_ge(w_used, W["mix"])
                fn(m_hi[:, d], merged[:, d], ACT.Copy).then_inc(s_mhi, 1)
            with ch.loop(0, 4, 0) as i:
                for j in range(2):
                    split_at(W["mix"] + 2 + j, i, 2, j)
                    d = i * 2 + j
                    src = xT[:, bass.ds(d, 1), :].rearrange("p o t -> p (o t)")
                    square(d + 16, src, j, freed[j], O[j]["mix"] + i + 1)
            root(4, D)
            norm_apply(2, scale3, SH3, W["gu10"])
            ffn(1, 2)
            root(5, D)
            act.wait_ge(s_rinv, 1)
            for t in range(NT):
                act.wait_ge(s_ftr, 2 * t + 2)
                fn(o_row[:, t, 512:D], final_bank(t, 1), ACT.Copy, scale=rcol[:, t:t + 1]).then_inc(s_orow[1], 1)

        @block.vector
        def _(dve):
            ch = Chain(dve, c_dve_sem)
            for s in (s_masked, s_ptb, s_dd, s_o, s_olo, s_vtok, s_conv, s_arg, s_xdte, s_wT, s_state, s_yev, s_gated):
                dve.sem_inc(s, CREDIT)
            v = nc.vector

            def flat(ps):
                return ps.rearrange("p a b -> p (a b)")

            def ada_reduce(q, src):
                dve.wait_ge(s_ada_mul, q - ADA_FIRST + 1)
                at_least(dve, s_ada_mm, q)
                v.tensor_reduce(ada_red[:], src.rearrange("p k m -> p m k"), AXX, ALU.add).then_inc(s_ada_red, 1)

            def ada_finish(q):
                dve.wait_ge(s_ada_mm, q + 1)
                if isinstance(q, int):
                    cols = slice(4 * q, 4 * q + 4)
                else:
                    cols = bass.ds(q * 4, 4)
                v.tensor_tensor(mod[:, cols], psO[:, 0:4], par[:, cols], ALU.add).then_inc(s_ada_done, 1)

            def diagonal(n, dst):
                dve.wait_ge(s_rt, n)
                ch.link(v.reciprocal(rcol[:], rcol[:]))
                v.tensor_tensor(dst.rearrange("p (t c) -> p t c", t=NT), ident.unsqueeze(1).to_broadcast([P, NT, P]),
                                rcol[:].unsqueeze(2).to_broadcast([P, NT, P]), ALU.mult).then_inc(s_diag, 1)

            def norm_apply(idx, n, scale, shift):
                dve.wait_ge(s_spread, n)

                def lo(d):
                    dve.wait_ge(s_hhi, 8 * idx + d + 1)
                    v.scalar_tensor_tensor(h_lo[:, d], xs[:, d % 4], mod[:, shift + d:shift + d + 1],
                                           h_hi[:, d].bitcast(F32), ALU.add, ALU.subtract).then_inc(s_hlo[0], 1)
                for d in range(8):
                    if d >= 4:
                        dve.wait_ge(s_hlo[d % 2], 4 * idx + (d - 4) // 2 + 1)
                    v.scalar_tensor_tensor(xs[:, d % 4], xT[:, d], scale[:, d:d + 1], flat(psS[:]),
                                           ALU.mult, ALU.mult).then_inc(s_xr, 1)
                    if d % 2:
                        lo(d - 1)

            def angles(u):
                two_pi = 2.0 * np.pi
                c1 = 6.28125
                c2 = float(np.float32(np.round((two_pi - c1) * 2 ** 19) / 2 ** 19))
                c3 = float(np.float32(two_pi - c1 - c2))
                magic = 1.5 * 2 ** 23
                turn, shift = ((0.0, 0.0), (0.25, float(np.pi / 2)))[u]
                if u == 0:
                    dve.wait_ge(s_pos, 16)
                    ch.link(v.tensor_copy(rt1[:], pos_i[:]))
                    ch.link(v.tensor_scalar(ang[:], rt1[:], invf, None, ALU.mult))
                ch.link(v.tensor_scalar(rt1[:], ang[:], float(1 / two_pi), turn, ALU.mult, ALU.add))
                ch.link(v.tensor_scalar(rt1[:], rt1[:], magic, None, ALU.add))
                ch.link(v.tensor_scalar(rt1[:], rt1[:], magic, None, ALU.subtract))
                if u:
                    dve.wait_ge(s_trig, 1)
                ch.link(v.scalar_tensor_tensor(rt2[:], rt1[:], -c1, ang[:], ALU.mult, ALU.add))
                ch.link(v.scalar_tensor_tensor(rt2[:], rt1[:], -c2, rt2[:], ALU.mult, ALU.add))
                ch.link(v.scalar_tensor_tensor(rt2[:], rt1[:], -c3, rt2[:], ALU.mult, ALU.add))
                ch.link(v.tensor_scalar(rt2[:], rt2[:], shift, None, ALU.add))
                v.tensor_scalar(rt2[:], rt2[:], 3.1415925, -3.1415925, ALU.min, ALU.max).then_inc(s_ang, 1)

            def ffn(x):
                for p, (f0, cnt) in enumerate(PARTS):
                    s = f"gu{x}{p}"
                    n0, G0, U0, F0 = W[s], O[0][s], O[1][s], FT * x + f0
                    if x == 0 and p >= 2:
                        angles(p - 2)

                    def body(i):
                        if x == 0 and p < 2:
                            if not (isinstance(i, int) and i + f0 == 0):
                                ada_finish(i + (f0 + ADA_FIRST - 1))
                            ada_reduce(i + (f0 + ADA_FIRST), ada[:])
                        dve.wait_ge(freed[0], i + G0 + 1)
                        dve.wait_ge(w_used, i * 2 + n0 + 2)
                        at_least(dve, s_hid_lo, i + F0)
                        v.tensor_tensor(tmp[:, 1], tmp[:, 0], flat(psG[:, 1]), ALU.mult).then_inc(freed[1], 1)
                    if p == 0:
                        body(0)
                        with ch.loop(1, cnt, 0) as i:
                            body(i)
                    else:
                        with ch.loop(0, cnt, 0) as i:
                            body(i)
                    if x == 0 and p == 0:
                        dve.wait_ge(s_ada_done, G1 // 4 + 2)
                        v.tensor_scalar(gate1, mod[:, G1:G1 + 8], 0.5, None, ALU.mult).then_inc(s_g1, 1)
                        dve.wait_ge(s_g1, 1)
                    if x == 0 and p == 1:
                        ada_finish(ADA_ALL - 1)
                        dve.wait_ge(s_ada_done, ADA_ALL)
                        ch.link(v.tensor_scalar(gate3, mod[:, G3:G3 + 8], 0.5, None, ALU.mult))
                        ch.link(v.scalar_tensor_tensor(scale3, mod[:, SC3:SC3 + 8], 1.0, par[:, R_N3:R_N3 + 8], ALU.add, ALU.mult))
                        v.scalar_tensor_tensor(scale2, mod[:, SC2:SC2 + 8], 1.0, par[:, R_N2:R_N2 + 8],
                                               ALU.add, ALU.mult).then_inc(s_first_cols, 1)
                    s = f"dn{x}{p}"
                    n1 = W[s]
                    g = gate1 if x == 0 else gate3
                    with ch.loop(0, 4, 0) as i:
                        for j in range(2):
                            d = i * 2 + j
                            dve.wait_ge(w_used, d + n1 + 1)
                            xd = xT[:, bass.ds(d, 1), :].rearrange("p o t -> p (o t)")
                            v.scalar_tensor_tensor(xd, flat(psG[:, j]), g[:, bass.ds(d, 1)], xd,
                                                   ALU.mult, ALU.add).then_inc(freed[j], 1)
                            if x == 1 and p == 3:
                                dve.wait_ge(freed[j], i + O[j][s] + 1)
                                v.tensor_scalar(x_w[:, bass.ds(d, 1), :].rearrange("p o t -> p (o t)"), xd,
                                                par[:, bass.ds(d + R_FN, 1)], None, ALU.mult).then_inc(s_xw, 1)

            v.memset(eps_col, EPS).then_inc(s_eps, 1)
            dve.wait_ge(s_par_ps, 1)
            v.tensor_copy(par[:], psT[:, 0:R_ALL]).then_inc(s_par, 1)
            for q in range(ADA_FIRST):
                if q == ADA_FIRST - 1:
                    diagonal(1, rstd[:])
                dve.wait_ge(s_row, q + 1)
                v.tensor_copy(mod_row[0:1, q], psG[0:1, q // 2, q % 2, :]).then_inc(s_row_out, 1)
            cols = 4 * ADA_FIRST
            dve.wait_ge(s_ada_mm, ADA_FIRST)
            v.tensor_tensor(mod[:, 0:cols], psO[:, 0:cols], par[:, 0:cols], ALU.add).then_inc(s_ada_done, ADA_FIRST)
            dve.wait_ge(s_ada_done, ADA_FIRST)
            v.scalar_tensor_tensor(scale1, mod[:, SC1:SC1 + 8], 1.0, par[:, R_N1:R_N1 + 8],
                                   ALU.add, ALU.mult).then_inc(s_first_cols, 1)
            dve.wait_ge(s_first_cols, 1)
            norm_apply(0, 1, scale1, SH1)
            ffn(0)
            diagonal(2, rstd[:])
            norm_apply(1, 2, scale2, SH2)

            dve.wait_ge(s_small, 16 * 3)
            for j in range(2):
                rows = slice(HD * j, HD * j + HD)
                ch.link(v.tensor_copy(d_col[rows], d_row[rows].rearrange("p (a b) -> p b a", b=2)[:, j]))
            dve.wait_ge(w_used, W["dt"] + 2)
            ch.link(v.tensor_scalar(dt_w[0][0:SH], flat(psG[0:SH, 0]), head_col[:, 0:1], None, ALU.add))
            dve.sem_inc(freed[0], 1)
            v.scalar_tensor_tensor(dt_w[1][0:SH], dt_w[0][0:SH], -1.0, dt_w[0][0:SH], ALU.mult, ALU.max).then_inc(s_dt_e, 1)
            dve.wait_ge(s_dt_ln, 1)
            ch.link(v.scalar_tensor_tensor(dtT[0:SH], dt_w[0][0:SH], 0.0, dt_w[3][0:SH], ALU.max, ALU.add))
            ch.link(v.tensor_scalar(dt_w[1][0:SH], dtT[0:SH], head_col[:, 2:3], -1.0, ALU.mult, ALU.mult))
            ch.link(v.memset(dt_w[2][0:SH], 1.0))
            for t in range(NT):
                tok = slice(t * P, (t + 1) * P)
                ins = v.tensor_tensor_scan(csT[0:SH, tok], dt_w[2][0:SH, tok], dt_w[1][0:SH, tok], 0.0, ALU.mult, ALU.add)
            ins.then_inc(s_dt_cs, 1)
            dve.wait_ge(s_dt_dte, 1)
            v.tensor_tensor(dteT[0:SH], dteT[0:SH], dtT[0:SH], ALU.mult).then_inc(s_dt_ready, 1)

            def v_out(i, par_):
                past(dve, s_vtr, i + 1)
                v.tensor_copy(v_tok[:, par_].rearrange("p a b -> p (a b)"), flat(psG[:, 1])).then_inc(s_vtok, 1)
                past(dve, s_vtok, i + 1)
                dve.sem_inc(freed[1], 1)

            def att_done(i, par_, e):
                if e[0] != "rot":
                    return
                b = e[1]
                src = (q_st, k_st)[b]
                past(dve, s_rot, i * 2 + b + 1)
                past(dve, s_cosed, i * 2 + b + 1)
                v.tensor_tensor(src[:], flat(psG[:, b]), sinT[:], ALU.mult).then_inc(freed[b], 1)

            def att_iter(i, par_, att, gemm):
                S = i * NA
                for s in range(NA + 2):
                    if att and s < NA:
                        q, h = ASTEPS[s]
                        w = (q + 1) * P
                        past(dve, s_qk, S + s + 1)
                        past(dve, s_tr, i * AGROUP0[NA] + (AGROUP0[s - 1] if s else -AGROUPS[NA - 1]))
                        dve.sem_inc(dve_turn, 1)
                        v.tensor_tensor_reduce(out=prob[:, s % 2, 0:w], in0=flat(psS)[:, 0:w], in1=mask[:, T - w:T],
                                               scale=1.0, scalar=3.0e38, op0=ALU.add, op1=ALU.min,
                                               accum_out=negmax[:, s % 2:s % 2 + 1]).then_inc(s_masked, 1)
                    if att and s == 1:
                        v_out(i, par_)
                    r = s - 1
                    if att and 0 <= r < NA:
                        q, h = ASTEPS[r]
                        past(dve, s_exp, S + r + 1)
                        ch.link(v.reciprocal(rden[:, h:h + 1], den[:, r % 4:r % 4 + 1]))
                        past(dve, s_pv, i * NT + q)
                        v.tensor_scalar(den_diag[:, h, :], ident, rden[:, h:h + 1], None, ALU.mult).then_inc(s_dd, 1)
                    r = s - 2
                    if att and 0 <= r < NA and r % 2 == 1:
                        q = ASTEPS[r][0]
                        past(dve, s_pv, i * NT + q + 1)
                        past(dve, s_olo, i * NT + q)
                        ch.link(v.tensor_copy(o_T[:], psO[:, P:2 * P]))
                        v.tensor_tensor(o_T[:], o_T[:], psO[:, 0:P], ALU.mult).then_inc(s_o, 1)
                    r = s - 1
                    if att and 0 <= r < NA and ASTEPS[r][0] >= 4:
                        q, h = ASTEPS[r]
                        past(dve, s_tr, i * AGROUP0[NA] + AGROUP0[r] + 2)
                        past(dve, s_pv, i * NT + q)
                        v.tensor_copy(probT[:, r % 2, 512:(q + 1) * P], psT[:, 0:(q - 3) * P]).then_inc(s_ptb, 1)
                    for e in step_events(s, gemm):
                        att_done(i + 1, 1 - par_, e)
                    r = s - 2
                    if att and 0 <= r < NA and r % 2 == 1:
                        q = ASTEPS[r][0]
                        past(dve, s_ohi, i * NT + q + 1)
                        tok = slice(q * P, (q + 1) * P)
                        hi = o_hi[:, bass.ds(i, 1), tok].rearrange("p o t -> p (o t)").bitcast(F32)
                        lo = o_lo[:, bass.ds(i, 1), tok].rearrange("p o t -> p (o t)")
                        v.tensor_tensor(lo, o_T[:], hi, ALU.subtract).then_inc(s_olo, 1)

            dve.wait_ge(s_trig_in, 16 * 2)
            att_iter(-1, 1, False, True)
            dve.wait_ge(s_dt_tr, 1)
            dve.wait_ge(s_mask, 16)
            ch.link(v.tensor_copy(cs_tok[:].rearrange("p a b -> p (a b)"), psS[:, 0, 0:256]))
            ch.link(v.tensor_copy(dt_keep[:], psS[:, 0, 256:512]))
            v.tensor_copy(dte_tok[:].rearrange("p a b -> p (a b)"), psS[:, 1, 0:256]).then_inc(s_dt_tok, 1)
            dve.wait_ge(s_dt_tok, 1)
            with ch.loop(0, PAIRS // 2 - 1, 2 * (NA + NT)) as i2:
                att_iter(i2 * 2, 0, True, True)
                att_iter(i2 * 2 + 1, 1, True, True)
            att_iter(PAIRS - 2, 0, True, True)
            att_iter(PAIRS - 1, 1, True, False)
            past(dve, s_olo, PAIRS * NT)
            nc.vector.drain().then_inc(dve_phase, 1)

            def ga(i, first):
                dve.wait_ge(freed[0], i + O[0]["ga"] + 1)
                dve.wait_ge(w_used, i * 2 + W["ga"] + 2)
                if not first:
                    dve.wait_ge(s_mg_out, i * 16)
                v.tensor_tensor(tmp[:, 1], tmp[:, 0], flat(psG[:, 1]), ALU.mult).then_inc(freed[1], 1)
            dve.wait_ge(act_phase, 1)
            ga(0, True)
            with ch.loop(1, 8, 0) as i:
                ga(i, False)

            def conv(i, p, j, n):
                C = i * 4 + j
                dve.wait_ge(freed[j % 2], n)
                t = (i * 2 + j) if j < 2 else i + (16 if j == 2 else 24)
                for u in range(4):
                    tap = par[:, bass.ds(t + (R_CW + 32 * (3 - u)), 1)]
                    src = conv_in[:, j % 2, 4 - u:4 - u + T]
                    if u == 0:
                        ch.link(v.tensor_scalar(xbc[:, p, j], src, tap, None, ALU.mult))
                    else:
                        ins = v.scalar_tensor_tensor(xbc[:, p, j], src, tap, xbc[:, p, j], ALU.mult, ALU.add)
                        if u < 3:
                            ch.link(ins)
                ins.then_inc(s_conv, 1)

            dve.wait_ge(w_used, W["ssdx"])
            dve.wait_ge(s_dec, 16)
            for j in range(2):
                dve.wait_ge(s_gt_out[j], 16 * 2)
            ch.link(v.tensor_copy(dt_tok[:].rearrange("p a b -> p (a b)"), dt_keep[:]))
            for j in range(2):
                ch.link(v.memset(conv_in[:, j, 0:4], 0.0))
            for j in range(4):
                conv(0, 0, j, O[j % 2]["ssdx"] + j // 2 + 1)

            def ssd_arg(i, p, c):
                n = i * NT + c
                dve.wait_ge(s_csb[c], i * 16 + 16)
                past(dve, s_wT, n - 1)
                for e in range(GH):
                    ins = v.scalar_tensor_tensor(decay[:, c % 2, e], cs_b[:, c, e], cs_tok[:, c, bass.ds(i * GH + e, 1)],
                                                 causal, ALU.subtract, ALU.add)
                ins.then_inc(s_arg, 1)

            def ssd_weigh(i, p, c):
                n = i * NT + c
                heads = bass.ds(i * GH, GH)
                past(dve, s_tokT, n + 1)
                past(dve, s_btok, n + 1)
                past(dve, s_y, n - 1)
                past(dve, s_st, i * (NT - 1) + max(c - 1, 0))
                xt = psT[:, 0:2 * P].rearrange("p (e d) -> p e d", e=GH)
                v.tensor_tensor(xdt[:, c % 2].rearrange("p (e d) -> p e d", e=GH), xt,
                                dt_tok[:, c, heads].unsqueeze(2).to_broadcast([P, GH, HD]), ALU.mult)
                v.tensor_tensor(xdte[:, c % 2].rearrange("p (e d) -> p e d", e=GH), xt,
                                dte_tok[:, c, heads].unsqueeze(2).to_broadcast([P, GH, HD]), ALU.mult).then_inc(s_xdte, 1)
                past(dve, s_dec_exp, n + 1)
                past(dve, s_cb, n + 1)
                v.tensor_tensor(wT[:, c % 2], decay[:, c % 2],
                                psS[:, 0, 0:P].unsqueeze(1).to_broadcast([P, GH, P]), ALU.mult).then_inc(s_wT, 1)

            def finish(i, p):
                past(dve, s_yev, i * NT + NT)
                for j in range(2):
                    dve.wait_ge(freed[j], i * 3 + O[j]["ssd"] + 3)
                    v.tensor_tensor(xbc[:, p, j], xbc[:, p, j], z_sil[:, j], ALU.mult).then_inc(s_gated, 1)

            def ssd_iter(i, p, gemm):
                blocks = range(4) if gemm else ()
                for c in range(NT):
                    n = i * NT + c
                    heads = bass.ds(i * GH, GH)
                    more = gemm or c < NT - 1
                    if more:
                        ssd_arg(*following(i, p, c))
                    past(dve, s_y, n + 1)
                    for j in range(2):
                        tok = slice(c * P, (c + 1) * P)
                        ins = v.scalar_tensor_tensor(xbc[:, p, j, tok], xbc[:, p, j, tok], d_col[:, bass.ds(i * 2 + j, 1)],
                                                     psS[:, 1, j * P:(j + 1) * P], ALU.mult, ALU.add)
                    ins.then_inc(s_yev, 1)
                    if c < NT - 1:
                        past(dve, s_st, i * (NT - 1) + c + 1)
                        if c == 0:
                            v.tensor_copy(state[:, 0], psO[:, 0:2 * P]).then_inc(s_state, 1)
                        else:
                            dcol = dec_b[:, heads, c:c + 1].to_broadcast([P, GH, HD])
                            cur = state[:, c % 2].rearrange("p (e d) -> p e d", e=GH)
                            old = state[:, (c - 1) % 2].rearrange("p (e d) -> p e d", e=GH)
                            ch.link(v.tensor_tensor(cur, old, dcol, ALU.mult))
                            v.tensor_tensor(state[:, c % 2], state[:, c % 2], psO[:, 0:2 * P], ALU.add).then_inc(s_state, 1)
                        past(dve, s_state, i * (NT - 1) + c + 1)
                    if more:
                        ssd_weigh(*following(i, p, c))
                    if c == 0 and not (isinstance(i, int) and i == 0):
                        finish(i - 1, 1 - p)
                    for j in blocks:
                        if CONV_AT[j] == c:
                            conv(i + 1, 1 - p, j, i * 3 + O[j % 2]["ssd"] + j // 2 + 1)
            ssd_arg(0, 0, 0)
            ssd_weigh(0, 0, 0)
            ssd_iter(0, 0, True)
            with ch.loop(0, NG // 2 - 1, 2 * (6 + 12)) as i2:
                ssd_iter(i2 * 2 + 1, 1, True)
                ssd_iter(i2 * 2 + 2, 0, True)
            ssd_iter(NG - 1, 1, False)
            finish(NG - 1, 1)
            nc.vector.drain().then_inc(dve_phase, 1)
            for k in range(16):
                dve.wait_ge(s_yhi, k + 1)
                v.scalar_tensor_tensor(y_lo[:, k], y_raw[:, k], par[:, R_SN + k:R_SN + k + 1], y_hi[:, k].bitcast(F32),
                                       ALU.mult, ALU.subtract).then_inc(s_ylo, 1)
            diagonal(3, y_rstd[:])
            dve.wait_ge(s_spread, 3)
            ch.link(v.tensor_copy(y_rstd[:], flat(psS[:])))
            dve.wait_ge(s_mg_in, 16)
            with ch.loop(0, 4, 2) as i:
                for j in range(2):
                    d = i * 2 + j
                    md = merged[:, bass.ds(d, 1), :].rearrange("p o t -> p (o t)")
                    dve.wait_ge(w_used, i * 4 + (W["yo"] + 2 * j + 2))
                    v.tensor_tensor(tmp[:, j], flat(psG[:, j]), y_rstd[:], ALU.mult).then_inc(freed[j], 1)
                    dve.wait_ge(freed[j], i + O[j]["yo"] + 1)
                    dve.wait_ge(s_gate, d + 1)
                    ch.link(v.tensor_tensor(tmp[:, j], tmp[:, j], gate[:], ALU.mult))
                    v.tensor_tensor(md, md, tmp[:, j], ALU.add).then_inc(s_mg, 1)
            for d in range(0, 8, 2):
                dve.wait_ge(s_mhi, d + 1)
                v.tensor_tensor(m_lo[:, d], merged[:, d], m_hi[:, d].bitcast(F32), ALU.subtract).then_inc(s_mlo[0], 1)
            dve.wait_ge(s_xback, 16)
            with ch.loop(0, 4, 0) as i:
                for j in range(2):
                    d = i * 2 + j
                    dve.wait_ge(w_used, d + W["mix"] + 1)
                    xd = xT[:, bass.ds(d, 1), :].rearrange("p o t -> p (o t)")
                    v.scalar_tensor_tensor(xd, flat(psG[:, j]), mod[:, bass.ds(d + G2, 1)], xd,
                                           ALU.mult, ALU.add).then_inc(freed[j], 1)
            diagonal(4, rstd[:])
            norm_apply(2, 4, scale3, SH3)
            ffn(1)
            dve.wait_ge(s_rt, 5)
            v.reciprocal(rcol[:], rcol[:]).then_inc(s_rinv, 1)
            dve.wait_ge(s_rinv, 1)
            for t in range(NT):
                dve.wait_ge(s_ftr, 2 * t + 1)
                v.tensor_scalar(o_row[:, t, 0:512], final_bank(t, 0), rcol[:, t:t + 1], None, ALU.mult).then_inc(s_orow[0], 1)

        @block.gpsimd
        def _(pool):
            ch = Chain(pool, c_pool_sem)
            for s in (s_cscaled, s_yacc, s_cosed, s_roped):
                pool.sem_inc(s, CREDIT)
            g = nc.gpsimd

            def split(n, j):
                pool.wait_ge(w_hi_done, n + 1)
                g.tensor_tensor(w_lo[:, j], w_raw[:, j], w_hi[:, j].bitcast(F32), ALU.subtract).then_inc(w_lo_done, 1)

            def ada_mul(buf, loaded, value):
                pool.wait_ge(loaded, value)
                g.tensor_tensor(buf, buf, c_act.unsqueeze(2).to_broadcast([P, 8, ADA_W]), ALU.mult).then_inc(s_ada_mul, 1)

            def norm_apply(idx):
                for d in range(1, 8, 2):
                    pool.wait_ge(s_hhi, 8 * idx + d + 1)
                    g.tensor_tensor(h_lo[:, d], xs[:, d % 4], h_hi[:, d].bitcast(F32), ALU.subtract).then_inc(s_hlo[1], 1)

            def add_square(count, j, first):
                pool.wait_ge(s_sq, count + 1)
                if first:
                    g.tensor_copy(acc[:], sq[:, j]).then_inc(s_acc, 1)
                else:
                    pool.wait_ge(s_acc, count)
                    g.tensor_tensor(acc[:], acc[:], sq[:, j], ALU.add).then_inc(s_acc, 1)

            def ffn(x, idx):
                for p, (f0, cnt) in enumerate(PARTS):
                    s = f"gu{x}{p}"
                    n0, F0 = W[s], FT * x + f0
                    if x == 0 and p == 2:
                        pool.wait_ge(w_used, W[s])
                        g.dma_start(pos_i[:], positions.to_broadcast([P, T])).then_inc(s_pos, 16)

                    def body(i):
                        late = isinstance(i, int)
                        if late:
                            split(i * 2 + (n0 + 2), 0)
                        if x == 0 and p < 2:
                            ada_mul(ada[:], s_ada[ADA_FIRST], i * 16 + (16 * f0 + 16))
                        if not late:
                            split(i * 2 + (n0 + 2), 0)
                        split(n0 + 3 + i * 2, 1)
                        pool.wait_ge(s_hid_hi, i + F0 + 1)
                        at = hid_hi[:, bass.ds(i, 1), :].rearrange("p o t -> p (o t)").bitcast(F32)
                        to = hid_lo[:, bass.ds(i, 1), :].rearrange("p o t -> p (o t)")
                        g.tensor_tensor(to, tmp[:, 1], at, ALU.subtract).then_inc(s_hid_lo, 1)
                    if p == 0:
                        body(0)
                        with ch.loop(1, cnt, 0) as i:
                            body(i)
                    else:
                        with ch.loop(0, cnt, 0) as i:
                            body(i)
                    s = f"dn{x}{p}"
                    n1 = W[s]

                    def down(i, tail=False):
                        for j in range(2):
                            if not tail:
                                split(n1 + 2 + j + i * 2, j)
                            if p == 3:
                                add_square(i * 2 + j + 8 * (idx + 1), j, isinstance(i, int) and i == 0 and j == 0)
                    last = x == 1 and p == 3
                    down(0)
                    with ch.loop(1, 3 if last else 4, 0) as i:
                        down(i)
                    if last:
                        down(3, True)

            pool.wait_ge(s_cact, 1)
            for d in range(8):
                add_square(d, d % 2, d == 0)
            split(0, 0)
            split(1, 1)
            norm_apply(0)
            ffn(0, 0)
            norm_apply(1)
            pool.wait_ge(s_xkeep, 16)
            pool.wait_ge(s_trig, 2)
            pool.wait_ge(s_xr, 16)
            g.dma_start(cosT[:], cos_w[:]).then_inc(s_trig_in, 16)
            g.dma_start(sinT[:], sin_w[:]).then_inc(s_trig_in, 16)
            g.dma_start(mask[:], table[:, K_MASK:K_MASK + T]).then_inc(s_mask, 16)
            split(W["dt"] + 2, 0)
            split(W["dt"] + 3, 1)

            def rope(i, p, b, step):
                src, dst = (q_st, k_st)[b], (qT, kT)[b]
                if step == 0:
                    pool.wait_ge(freed[b], i * 3 + O[b]["att"] + 1)
                    past(pool, s_qk, (i - 1) * NA)
                    g.tensor_tensor(dst[:, p], src[:], cosT[:], ALU.mult).then_inc(s_cosed, 1)
                else:
                    pool.wait_ge(freed[b], i * 3 + O[b]["att"] + 2)
                    past(pool, s_cosed, i * 2 + b + 1)
                    g.tensor_tensor(dst[:, p], dst[:, p], src[:], ALU.add).then_inc(s_roped, 1)

            pool.wait_ge(s_trig_in, 16 * 2)
            with ch.loop(0, PAIRS // 2, 0) as i2:
                for p in range(2):
                    i = i2 * 2 + p
                    split(W["att"] + 2 + i * 4, 0)
                    rope(i, p, 0, 0)
                    rope(i, p, 0, 1)
                    split(W["att"] + 3 + i * 4, 1)
                    rope(i, p, 1, 0)
                    split(W["att"] + 4 + i * 4, 0)
                    rope(i, p, 1, 1)
                    split(W["att"] + 5 + i * 4, 1)
            for j in range(4):
                split(W["gba"] + 2 + j, j % 2)
            nc.gpsimd.drain().then_inc(pool_phase, 1)
            with ch.loop(0, 8, 0) as i:
                for j in range(2):
                    split(W["ga"] + 2 + j + i * 2, j)
            g.memset(y_acc[:], 0.0).then_inc(s_yacc, 1)
            past(pool, s_yacc, 1)
            for j in range(4):
                split(W["ssdx"] + 2 + j, j % 2)

            def finish(i, p):
                for j in range(2):
                    past(pool, s_ysq, i * 2 + j + 1)
                    past(pool, s_yacc, i * 2 + j + 1)
                    g.tensor_tensor(y_acc[:], y_acc[:], y_sq[:], ALU.add).then_inc(s_yacc, 1)

            def scale_c(i, p, c):
                n = i * NT + c
                if c == 0:
                    past(pool, s_conv_act, i * 4 + 4)
                past(pool, s_ecs, n + 1)
                past(pool, s_y, n - 1)
                g.tensor_tensor(c_scaled[:, c % 2], ecs[:, c % 2],
                                xbc[:, p, 3, c * P:(c + 1) * P].unsqueeze(1).to_broadcast([P, GH, P]),
                                ALU.mult).then_inc(s_cscaled, 1)

            def ssd_iter(i, p, gemm):
                for c in range(NT):
                    if gemm or c < NT - 1:
                        scale_c(*following(i, p, c))
                    if c == 0 and not (isinstance(i, int) and i == 0):
                        finish(i - 1, 1 - p)
                    for j in range(6):
                        if (8 * j + 7) // 6 == c:
                            split(W["ssd"] + 2 + j + i * 6, j % 2)

            scale_c(0, 0, 0)
            ssd_iter(0, 0, True)
            with ch.loop(0, NG // 2 - 1, 0) as i2:
                ssd_iter(i2 * 2 + 1, 1, True)
                ssd_iter(i2 * 2 + 2, 0, True)
            ssd_iter(NG - 1, 1, False)
            finish(NG - 1, 1)
            nc.gpsimd.drain().then_inc(pool_phase, 1)
            with ch.loop(0, 8, 0) as i:
                for j in range(2):
                    split(W["yo"] + 2 + j + i * 2, j)
            for d in range(1, 8, 2):
                pool.wait_ge(s_mhi, d + 1)
                g.tensor_tensor(m_lo[:, d], merged[:, d], m_hi[:, d].bitcast(F32), ALU.subtract).then_inc(s_mlo[1], 1)

            def mix(i):
                for j in range(2):
                    split(W["mix"] + 2 + j + i * 2, j)
                    add_square(i * 2 + j + 16, j, isinstance(i, int) and i == 0 and j == 0)
            mix(0)
            with ch.loop(1, 4, 0) as i:
                mix(i)
            norm_apply(2)
            ffn(1, 2)


_INS = ["x", "c", "positions", "w_ada", "b_ada", "norm1_w", "ffn1_w_gu", "ffn1_w_down", "norm2_w", "w_in",
        "conv_w", "conv_b", "dt_bias", "a_log", "d_skip", "ssd_norm_w", "w_att_out", "w_ssd_out", "w_mix_out",
        "norm3_w", "ffn2_w_gu", "ffn2_w_down", "final_norm_w"]


def kernel(**inputs):
    import numpy as _np
    import concourse.bacc as _bacc
    from concourse import mybir as _mybir
    from concourse.bass_utils import run_bass_kernel_spmd as _run

    nc = _bacc.Bacc("TRN2", target_bir_lowering=False, num_devices=1)
    arrays, args = {}, []
    for name in _INS:
        a = _np.ascontiguousarray(inputs[name])
        arrays[f"in_{name}"] = a
        args.append(nc.dram_tensor(f"in_{name}", a.shape, _mybir.dt.from_np(a.dtype), kind="ExternalInput").ap())
    arrays["in_table"] = constants()
    args.append(nc.dram_tensor("in_table", arrays["in_table"].shape, F32, kind="ExternalInput").ap())
    shape = tuple(inputs["x"].shape)
    args.append(nc.dram_tensor("out_0", shape, F32, kind="ExternalOutput").ap())
    kernel_program(nc, *args)
    r = _run(nc, [arrays], core_ids=[0])
    return r.results[0]["out_0"]
```
